# Optimizing a Trainium2 kernel written in Bass

```python
import math
import jax
import jax.numpy as jnp
from jax import lax
import numpy as np
import jax, jax.numpy as jnp

D_MODEL = 1024
BATCH = 1
SEQ = 256
DEPTH = 1

HEAD_DIM = 64
N_HEADS_NA = 8
N_HEADS_DIL = 8
N_HEADS = N_HEADS_NA + N_HEADS_DIL
D_NA = N_HEADS_NA * HEAD_DIM
D_DIL = N_HEADS_DIL * HEAD_DIM
D_MIX = D_NA + D_DIL
D_FF = 2816
GRID_W = 64
NA_KH = 8
NA_KW = 16
NA_COL_BLOCK = 16
NA_COL_SPAN = 32
DIL_PATTERNS = ((128, 1), (512, 4), (2048, 16))
DIL_QBLOCK = 128
T5_BUCKETS = 32
T5_MAX_DIST = 1024
NORM_EPS = 1e-6
MASK_VALUE = -1e30


def rmsnorm(x, g):
    xf = x.astype(jnp.float32)
    y = xf * lax.rsqrt(jnp.mean(xf * xf, axis=-1, keepdims=True) + NORM_EPS)
    return (y * g.astype(jnp.float32)).astype(x.dtype)

def swiglu(x, w_gate, w_up, w_down):
    return (jax.nn.silu(x @ w_gate) * (x @ w_up)) @ w_down

def t5_bucket(rel):
    nb = T5_BUCKETS // 2
    max_exact = nb // 2
    n = jnp.abs(rel)
    large = max_exact + (jnp.log(jnp.maximum(n, 1).astype(jnp.float32) / max_exact)
                         / math.log(T5_MAX_DIST / max_exact) * (nb - max_exact)).astype(jnp.int32)
    large = jnp.minimum(large, nb - 1)
    return jnp.where(rel > 0, nb, 0) + jnp.where(n < max_exact, n, large)

def neighbourhood_attention(q, k, v, rel_bias):
    B, H, S, Dh = q.shape
    rows = S // GRID_W
    kh = min(NA_KH, rows)
    ncb = GRID_W // NA_COL_BLOCK
    n_keys = kh * NA_COL_SPAN
    r = jnp.arange(rows)
    key_rows = jnp.clip(r - kh // 2, 0, rows - kh)[:, None] + jnp.arange(kh)[None, :]
    cb = jnp.arange(ncb)
    key_cols = (jnp.clip(cb * NA_COL_BLOCK - NA_KW // 2, 0, GRID_W - NA_COL_SPAN)[:, None]
                + jnp.arange(NA_COL_SPAN)[None, :])
    key_idx = (key_rows[:, None, :, None] * GRID_W
               + key_cols[None, :, None, :]).reshape(rows, ncb, n_keys)
    kr = jnp.repeat(key_rows, NA_COL_SPAN, axis=1)
    kc = jnp.tile(key_cols, (1, kh))
    q_col = cb[:, None] * NA_COL_BLOCK + jnp.arange(NA_COL_BLOCK)[None, :]
    q_col_start = jnp.clip(q_col - NA_KW // 2, 0, GRID_W - NA_KW)
    col_valid = ((kc[:, None, :] >= q_col_start[:, :, None])
                 & (kc[:, None, :] < q_col_start[:, :, None] + NA_KW))
    dc_idx = jnp.clip(kc[:, None, :] - q_col[:, :, None] + NA_KW - 1, 0, 2 * NA_KW - 2)
    dr_idx = kr - r[:, None] + NA_KH - 1
    scale = HEAD_DIM ** -0.5
    q_rows = jnp.moveaxis(q.reshape(B, H, rows, ncb, NA_COL_BLOCK, Dh), 2, 0)

    def row_block(args):
        q_r, idx_r, dr_r = args
        k_r = k[:, :, idx_r]
        v_r = v[:, :, idx_r]
        s = jnp.einsum('bhnqe,bhnke->bhnqk', q_r, k_r,
                       preferred_element_type=jnp.float32) * scale
        bias = rel_bias[:, dr_r[None, None, :], dc_idx].astype(jnp.float32)
        s = jnp.where(col_valid, s + bias, MASK_VALUE)
        p = jax.nn.softmax(s, axis=-1)
        return jnp.einsum('bhnqk,bhnke->bhnqe', p.astype(v.dtype), v_r)

    out = lax.map(row_block, (q_rows, key_idx, dr_idx))
    return jnp.moveaxis(out, 0, 2).reshape(B, H, S, Dh)

def dilated_window_attention(q, k, v, t5_bias, window, dilation):
    B, H, S, Dh = q.shape
    radius = window // (2 * dilation)
    L = S // dilation
    qb = min(DIL_QBLOCK, L)
    nb = -(-L // qb)
    Lp = nb * qb
    kb_len = qb + 2 * radius

    def to_sub(t):
        return t.reshape(B, H, L, dilation, Dh).transpose(0, 1, 3, 2, 4)

    qs = jnp.pad(to_sub(q), ((0, 0), (0, 0), (0, 0), (0, Lp - L), (0, 0))).reshape(B, H, dilation, nb, qb, Dh)
    pad_k = ((0, 0), (0, 0), (0, 0), (radius, radius + Lp - L), (0, 0))
    ks = jnp.pad(to_sub(k), pad_k)
    vs = jnp.pad(to_sub(v), pad_k)
    k_idx = jnp.arange(nb)[:, None] * qb + jnp.arange(kb_len)[None, :]
    k_blk = ks[:, :, :, k_idx]
    v_blk = vs[:, :, :, k_idx]
    q_pos = jnp.arange(nb)[:, None] * qb + jnp.arange(qb)[None, :]
    k_pos = k_idx - radius
    off = k_pos[:, None, :] - q_pos[:, :, None]
    valid = (jnp.abs(off) <= radius) & (k_pos[:, None, :] >= 0) & (k_pos[:, None, :] < L)
    bias = t5_bias[:, t5_bucket(off * dilation)].astype(jnp.float32)
    s = jnp.einsum('bhdnqe,bhdnke->bhdnqk', qs, k_blk,
                   preferred_element_type=jnp.float32) * HEAD_DIM ** -0.5
    s = jnp.where(valid, s + bias[:, None], MASK_VALUE)
    m = jnp.max(s, axis=-1, keepdims=True)
    p = jnp.exp(s - m)
    den = jnp.sum(p, axis=-1)
    o = jnp.einsum('bhdnqk,bhdnke->bhdnqe', p.astype(v.dtype), v_blk,
                   preferred_element_type=jnp.float32) / den[..., None]
    lse = m[..., 0] + jnp.log(den)
    o = o.reshape(B, H, dilation, Lp, Dh)[:, :, :, :L].transpose(0, 1, 3, 2, 4).reshape(B, H, S, Dh)
    lse = lse.reshape(B, H, dilation, Lp)[..., :L].transpose(0, 1, 3, 2).reshape(B, H, S)
    return o, lse

def dilated_mixture_attention(q, k, v, t5_bias):
    results = [dilated_window_attention(q, k, v, t5_bias, w, d) for w, d in DIL_PATTERNS]
    outs = jnp.stack([res[0] for res in results])
    lses = jnp.stack([res[1] for res in results])
    wts = jax.nn.softmax(lses, axis=0)
    return jnp.sum(wts[..., None] * outs, axis=0).astype(q.dtype)

def first_inputs(seed: int = 0) -> dict:
    key = jax.random.key(seed)
    ks = jax.random.split(key, 20)

    def nrm(k, shape, scale):
        return jax.random.normal(k, shape, jnp.float32) * scale

    def gain(k, shape):
        return 1.0 + 0.05 * jax.random.normal(k, shape, jnp.float32)

    return {
        'x': nrm(ks[0], (BATCH, SEQ, D_MODEL), 1.0),
        'ffn1_pre_g': gain(ks[1], (DEPTH, D_MODEL)),
        'ffn1_w_gate': nrm(ks[2], (DEPTH, D_MODEL, D_FF), D_MODEL ** -0.5),
        'ffn1_w_up': nrm(ks[3], (DEPTH, D_MODEL, D_FF), D_MODEL ** -0.5),
        'ffn1_w_down': nrm(ks[4], (DEPTH, D_FF, D_MODEL), D_FF ** -0.5),
        'ffn1_post_g': gain(ks[5], (DEPTH, D_MODEL)),
        'mix_pre_g': gain(ks[6], (DEPTH, D_MODEL)),
        'w_qkv': nrm(ks[7], (DEPTH, D_MODEL, 3 * D_MIX), D_MODEL ** -0.5),
        'na_rel_bias': nrm(ks[8], (DEPTH, N_HEADS_NA, 2 * NA_KH - 1, 2 * NA_KW - 1), 0.5),
        't5_rel_bias': nrm(ks[9], (N_HEADS_DIL, T5_BUCKETS), 0.5),
        'na_out_g': gain(ks[10], (DEPTH, D_NA)),
        'dil_out_g': gain(ks[11], (DEPTH, D_DIL)),
        'w_out': nrm(ks[12], (DEPTH, D_MIX, D_MODEL), D_MIX ** -0.5),
        'mix_post_g': gain(ks[13], (DEPTH, D_MODEL)),
        'ffn2_pre_g': gain(ks[14], (DEPTH, D_MODEL)),
        'ffn2_w_gate': nrm(ks[15], (DEPTH, D_MODEL, D_FF), D_MODEL ** -0.5),
        'ffn2_w_up': nrm(ks[16], (DEPTH, D_MODEL, D_FF), D_MODEL ** -0.5),
        'ffn2_w_down': nrm(ks[17], (DEPTH, D_FF, D_MODEL), D_FF ** -0.5),
        'ffn2_post_g': gain(ks[18], (DEPTH, D_MODEL)),
    }

def first_block(x, ffn1_pre_g, ffn1_w_gate, ffn1_w_up, ffn1_w_down, ffn1_post_g,
              mix_pre_g, w_qkv, na_rel_bias, t5_rel_bias, na_out_g, dil_out_g, w_out,
              mix_post_g, ffn2_pre_g, ffn2_w_gate, ffn2_w_up, ffn2_w_down, ffn2_post_g):
    B, S, _ = x.shape
    for l in range(DEPTH):
        h = swiglu(rmsnorm(x, ffn1_pre_g[l]), ffn1_w_gate[l], ffn1_w_up[l], ffn1_w_down[l])
        x = x + 0.5 * rmsnorm(h, ffn1_post_g[l])
        h = rmsnorm(x, mix_pre_g[l])
        qkv = (h @ w_qkv[l]).reshape(B, S, 3, N_HEADS, HEAD_DIM).transpose(2, 0, 3, 1, 4)
        q, k, v = qkv[0], qkv[1], qkv[2]
        o_na = neighbourhood_attention(q[:, :N_HEADS_NA], k[:, :N_HEADS_NA], v[:, :N_HEADS_NA],
                                       na_rel_bias[l])
        o_dil = dilated_mixture_attention(q[:, N_HEADS_NA:], k[:, N_HEADS_NA:], v[:, N_HEADS_NA:],
                                          t5_rel_bias)
        o_na = rmsnorm(o_na.transpose(0, 2, 1, 3).reshape(B, S, D_NA), na_out_g[l])
        o_dil = rmsnorm(o_dil.transpose(0, 2, 1, 3).reshape(B, S, D_DIL), dil_out_g[l])
        mixed = jnp.concatenate([o_na, o_dil], axis=-1) @ w_out[l]
        x = x + rmsnorm(mixed, mix_post_g[l])
        h = swiglu(rmsnorm(x, ffn2_pre_g[l]), ffn2_w_gate[l], ffn2_w_up[l], ffn2_w_down[l])
        x = x + 0.5 * rmsnorm(h, ffn2_post_g[l])
    return x


DEPTH_2 = 2

CTX_LEN = 256
EPS = 1e-6
NEG_BIG = -1e30
LB_FLOOR = 1e-30

N_BRANCH = 3
BRANCH_WIDTH = D_MODEL // 2

FOURIER_GROUPS = 4
FOURIER_WIDTH = BRANCH_WIDTH
FOURIER_GROUP_DIM = FOURIER_WIDTH // FOURIER_GROUPS

ATTN_HEADS = BRANCH_WIDTH // HEAD_DIM
ATTN_KV_HEADS = ATTN_HEADS // 4
ATTN_WIDTH = ATTN_HEADS * HEAD_DIM
KV_WIDTH = ATTN_KV_HEADS * HEAD_DIM
WINDOW = 128
BLOCK = 128
ROPE_THETA = 10000.0

HGRN_HEADS = 4
HGRN_DK = BRANCH_WIDTH // HGRN_HEADS
HGRN_DV = BRANCH_WIDTH // HGRN_HEADS
HGRN_KW = HGRN_HEADS * HGRN_DK
HGRN_VW = HGRN_HEADS * HGRN_DV
CHUNK = 64

D_FF_2 = 4 * D_MODEL

_SEG_SIZES = (KV_WIDTH, KV_WIDTH, HGRN_VW, HGRN_KW, HGRN_KW,
              ATTN_WIDTH, HGRN_KW, HGRN_VW, FOURIER_WIDTH, N_BRANCH * D_MODEL)
IN_SPLITS = [sum(_SEG_SIZES[:i + 1]) for i in range(len(_SEG_SIZES) - 1)]
D_IN = sum(_SEG_SIZES)
N_STATE_COLS = sum(_SEG_SIZES[:5])
STATE_SPLITS = IN_SPLITS[:4]


F32 = jnp.float32

def rms_norm(x, g):
    xf = x.astype(F32)
    y = xf * lax.rsqrt(jnp.mean(xf * xf, axis=-1, keepdims=True) + EPS)
    return (y * g.astype(F32)).astype(x.dtype)

def adaln_norm(x, g, shift, scale):
    return rms_norm(x, g) * (1 + scale) + shift

def modulation(cond, w, b):
    m = jax.nn.silu(cond) @ w + b
    return jnp.split(m, 6, axis=-1)

def _heads(a, n):
    return a.reshape(a.shape[:-1] + (n, a.shape[-1] // n))

def _to_bhtd(a, n):
    return jnp.swapaxes(_heads(a, n), 1, 2)

def _flip_t(a):
    return jnp.flip(a, axis=2)

def axial_rope_tables(n_tok):
    n_rows = n_tok // GRID_W
    row = jnp.repeat(jnp.arange(n_rows), GRID_W).astype(F32)
    col = jnp.tile(jnp.arange(GRID_W), n_rows).astype(F32)
    axis_dim = HEAD_DIM // 2
    inv_freq = ROPE_THETA ** (-jnp.arange(0, axis_dim, 2, dtype=F32) / axis_dim)
    ang_r = row[:, None] * inv_freq
    ang_c = col[:, None] * inv_freq
    return (jnp.cos(ang_r), jnp.sin(ang_r), jnp.cos(ang_c), jnp.sin(ang_c))

def apply_axial_rope(t, rope):
    cos_r, sin_r, cos_c, sin_c = rope

    def rot(u, cos, sin):
        u1, u2 = jnp.split(u, 2, axis=-1)
        cos = cos[None, :, None, :]
        sin = sin[None, :, None, :]
        return jnp.concatenate([u1 * cos - u2 * sin, u2 * cos + u1 * sin], axis=-1)

    tr, tc = jnp.split(t, 2, axis=-1)
    return jnp.concatenate([rot(tr, cos_r, sin_r), rot(tc, cos_c, sin_c)], axis=-1).astype(t.dtype)

def _sink_column(sink, ref):
    g = ATTN_HEADS // ATTN_KV_HEADS
    return jnp.broadcast_to(sink.astype(F32).reshape(ATTN_KV_HEADS, g, 1, 1), ref.shape[:-1] + (1,))

def window_attention(q, k, v, kc, vc, sink):
    b, s, _, dh = q.shape
    nb = s // BLOCK
    g = ATTN_HEADS // ATTN_KV_HEADS
    scale = dh ** -0.5
    qb = q.reshape(b, nb, BLOCK, ATTN_KV_HEADS, g, dh)
    pad = ((0, 0), (BLOCK, BLOCK), (0, 0), (0, 0))
    kp = jnp.pad(k, pad).reshape(b, nb + 2, BLOCK, ATTN_KV_HEADS, dh)
    vp = jnp.pad(v, pad).reshape(b, nb + 2, BLOCK, ATTN_KV_HEADS, dh)
    kw = jnp.concatenate([kp[:, :-2], kp[:, 1:-1], kp[:, 2:]], axis=2)
    vw = jnp.concatenate([vp[:, :-2], vp[:, 1:-1], vp[:, 2:]], axis=2)
    s_win = jnp.einsum('bnqhgd,bnkhd->bnhgqk', qb, kw).astype(F32) * scale
    s_ctx = jnp.einsum('bnqhgd,bchd->bnhgqc', qb, kc).astype(F32) * scale
    t_pos = jnp.arange(nb)[:, None, None] * BLOCK + jnp.arange(BLOCK)[None, :, None]
    k_pos = jnp.arange(nb)[:, None, None] * BLOCK - BLOCK + jnp.arange(3 * BLOCK)[None, None, :]
    valid = (jnp.abs(k_pos - t_pos) <= WINDOW) & (k_pos >= 0) & (k_pos < s)
    s_win = jnp.where(valid[None, :, None, None], s_win, NEG_BIG)
    logits = jnp.concatenate([s_win, s_ctx, _sink_column(sink, s_win)], axis=-1)
    p = jax.nn.softmax(logits, axis=-1)
    nw = 3 * BLOCK
    nc = kc.shape[1]
    o = (jnp.einsum('bnhgqk,bnkhd->bnqhgd', p[..., :nw].astype(v.dtype), vw)
         + jnp.einsum('bnhgqc,bchd->bnqhgd', p[..., nw:nw + nc].astype(v.dtype), vc))
    return o.reshape(b, s, ATTN_HEADS * dh)

def context_attention(qc, kc, vc, sink):
    b, lc, _, dh = qc.shape
    g = ATTN_HEADS // ATTN_KV_HEADS
    qg = qc.reshape(b, lc, ATTN_KV_HEADS, g, dh)
    s = jnp.einsum('bqhgd,bkhd->bhgqk', qg, kc).astype(F32) * dh ** -0.5
    p = jax.nn.softmax(jnp.concatenate([s, _sink_column(sink, s)], axis=-1), axis=-1)
    o = jnp.einsum('bhgqk,bkhd->bqhgd', p[..., :lc].astype(vc.dtype), vc)
    return o.reshape(b, lc, ATTN_HEADS * dh)

def fourier_mix(a):
    b, t, _ = a.shape
    ag = a.astype(F32).reshape(b, t, FOURIER_GROUPS, FOURIER_GROUP_DIM)
    y = jnp.fft.fft2(ag, axes=(1, 3), norm='ortho').real
    return y.reshape(b, t, FOURIER_WIDTH).astype(a.dtype)

def hgrn_forget(z, lb):
    zf = z.astype(F32)
    lbf = lb.astype(F32)
    k = (1.0 - lbf) * jax.nn.sigmoid(-zf)
    logf = jnp.logaddexp(jax.nn.log_sigmoid(zf),
                         jnp.log(jnp.maximum(lbf, LB_FLOOR)) + jax.nn.log_sigmoid(-zf))
    return k, logf

def hgrn_kv(i_raw, ff_raw, fb_raw, lb):
    v = _to_bhtd(i_raw.astype(F32), HGRN_HEADS)
    kf, lff = hgrn_forget(ff_raw, lb[0])
    kb, lfb = hgrn_forget(fb_raw, lb[1])
    return (v, _to_bhtd(kf, HGRN_HEADS), _to_bhtd(lff, HGRN_HEADS),
            _to_bhtd(kb, HGRN_HEADS), _to_bhtd(lfb, HGRN_HEADS))

def hgrn_q(q_raw):
    return _to_bhtd(jax.nn.silu(q_raw).astype(F32), HGRN_HEADS)

def gla_chunked(q, k, v, logf, s0):
    b, h, t, dk = q.shape
    dv = v.shape[-1]
    n = t // CHUNK

    def to_chunks(a):
        return jnp.moveaxis(a.reshape(b, h, n, CHUNK, a.shape[-1]), 2, 0)

    lower = jnp.tril(jnp.ones((CHUNK, CHUNK), dtype=bool))[:, :, None]

    def step(state, inp):
        qc, kc, vc, lc = inp
        g = jnp.cumsum(lc, axis=2)
        o_inter = jnp.einsum('bhtk,bhkv->bhtv', qc * jnp.exp(g), state)
        diff = g[:, :, :, None, :] - g[:, :, None, :, :]
        decay = jnp.where(lower, jnp.exp(jnp.where(lower, diff, 0.0)), 0.0)
        a = jnp.einsum('bhtsk,bhsk->bhts', qc[:, :, :, None, :] * decay, kc)
        o = o_inter + jnp.einsum('bhts,bhsv->bhtv', a, vc)
        g_last = g[:, :, -1:, :]
        new_state = (jnp.exp(g_last[:, :, 0, :])[..., None] * state
                     + jnp.einsum('bhsk,bhsv->bhkv', kc * jnp.exp(g_last - g), vc))
        return new_state, o

    s_fin, o = lax.scan(step, s0, (to_chunks(q), to_chunks(k), to_chunks(v), to_chunks(logf)))
    o = jnp.moveaxis(o, 0, 2).reshape(b, h, t, dv)
    return o, s_fin

def gla_final_state(k, v, logf):
    g = jnp.cumsum(logf, axis=2)
    return jnp.einsum('bhsk,bhsv->bhkv', k * jnp.exp(g[:, :, -1:, :] - g), v)

def hgrn_bidir(q, kf, lff, kb, lfb, v, s_f, s_b):
    o_f, s_f_new = gla_chunked(q, kf, v, lff, s_f)
    o_b, s_b_new = gla_chunked(_flip_t(q), _flip_t(kb), _flip_t(v), _flip_t(lfb), s_b)
    return o_f + _flip_t(o_b), s_f_new, s_b_new

def hgrn_readout(o, g_raw, norm_g):
    o = rms_norm(jnp.swapaxes(o, 1, 2), norm_g)
    return o.reshape(g_raw.shape).astype(g_raw.dtype) * jax.nn.silu(g_raw)

def merge_branches(o_four, o_attn, o_hgrn, gate_raw, w_branch, w_out):
    br = jnp.stack([o_four, o_attn, o_hgrn], axis=-2)
    proj = jnp.einsum('btnc,ncd->btnd', br, w_branch)
    gates = jax.nn.sigmoid(gate_raw.reshape(gate_raw.shape[:-1] + (N_BRANCH, D_MODEL)))
    return jnp.sum(gates * proj, axis=-2) @ w_out

def sq_relu_mlp(h, w1, w2):
    return jnp.square(jax.nn.relu(h @ w1)) @ w2

def second_inputs(seed: int = 0) -> dict:
    key = jax.random.key(seed)
    ks = jax.random.split(key, 18)

    def nrm(k, shape, s):
        return jax.random.normal(k, shape, F32) * s

    return {
        "x": nrm(ks[0], (BATCH, SEQ, D_MODEL), 1.0),
        "c": nrm(ks[1], (BATCH, D_MODEL), 1.0),
        "ctx": nrm(ks[2], (BATCH, CTX_LEN, D_MODEL), 1.0),
        "c_ctx": nrm(ks[3], (D_MODEL,), 1.0),
        "w_mod": nrm(ks[4], (DEPTH_2, D_MODEL, 6 * D_MODEL), 0.5 * D_MODEL ** -0.5),
        "b_mod": nrm(ks[5], (DEPTH_2, 6 * D_MODEL), 0.02),
        "norm1_g": 1.0 + nrm(ks[6], (DEPTH_2, D_MODEL), 0.02),
        "norm2_g": 1.0 + nrm(ks[7], (DEPTH_2, D_MODEL), 0.02),
        "w_in": nrm(ks[8], (DEPTH_2, D_MODEL, D_IN), D_MODEL ** -0.5),
        "q_norm_g": 1.0 + nrm(ks[9], (DEPTH_2, HEAD_DIM), 0.02),
        "k_norm_g": 1.0 + nrm(ks[10], (DEPTH_2, HEAD_DIM), 0.02),
        "attn_sink": nrm(ks[11], (DEPTH_2, ATTN_HEADS), 0.5),
        "hgrn_lb_logits": nrm(ks[12], (DEPTH_2, 2, HGRN_KW), 0.5),
        "hgrn_norm_g": 1.0 + nrm(ks[13], (DEPTH_2, HGRN_DV), 0.02),
        "w_branch": nrm(ks[14], (DEPTH_2, N_BRANCH, BRANCH_WIDTH, D_MODEL), BRANCH_WIDTH ** -0.5),
        "w_out": nrm(ks[15], (DEPTH_2, D_MODEL, D_MODEL), D_MODEL ** -0.5),
        "w_ff1": nrm(ks[16], (DEPTH_2, D_MODEL, D_FF_2), D_MODEL ** -0.5),
        "w_ff2": nrm(ks[17], (DEPTH_2, D_FF_2, D_MODEL), D_FF_2 ** -0.5),
    }

def second_block(x, c, ctx, c_ctx, w_mod, b_mod, norm1_g, norm2_g, w_in, q_norm_g, k_norm_g,
              attn_sink, hgrn_lb_logits, hgrn_norm_g, w_branch, w_out, w_ff1, w_ff2):
    bsz, n_tok, _ = x.shape
    rope = axial_rope_tables(n_tok)
    lb_p = jax.nn.softmax(hgrn_lb_logits.astype(F32), axis=0)
    lb_all = jnp.cumsum(lb_p, axis=0) - lb_p[0:1]
    xc = ctx
    for l in range(DEPTH_2):
        last = l == DEPTH_2 - 1
        mx = [m[:, None, :] for m in modulation(c, w_mod[l], b_mod[l])]
        mc = modulation(c_ctx, w_mod[l], b_mod[l])
        h = adaln_norm(x, norm1_g[l], mx[0], mx[1])
        hc = adaln_norm(xc, norm1_g[l], mc[0], mc[1])

        if last:
            kc_raw, vc_raw, ic_raw, fcf_raw, fcb_raw = jnp.split(
                hc @ w_in[l][:, :N_STATE_COLS], STATE_SPLITS, axis=-1)
        else:
            (kc_raw, vc_raw, ic_raw, fcf_raw, fcb_raw, qc_raw, qhc_raw, ghc_raw,
             fourc_raw, gatec_raw) = jnp.split(hc @ w_in[l], IN_SPLITS, axis=-1)
        kc = rms_norm(_heads(kc_raw, ATTN_KV_HEADS), k_norm_g[l])
        vc = _heads(vc_raw, ATTN_KV_HEADS)
        vhc, kfc, lffc, kbc, lfbc = hgrn_kv(ic_raw, fcf_raw, fcb_raw, lb_all[l])
        if last:
            s_f = gla_final_state(kfc, vhc, lffc)
            s_b = gla_final_state(_flip_t(kbc), _flip_t(vhc), _flip_t(lfbc))
        else:
            zeros = jnp.zeros((bsz, HGRN_HEADS, HGRN_DK, HGRN_DV), F32)
            oc_h, s_f, s_b = hgrn_bidir(hgrn_q(qhc_raw), kfc, lffc, kbc, lfbc, vhc, zeros, zeros)
            qc = rms_norm(_heads(qc_raw, ATTN_HEADS), q_norm_g[l])
            oc_a = context_attention(qc, kc, vc, attn_sink[l])
            oc_f = fourier_mix(fourc_raw)
            oc_hr = hgrn_readout(oc_h, ghc_raw, hgrn_norm_g[l])
            yc = merge_branches(oc_f, oc_a, oc_hr, gatec_raw, w_branch[l], w_out[l])
            xc = xc + mc[2] * yc
            hc2 = adaln_norm(xc, norm2_g[l], mc[3], mc[4])
            xc = xc + mc[5] * sq_relu_mlp(hc2, w_ff1[l], w_ff2[l])

        (k_raw, v_raw, i_raw, ff_raw, fb_raw, q_raw, qh_raw, gh_raw,
         four_raw, gate_raw) = jnp.split(h @ w_in[l], IN_SPLITS, axis=-1)
        q = apply_axial_rope(rms_norm(_heads(q_raw, ATTN_HEADS), q_norm_g[l]), rope)
        k = apply_axial_rope(rms_norm(_heads(k_raw, ATTN_KV_HEADS), k_norm_g[l]), rope)
        v = _heads(v_raw, ATTN_KV_HEADS)
        o_a = window_attention(q, k, v, kc, vc, attn_sink[l])
        vh, kf, lff, kb, lfb = hgrn_kv(i_raw, ff_raw, fb_raw, lb_all[l])
        o_h, _, _ = hgrn_bidir(hgrn_q(qh_raw), kf, lff, kb, lfb, vh, s_f, s_b)
        o_hr = hgrn_readout(o_h, gh_raw, hgrn_norm_g[l])
        o_f = fourier_mix(four_raw)
        y = merge_branches(o_f, o_a, o_hr, gate_raw, w_branch[l], w_out[l])
        x = x + mx[2] * y
        h2 = adaln_norm(x, norm2_g[l], mx[3], mx[4])
        x = x + mx[5] * sq_relu_mlp(h2, w_ff1[l], w_ff2[l])
    return x


def setup_inputs(seed=0):
    out = dict(first_inputs(seed))
    for name, value in second_inputs(seed + 1).items():
        if name != "x":
            out[name + "_2"] = value
    return out


def reference(
    x, ffn1_pre_g, ffn1_w_gate, ffn1_w_up, ffn1_w_down, ffn1_post_g, mix_pre_g, w_qkv,
    na_rel_bias, t5_rel_bias, na_out_g, dil_out_g, w_out, mix_post_g, ffn2_pre_g, ffn2_w_gate,
    ffn2_w_up, ffn2_w_down, ffn2_post_g, c_2, ctx_2, c_ctx_2, w_mod_2, b_mod_2, norm1_g_2,
    norm2_g_2, w_in_2, q_norm_g_2, k_norm_g_2, attn_sink_2, hgrn_lb_logits_2, hgrn_norm_g_2,
    w_branch_2, w_out_2, w_ff1_2, w_ff2_2,
):
    x = first_block(
        x, ffn1_pre_g, ffn1_w_gate, ffn1_w_up, ffn1_w_down, ffn1_post_g, mix_pre_g, w_qkv,
        na_rel_bias, t5_rel_bias, na_out_g, dil_out_g, w_out, mix_post_g, ffn2_pre_g,
        ffn2_w_gate, ffn2_w_up, ffn2_w_down, ffn2_post_g,
    )
    return second_block(
        x, c_2, ctx_2, c_ctx_2, w_mod_2, b_mod_2, norm1_g_2, norm2_g_2, w_in_2, q_norm_g_2,
        k_norm_g_2, attn_sink_2, hgrn_lb_logits_2, hgrn_norm_g_2, w_branch_2, w_out_2, w_ff1_2,
        w_ff2_2,
    )


_drawn_inputs = setup_inputs


def setup_inputs(seed=0):
    import zlib

    import numpy as np

    out = dict(_drawn_inputs(seed))
    spreads = {}
    factors = {'ffn2_post_g': 3.596,
     'ctx_2': 6.123,
     'norm1_g_2': 8.0,
     'norm2_g_2': 6.651,
     'q_norm_g_2': 8.0,
     'k_norm_g_2': 8.0,
     'attn_sink_2': 8.0,
     'hgrn_lb_logits_2': 8.0,
     'hgrn_norm_g_2': 8.0}
    for name, (base, spread) in spreads.items():
        noise = np.random.default_rng([zlib.crc32(name.encode()), seed]).standard_normal(out[name].shape)
        drawn = base * np.exp(spread * noise) if base else spread * noise
        out[name] = jnp.asarray(drawn.astype(out[name].dtype))
    for name, factor in factors.items():
        out[name] = (out[name] * factor).astype(out[name].dtype)
    return out
```

```python
from contextlib import ExitStack

import numpy as np

import concourse.bass as bass
from concourse import mybir

ALU = mybir.AluOpType
ACT = mybir.ActivationFunctionType
F32 = mybir.dt.float32
U8 = mybir.dt.uint8
AX = mybir.AxisListType.X

NEG = -1e30
EPS = 1e-6
LOG_FLOOR = float(np.log(np.float32(1e-30)))
NSLOT = 4


def const_arrays():
    i = np.arange(128)
    t = np.arange(256)
    c = {}
    c["ident"] = np.eye(128)
    c["ones"] = np.ones((128, 128))
    c["blk"] = (i[:, None] // 64 == i[None, :] // 64).astype(float)
    perm = np.zeros((128, 128))
    for d in range(128):
        if d % 32 < 16:
            perm[d + 16, d] = -1.0
        else:
            perm[d - 16, d] = 1.0
    c["perm"] = perm
    freq = (np.float32(10000.0) ** (-np.arange(0, 32, 2, dtype=np.float32) / np.float32(32))).astype(np.float32)
    pos = np.where((i[:, None] % 64) < 32, (t // 64)[None, :], (t % 64)[None, :]).astype(np.float32)
    ang = (pos * freq[i % 16][:, None]).astype(np.float32).astype(np.float64)
    c["ropec"], c["ropes"] = np.cos(ang), np.sin(ang)
    w = 2 * np.pi * np.outer(i, i) / 128
    c["cdsd"] = np.concatenate([np.cos(w), np.sin(w)], 1) / np.sqrt(128.0)
    w = 2 * np.pi * (np.outer(t, t) % 256) / 256
    c["ct"] = np.concatenate([np.cos(w)[:128], np.cos(w)[128:]], 1) / 16.0
    c["nst"] = -np.concatenate([np.sin(w)[:128], np.sin(w)[128:]], 1) / 16.0
    k = np.arange(256)
    win = []
    for a in range(2):
        q = a * 128 + i
        win.append(np.where(np.abs(k[None] - q[:, None]) <= 128, 0.0, NEG))
        win.append(np.zeros((128, 256)))
    c["win"] = np.concatenate(win, 1)
    na, dil = [], []
    for a in range(2):
        q = a * 128 + i
        s = np.clip(q % 64 - 8, 0, 48)
        kc = k % 64
        na.append(np.where((kc[None] >= s[:, None]) & (kc[None] < s[:, None] + 16), 0.0, NEG))
        d = k[None] - q[:, None]
        n = (np.abs(d) <= 64).astype(int) + (d % 4 == 0) + (d % 16 == 0)
        dil.append(np.where(n > 0, np.log(np.maximum(n, 1)), NEG))
    c["b1mask"] = np.concatenate(na + dil, 1)
    return {n: np.ascontiguousarray(v, dtype=np.float32) for n, v in c.items()}


def bucket_onehot():
    rel = np.arange(-255, 257)
    n = np.abs(rel)
    large = 8 + (np.log(np.maximum(n, 1).astype(np.float32) / np.float32(8))
                 / np.float32(np.log(1024 / 8)) * np.float32(8)).astype(np.int32)
    b = np.where(rel > 0, 16, 0) + np.where(n < 8, n, np.minimum(large, 15))
    return (np.arange(32)[:, None] == b[None, :]).astype(np.float32)


def level_masks():
    i = np.arange(128)
    m = []
    for lv in range(7):
        h = 1 << lv
        same = i[:, None] // (2 * h) == i[None, :] // (2 * h)
        m.append(same & ((i[:, None] // h) % 2 != (i[None, :] // h) % 2))
    return np.concatenate(m, 1).astype(np.float32)


CONSTS = ["ident", "ones", "blk", "perm", "ropec", "ropes", "cdsd", "ct", "nst", "win"]
VEC = {}


def vec_columns():
    at = 0
    for name, n in [("ffn1_pre_g", 8), ("ffn1_post_g", 8), ("mix_pre_g", 8), ("na_out_g", 4), ("dil_out_g", 4),
                    ("mix_post_g", 8), ("ffn2_pre_g", 8), ("ffn2_post_g", 8), ("cc", 16), ("b_mod_2", 96),
                    ("norm1_g_2", 16), ("norm2_g_2", 16), ("q_norm_g_2", 2), ("k_norm_g_2", 2),
                    ("hgrn_lb_logits_2", 16), ("hgrn_norm_g_2", 2), ("attn_sink_2", 16), ("eps", 1), ("neglb", 1)]:
        VEC[name] = (at, n)
        at += n
    return at


NVEC = vec_columns()


class Tok:
    def __init__(self, sem=None, val=None):
        self.sem, self.val, self.used = sem, val, False


class Queue:

    def __init__(self, sem):
        self.sem, self.ops = sem, []

    def __call__(self, fn, *after):
        tok = self.last = Tok()
        self.ops.append((fn, self.flat(after), tok, None))
        return tok

    def dma(self, fn, sem, val, *after):
        self.ops.append((fn, self.flat(after), None, sem))
        return Tok(sem, val)

    @staticmethod
    def flat(x):
        out = []
        for t in x:
            if isinstance(t, (list, tuple)):
                out += Queue.flat(t)
            elif t is not None:
                t.used = True
                out.append(t)
        return out

    def number(self):
        n = 0
        for _, _, tok, _ in self.ops:
            if tok is not None and tok.used:
                n += 1
                tok.sem, tok.val = self.sem, n

    def emit(self, eng):
        seen = {}
        for fn, after, tok, dsem in self.ops:
            need = {}
            for t in after:
                if self.skip_own and t.sem is self.sem:
                    continue
                k = id(t.sem)
                if t.val > need.get(k, (None, 0))[1]:
                    need[k] = (t.sem, t.val)
            for k, (s, v) in need.items():
                if seen.get(k, 0) < v:
                    eng.wait_ge(s, v)
                    seen[k] = v
            if fn is None:
                continue
            ins = fn(eng)
            if dsem is not None:
                ins.then_inc(dsem, 16)
            elif tok.used:
                ins.then_inc(self.sem, 1)

    skip_own = False


def bc(ap, dim, n):
    a = [list(x) for x in ap.ap]
    a.insert(dim, [0, n])
    return bass.AP(ap.tensor, ap.offset, a)


class Banks:
    def __init__(self, tensors):
        self.banks = [{"ap": t, "free": []} for t in tensors]
        self.at = 0

    def get(self):
        b = self.banks[self.at % len(self.banks)]
        self.at += 1
        return b


def build_program(nc, shapes, order, debug=None):
    ctx = ExitStack()

    def sb(name, shape, dt=F32):
        return ctx.enter_context(nc.sbuf_tensor(name, shape, dt))

    def sem(name):
        return ctx.enter_context(nc.semaphore(name))

    def dram(name, shape, dt=F32, kind="ExternalInput"):
        return nc.dram_tensor(name, shape, dt, kind=kind).ap()

    with ctx:
        csizes = shapes["consts"]
        nconst = sum(csizes.values())
        d_x = dram("xin", (128, 4096))
        d_c = dram("consts", (128, nconst))
        d_bm = dram("b1mask", (128, 1024))
        d_v = dram("vecs", (128, NVEC))
        d_m = dram("lmask", (128, 896))
        d_oh = dram("onehot", (32, 512))
        d_t5 = dram("t5t", (32, 8))
        d_na = dram("narel", (8, 465))
        d_out = dram("yout", (128, 2048), kind="ExternalOutput")
        d_line = dram("lines", (8, 512), kind="Internal")
        d_sk = dram("dilskew", (8, 128, 512), kind="Internal")
        d_nk = dram("naskew", (8, 64, 465), kind="Internal")

        WR = [sb(f"wr{i}", [128, 2048]) for i in range(NSLOT)]
        X = sb("X", [128, 8, 512])
        H = sb("H", [128, 8, 512])
        S = sb("S", [128, 4096])
        BIG = sb("BIG", [128, 16384])
        R = sb("R", [128, 10496])
        CT = sb("CT", [128, nconst])
        V = sb("V", [128, NVEC])
        LM = sb("LM", [128, 896], U8)
        MOD = sb("MOD", [128, 2, 48, 2])
        GS = sb("GS", [128, 2, 2, 8, 2])
        CS = sb("CS", [128, 8, 32])
        LB = sb("LB", [128, 5, 8])
        RS = sb("RS", [128, 512])
        ST = sb("ST", [128, 3, 8])
        S3 = S[:, :].rearrange("p (k t) -> p k t", k=8)

        psum = [ctx.enter_context(nc.psum_tensor(f"ps{i}", [128, 512], F32)) for i in range(8)]
        main = Banks(psum[0:4])
        aux = Banks(psum[4:8])

        sync, pe = Queue(sem("s_sync")), Queue(sem("s_pe"))
        act, dve, pool = Queue(sem("s_act")), Queue(sem("s_dve")), Queue(sem("s_pool"))
        pe.skip_own = True
        slot_sem = [sem(f"s_w{i}") for i in range(NSLOT)]
        s_out = sem("s_out")

        const = {}
        at = 0
        for n, w in csizes.items():
            const[n] = CT[:, at:at + w]
            at += w
        ident, ones, blk = const["ident"], const["ones"], const["blk"]
        ones256 = bass.AP(ones.tensor, ones.offset, [list(ones.ap[0]), [0, 256]])

        def vec(name, j, n=1):
            return V[:, VEC[name][0] + j:VEC[name][0] + j + n]

        class Stream:
            def __init__(self):
                self.n, self.col = 0, 2048
                self.last = [None] * NSLOT

            def get(self, name, k, cols):
                w = sum(b - a for a, b in cols)
                if self.col + w > 2048:
                    slot = self.n % NSLOT
                    n = self.n
                    self.tok = sync.dma(lambda e: e.dma_start(WR[slot][:, :], d_w[n]),
                                        slot_sem[slot], 16 * (n // NSLOT + 1), self.last[slot])
                    self.slot = slot
                    self.n += 1
                    self.col = 0
                ap = WR[self.slot][:, self.col:self.col + w]
                order.append((self.n - 1, self.col, name, k, tuple(cols)))
                self.col += w
                return ap, self.tok

            def used(self, tok):
                self.last[self.slot] = tok

        W = Stream()

        def mm(out, lhsT, rhs, start, stop, *after, **kw):
            return pe(lambda e: e.matmul(out, lhsT, rhs, start=start, stop=stop, **kw), *after)

        def tr(out, in_, *after):
            return pe(lambda e: e.transpose(out, in_, ident), *after)

        def wmm(bank_ap, name, ks, cols, rhs, *after):
            t = None
            for i, k in enumerate(ks):
                ap, wt = W.get(name, k, cols)
                t = mm(bank_ap, ap, rhs(i), i == 0, i == len(ks) - 1, wt, after if i == 0 else None)
                W.used(t)
            return t

        def a_act(out, in_, func, *after, **kw):
            return act(lambda e: e.activation(out, in_, func, **kw), *after)

        def tt(out, a, b, op, *after, q=None):
            return (q or dve)(lambda e: e.tensor_tensor(out, a, b, op), *after)

        def ts(out, a, s1, s2, op0, op1, *after):
            if op1 is None:
                return dve(lambda e: e.tensor_scalar(out, a, s1, None, op0), *after)
            return dve(lambda e: e.tensor_scalar(out, a, s1, s2, op0, op1), *after)

        def stt(out, a, s, b, op0, op1, *after):
            return dve(lambda e: e.scalar_tensor_tensor(out=out, in0=a, scalar=s, in1=b, op0=op0, op1=op1), *after)

        def vcopy(out, a, *after):
            return dve(lambda e: e.tensor_copy(out, a), *after)

        n_load = [0]

        def load(q, dst, src, *after):
            s = sem(f"s_ld{n_load[0]}")
            n_load[0] += 1
            return q.dma(lambda e: e.dma_start(dst, src), s, 16, *after)

        def dump(name, ap, *after):
            if debug is not None and name in debug:
                shp = [p for p in ap.shape]
                d = nc.dram_tensor("dbg_" + name, shp, F32, kind="ExternalOutput").ap()
                outs.append(pool.dma(lambda e: e.dma_start(d, ap), sem("s_d" + name), 16, *after))
                for q in (pe, act, dve, pool):
                    q(None, outs[-1])

        outs = []
        t_x = load(act, X[:, :, :], d_x.rearrange("p (k t) -> p k t", k=8))
        t_c = load(act, CT[:, :], d_c)
        t_v = load(act, V[:, :], d_v)
        OH = S[0:32, 0:512]
        T5 = S[0:32, 512:520]
        t_oh = load(act, OH, d_oh)
        t_t5 = load(act, T5, d_t5)
        t_lm = load(pool, S[:, 2048:2944], d_m)
        t_lm = dve(lambda e: e.tensor_copy(LM[:, :], S[:, 2048:2944]), t_lm)
        B1M = R[:, 0:1024]
        t_bm = load(pool, B1M, d_bm)
        NAB = BIG[:, 6144:10240].rearrange("p (a h k) -> p a h k", a=2, h=8)
        DILB = BIG[:, 10240:14336].rearrange("p (a h k) -> p a h k", a=2, h=8)

        t_nk = pool.dma(lambda e: e.dma_start(d_nk, bass.AP(d_na.tensor, 0, [[465, 8], [0, 64], [1, 465]])),
                        sem("s_nk"), 16)
        b = aux.get()
        t = mm(b["ap"][0:8, :], T5, OH, True, True, t_oh, t_t5)
        LINE = S[0:8, 1024:1536]
        t = vcopy(LINE, b["ap"][0:8, :], t)
        b["free"] = [t]
        t_oh_free = t
        t_ln = load(pool, d_line, LINE, t)
        t_line_free = t_ln
        t_sk = pool.dma(lambda e: e.dma_start(d_sk, bass.AP(d_line.tensor, 0, [[512, 8], [0, 128], [1, 512]])),
                        sem("s_sk"), 16, t_ln)
        s_nb = sem("s_nb")
        nb = 0
        for a in range(2):
            for r in range(2):
                for kr in range(4):
                    row = 2 * a + r
                    src = bass.AP(d_nk.tensor, (kr - row + 7) * 31 + 15, [[464, 64], [64 * 465, 8], [1, 64]])
                    dst = NAB[64 * r:64 * r + 64, a, :, kr * 64:kr * 64 + 64]
                    nb += 1
                    t_nb = pool.dma(lambda e, src=src, dst=dst: e.dma_start(dst, src), s_nb, 16 * 16, t_nk)
        s_db = sem("s_db")
        for a in range(2):
            src = bass.AP(d_sk.tensor, 255 - 128 * a, [[511, 128], [65536, 8], [1, 256]])
            t_db = pool.dma(lambda e, src=src, a=a: e.dma_start(DILB[:, a], src), s_db, 32, t_sk)

        t = dve(lambda e: e.memset(CS[:, :, :], 0.0))
        cc = V[:, VEC["cc"][0]:VEC["cc"][0] + 16].rearrange("p (k c) -> p k c", c=2)
        t_cs = a_act(CS[:, :, 0:2], cc, ACT.Silu, t, t_v)

        def modulation(l):
            for r in range(3):
                b = aux.get()
                free = list(b["free"])
                for k in range(8):
                    for j in range(4):
                        ap, wt = W.get(("w_mod_2", l), k, [((4 * r + j) * 512, (4 * r + j + 1) * 512)])
                        t = mm(b["ap"][32 * j:32 * j + 32, :], CS[:, k, :], ap, k == 0, k == 7,
                               wt, t_cs, free if k == 0 else None)
                        W.used(t)
                yield
                tmp = RS[:, :]
                t = vcopy(tmp, b["ap"][:, :], t, rs_free)
                b["free"] = [t]
                b = aux.get()
                for c in range(4):
                    t2 = tr(b["ap"][:, 128 * c:128 * c + 128], tmp[:, 128 * c:128 * c + 128], t, b["free"], t_c)
                rs_free[:] = [t2]
                src = b["ap"][:, :].rearrange("p (ch j z) -> p ch j z", ch=4, j=4)[:, :, :, 0:2]
                dst = MOD[:, l, 16 * r:16 * r + 16, :].rearrange("p (j ch) c -> p ch j c", ch=4)
                bm = bc(vec("b_mod_2", 48 * l + 16 * r, 16).rearrange("p (j ch) -> p ch j", ch=4), 3, 2)
                t = tt(dst, src, bm, ALU.add, t2)
                b["free"] = [t]
            for i, (nm, sc) in enumerate((("norm1_g_2", 8), ("norm2_g_2", 32))):
                g = bc(vec(nm, 8 * l, 8), 2, 2)
                t = stt(GS[:, l, i], MOD[:, l, sc:sc + 8, :], 1.0, g, ALU.add, ALU.mult, t)
            t_mod[l] = t
            yield

        rs_free = []
        t_mod = [None, None]

        lg = vec("hgrn_lb_logits_2", 0, 16)
        l0, l1 = lg[:, 0:8], lg[:, 8:16]
        t = tt(LB[:, 0, :], l0, l1, ALU.max, t_v)
        t1 = tt(LB[:, 1, :], l0, LB[:, 0, :], ALU.subtract, t)
        t2 = tt(LB[:, 2, :], l1, LB[:, 0, :], ALU.subtract, t)
        t = a_act(LB[:, 3:5, :], LB[:, 1:3, :], ACT.Exp, t1, t2)
        t = tt(LB[:, 0, :], LB[:, 3, :], LB[:, 4, :], ALU.add, t)
        t = a_act(LB[:, 1, :], LB[:, 0, :], ACT.Ln, t)
        t = tt(LB[:, 2, :], LB[:, 2, :], LB[:, 1, :], ALU.subtract, t)
        t1 = a_act(LB[:, 3, :], LB[:, 2, :], ACT.Exp, t)
        t2 = ts(LB[:, 0, :], LB[:, 2, :], LOG_FLOOR, None, ALU.max, None, t1)
        t_lb = ts(LB[:, 1, :], LB[:, 3, :], -1.0, 1.0, ALU.mult, ALU.add, t1)
        t_lb = [t_lb, t2, ts(LB[:, 4, :], LB[:, 0, :], -1.0, None, ALU.mult, None, t2)]

        def rstd(src, n, T, D, s_free, *after, ones_=None, sq=None, out=None, dst=None):
            sq = sq or (lambda i: S3[:, i, 0:T])
            b = aux.get()
            for i in range(n):
                t = a_act(sq(i), src(i), ACT.Square, after, s_free if i == 0 else None)
                t = mm(b["ap"][:, 0:T], ones_ if ones_ is not None else ones, sq(i), i == 0, i == n - 1,
                       t, t_c, b["free"] if i == 0 else None)
            out = RS[:, 0:T] if out is None else out
            last_mm = t
            t = a_act(out, b["ap"][:, 0:T], ACT.Ln, t, rs_free, bias=vec("eps", 0), scale=1.0 / D)
            b["free"] = [t]
            t = a_act(out, out, ACT.Exp, t, scale=-0.5)
            return t, last_mm

        s_free = [t_oh_free, t_line_free, t_lm]

        def norm_plain(g, *after):
            t, m = rstd(lambda i: X[:, i, 0:256], 8, 256, 1024, s_free, *after)
            s_free[:] = [m]
            toks = []
            for i in range(8):
                toks.append(stt(H[:, i, 0:256], X[:, i, 0:256], vec(g, i), RS[:, 0:256], ALU.mult, ALU.mult,
                                t, h_free, t_v))
            rs_free[:] = [toks[-1]]
            return toks

        h_free = []

        def residual_norm(g, half, toks):
            t, m = rstd(lambda i: H[:, i, 0:256], 8, 256, 1024, s_free, toks)
            s_free[:] = [m]
            out = []
            for i in range(8):
                t2 = stt(H[:, i, 0:256], H[:, i, 0:256], vec(g, i), RS[:, 0:256], ALU.mult, ALU.mult, t)
                out.append(stt(X[:, i, 0:256], H[:, i, 0:256], half, X[:, i, 0:256], ALU.mult, ALU.add, t2))
            rs_free[:] = [out[-1]]
            h_free[:] = [out[-1]]
            return out

        def pair_out(name, ks, rhs, n_pairs, dst, *after):
            toks = []
            for j in range(n_pairs):
                b = main.get()
                for h in range(2):
                    c = (2 * j + h) * 128
                    t = wmm(b["ap"][:, 256 * h:256 * h + 256], name, ks, [(c, c + 128)], rhs, b["free"], after)
                out = dst(j)
                src = b["ap"][:, :].rearrange("p (h t) -> p h t", h=2)
                if j % 2:
                    t = a_act(out, src, ACT.Copy, t)
                else:
                    t = vcopy(out, src, t)
                b["free"] = [t]
                toks.append(t)
            return toks

        def ffn(n, toks, fill=None):
            hid = BIG[:, 0:5632].rearrange("p (f t) -> p f t", f=22)
            tmp = [R[:, 3072 + 256 * i:3328 + 256 * i] for i in range(2)]
            tfree = [None, None]
            ht = []
            for f in range(22):
                b = main.get()
                c = [(f * 128, f * 128 + 128)]
                t = wmm(b["ap"][:, 0:256], (f"ffn{n}_w_gate", 0), range(8), c, lambda i: H[:, i, 0:256],
                        toks, b["free"])
                t = wmm(b["ap"][:, 256:512], (f"ffn{n}_w_up", 0), range(8), c, lambda i: H[:, i, 0:256])
                t1 = a_act(tmp[f % 2], b["ap"][:, 0:256], ACT.Silu, t, tfree[f % 2])
                t1 = tt(hid[:, f, :], tmp[f % 2], b["ap"][:, 256:512], ALU.mult, t1, big_free)
                tfree[f % 2] = t1
                b["free"] = [t1]
                ht.append(t1)
            out = pair_out((f"ffn{n}_w_down", 0), range(22), lambda i: hid[:, i, :], 4,
                           lambda j: H[:, 2 * j:2 * j + 2, 0:256], ht, t)
            big_free[:] = [out[-1], out[-2]]
            return out

        big_free = []

        toks = norm_plain("ffn1_pre_g", t_x)
        toks = ffn(1, toks)
        toks = residual_norm("ffn1_post_g", 0.5, toks)
        dump("x1", X[:, :, 0:256], toks)
        toks = norm_plain("mix_pre_g", toks)

        QT = BIG[:, 0:2048].rearrange("p (j t) -> p j t", j=8)
        KT = BIG[:, 2048:4096].rearrange("p (j t) -> p j t", j=8)
        VR = BIG[:, 4096:6144].rearrange("p (a n) -> p a n", a=2)
        OT = BIG[:, 14336:16384].rearrange("p (j t) -> p j t", j=8)
        qk = pair_out(("w_qkv", 0), range(8), lambda i: H[:, i, 0:256], 8,
                      lambda j: (QT if j < 4 else KT)[:, 2 * (j % 4):2 * (j % 4) + 2, :], toks, big_free)
        vt = []
        for h in range(2):
            bs = [main.get(), main.get()]
            for k in range(8):
                ap, wt = W.get(("w_qkv", 0), k, [(2048 + 512 * h, 2560 + 512 * h)])
                for a in range(2):
                    t = mm(bs[a]["ap"][:, :], H[:, k, 128 * a:128 * a + 128], ap, k == 0, k == 7, wt,
                           bs[a]["free"] if k == 0 else None)
                W.used(t)
            for a in range(2):
                t2 = vcopy(VR[:, a, 512 * h:512 * h + 512], bs[a]["ap"][:, :], t, big_free)
                bs[a]["free"] = [t2]
                vt.append(t2)
        h_free[:] = [t]

        bt = []
        for m, B, tb in ((0, NAB, t_nb), (1, DILB, t_db)):
            for a in range(2):
                mk = B1M[:, 512 * m + 256 * a:512 * m + 256 * a + 256]
                bt.append(tt(B[:, a], B[:, a], bc(mk, 1, 8), ALU.add, tb, t_bm))

        NB_ = 3
        Sb = [R[:, 7168 + 512 * i:7680 + 512 * i] for i in range(NB_)]
        Pb = [R[:, 8704 + 512 * i:9216 + 512 * i] for i in range(NB_)]
        sb_free = [[] for _ in range(NB_)]
        pb_free = [[] for _ in range(NB_)]
        st_free = [[] for _ in range(NB_)]
        unit_no = [0]

        class Unit:

            def __init__(self, score, rows, bias, sinkcol, pv, after_score, after_v):
                self.score, self.rows, self.bias, self.sinkcol = score, rows, bias, sinkcol
                self.pv, self.after_score, self.after_v = pv, after_score, after_v
                self.i = unit_no[0] % NB_
                unit_no[0] += 1

            def first(self):
                i, rows = self.i, self.rows
                n = 512 // rows
                b = aux.get()
                t = self.score(b, self.after_score)
                s = Sb[i]
                if self.bias is not None:
                    bias, tb = self.bias
                    src = b["ap"][:, :] if rows == 1 else b["ap"][:, :].rearrange("p (r k) -> p r k", r=rows)
                    dst = s if rows == 1 else s.rearrange("p (r k) -> p r k", r=rows)
                    t = stt(dst, src, 0.125, bias, ALU.mult, ALU.add, t, tb, sb_free[i])
                else:
                    t = ts(s, b["ap"][:, :], 0.125, None, ALU.mult, None, t, sb_free[i])
                b["free"] = [t]
                sv = s.rearrange("p (r k) -> p r k", r=rows)
                mx = ST[:, i, 0:rows]
                t = dve(lambda e: e.tensor_reduce(mx, sv, AX, ALU.max), t, st_free[i])
                nm = ST[:, i, 2:2 + rows]
                if self.sinkcol is not None:
                    t = ts(nm, mx, self.sinkcol, -1.0, ALU.max, ALU.mult, t, t_v)
                else:
                    t = ts(nm, mx, -1.0, None, ALU.mult, None, t)
                den = ST[:, i, 4:4 + rows]
                tn = t
                ta = []
                for r in range(rows):
                    ta.append(a_act(sv[:, r, :], sv[:, r, :], ACT.Exp, tn, bias=nm[:, r:r + 1],
                                    accum_out=den[:, r:r + 1]))
                if self.sinkcol is not None:
                    t = a_act(ST[:, i, 6:6 + rows], nm, ACT.Exp, tn, bias=self.sinkcol)
                    t = tt(den, den, ST[:, i, 6:6 + rows], ALU.add, ta, t)
                    ta = [t]
                t = dve(lambda e: e.reciprocal(den, den), ta)
                self.t = tt(sv, sv, bc(den, 2, n), ALU.mult, t)
                st_free[i] = [self.t]

            def second(self):
                i = self.i
                b = aux.get()
                for c in range(4):
                    t = tr(b["ap"][:, 128 * c:128 * c + 128], Sb[i][:, 128 * c:128 * c + 128], self.t, b["free"])
                sb_free[i] = [t]
                t = a_act(Pb[i], b["ap"][:, :], ACT.Copy, t, pb_free[i])
                b["free"] = [t]
                self.t2 = t

            def third(self):
                t = self.pv(Pb[self.i], self.t2, self.after_v)
                pb_free[self.i] = [t]

        def run_units(units, fill=lambda: None):
            n = len(units)
            for j in range(n + 2):
                if j < n:
                    units[j].first()
                if 1 <= j <= n:
                    units[j - 1].second()
                fill()
                if j >= 2:
                    units[j - 2].third()

        otoks = []

        def block1_unit(kind, h):
            head = 8 * kind + h
            j, off = head // 2, 64 * (head % 2)

            def score(b, after):
                for a in range(2):
                    t = mm(b["ap"][:, 256 * a:256 * a + 256], QT[off:off + 64, j, 128 * a:128 * a + 128],
                           KT[off:off + 64, j, :], True, True, after, b["free"])
                return t

            def pv(P, tp, after):
                if off == 0:
                    block1_unit.bank = main.get()
                b = block1_unit.bank
                for a in range(2):
                    for kt in range(2):
                        t = mm(b["ap"][off:off + 64, 128 * a:128 * a + 128],
                               VR[:, kt, 64 * head:64 * head + 64], P[:, 256 * a + 128 * kt:256 * a + 128 * kt + 128],
                               kt == 0, kt == 1, tp, after, b["free"])
                if off:
                    t2 = vcopy(OT[:, j, :], b["ap"][:, 0:256], t, big_free)
                    b["free"] = [t2]
                    otoks.append(t2)
                return t
            return Unit(score, 2, ((NAB, DILB)[kind][:, :, h, :], bt), None, pv, qk, vt)

        mods = [modulation(0), modulation(1)]

        def fill_mod():
            for g in mods:
                if next(g, "end") != "end":
                    return

        run_units([block1_unit(kind, h) for kind in range(2) for h in range(8)], fill_mod)
        for _ in range(10):
            fill_mod()
        dump("o1", OT[:, :, :], otoks)
        for part, g in ((0, "na_out_g"), (1, "dil_out_g")):
            t, m = rstd(lambda i: OT[:, 4 * part + i, :], 4, 256, 512, s_free, otoks)
            s_free[:] = [m]
            ts_ = []
            for i in range(4):
                ts_.append(stt(OT[:, 4 * part + i, :], OT[:, 4 * part + i, :], vec(g, i), RS[:, 0:256],
                               ALU.mult, ALU.mult, t))
            rs_free[:] = [ts_[-1]]
            otoks = otoks + ts_
        toks = pair_out(("w_out", 0), range(8), lambda i: OT[:, i, :], 4,
                        lambda j: H[:, 2 * j:2 * j + 2, 0:256], otoks, h_free)
        big_free[:] = [toks[-1], toks[-2]]
        toks = residual_norm("mix_post_g", 1.0, toks)
        dump("x2", X[:, :, 0:256], toks)
        toks = norm_plain("ffn2_pre_g", toks)
        toks = ffn(2, toks)
        xt = residual_norm("ffn2_post_g", 0.5, toks)
        dump("x3", X[:, :, 0:256], xt)
        ct_ = [t_x]

        G = BIG[:, 0:12288].rearrange("p (n t) -> p n t", n=24)
        Qh = BIG[:, 12288:14336].rearrange("p (h t) -> p h t", h=4)
        KF = BIG[:, 14336:16384].rearrange("p (h t) -> p h t", h=4)
        KB = R[:, 0:2048].rearrange("p (h t) -> p h t", h=4)
        EF = R[:, 2048:4104].rearrange("p (h s t) -> p h s t", h=4, s=2)
        EB = R[:, 4104:6160].rearrange("p (h s t) -> p h s t", h=4, s=2)
        VH = R[:, 6160:8208].rearrange("p (a n) -> p a n", a=4)
        AT = R[:, 8208:10256].rearrange("p (a h t) -> p a h t", a=2, h=4)
        D = [S[:, 2048 * i:2048 * i + 2048].rearrange("p (z h t) -> p z h t", z=2, h=4) for i in range(2)]

        c_ = {}
        at = 0
        for n, w in (("k", 128), ("v", 128), ("i", 512), ("ff", 512), ("fb", 512), ("q", 512), ("qh", 512),
                     ("gh", 512), ("four", 512), ("gate", 3072)):
            c_[n] = at
            at += w

        def adaln(l, i, T, xt, ct):
            t, m = rstd(lambda k: X[:, k, 0:T], 8, T, 1024, s_free, xt, ct)
            s_free[:] = [m]
            toks = []
            for k in range(8):
                for c in range(T // 256):
                    sl = slice(256 * c, 256 * c + 256)
                    t2 = stt(H[:, k, sl], X[:, k, sl], GS[:, l, i, k, c:c + 1], RS[:, sl], ALU.mult, ALU.mult,
                             t, h_free, t_mod[l])
                    toks.append(a_act(H[:, k, sl], H[:, k, sl], ACT.Identity, t2,
                                      bias=MOD[:, l, 24 * i + k, c:c + 1]))
            rs_free[:] = [t2]
            return toks

        for l in range(2):
            T = 512 if l == 0 else 256
            win = ("w_in_2", l)
            ht = adaln(l, 0, 512, xt, ct_)
            dump(f"h{l}", H[:, :, :], ht)
            rhsT = lambda i: H[:, i, 0:T]
            rhs512 = lambda i: H[:, i, :]

            f_tok = []
            for dr, seg in ((0, "ff"), (1, "fb")):
                Z = BIG[:, 6144 * dr:6144 * dr + 2048].rearrange("p (h t) -> p h t", h=4)
                P1 = BIG[:, 6144 * dr + 2048:6144 * dr + 4096].rearrange("p (h t) -> p h t", h=4)
                LF = BIG[:, 6144 * dr + 4096:6144 * dr + 6144].rearrange("p (h t) -> p h t", h=4)
                A = S[:, :].rearrange("p (z h t) -> p z h t", z=2, h=4)
                if l == 0:
                    loglb = [LOG_FLOOR] * 4
                    neglb = [vec("neglb", 0)] * 4
                    oml = [1.0] * 4
                else:
                    loglb = [LB[:, 0, 4 * dr + h:4 * dr + h + 1] for h in range(4)]
                    neglb = [LB[:, 4, 4 * dr + h:4 * dr + h + 1] for h in range(4)]
                    oml = [LB[:, 1, 4 * dr + h:4 * dr + h + 1] for h in range(4)]
                zt, a1 = [], []
                for h in range(4):
                    b = main.get()
                    c = c_[seg] + 128 * h
                    t = wmm(b["ap"][:, :], win, range(8), [(c, c + 128)], rhs512, ht, b["free"])
                    t = a_act(Z[:, h, :], b["ap"][:, :], ACT.Copy, t, big_free)
                    b["free"] = [t]
                    zt.append(t)
                    a1.append(a_act(A[:, 1, h, :], Z[:, h, :], ACT.Abs, t, s_free, t_lb, bias=neglb[h]))
                a1.append(stt(A[:, 0], Z, -1.0, Z, ALU.mult, ALU.max, zt, s_free))
                t = a_act(A, A, ACT.Exp, a1, scale=-1.0)
                tl = a_act(A, A, ACT.Ln, t, bias=1.0)
                tp = ts(P1, Z, 0.0, None, ALU.max, None, zt, big_free)
                tz = []
                for h in range(4):
                    tz.append(stt(Z[:, h, :], Z[:, h, :], loglb[h], P1[:, h, :], ALU.max, ALU.subtract, tp, a1))
                td = tt(LF, A[:, 1], A[:, 0], ALU.subtract, tl, big_free)
                tf = tt(LF, LF, Z, ALU.add, td, tz)
                tp = tt(P1, P1, A[:, 0], ALU.add, tl, tz)
                s_free[:] = [tp, td]
                K = (KF, KB)[dr]
                tk = a_act(K, P1, ACT.Exp, tp, big_free, scale=-1.0)
                for h in range(4):
                    if l:
                        tk = ts(K[:, h, :], K[:, h, :], oml[h], None, ALU.mult, None, tk)
                E = (EF, EB)[dr]
                tm = dve(lambda e, E=E: e.memset(E[:, :, :, 0:1], 0.0), big_free)
                for h in range(4):
                    for s in range(2):
                        t = dve(lambda e, E=E, LF=LF, h=h, s=s: e.tensor_tensor_scan(
                            E[:, h, s, 1:257], ones256,
                            LF[:, h, 256 * s:256 * s + 256], 0.0, ALU.mult, ALU.add), tf, t_c)
                f_tok += [tk, t, tm]
            z_done = f_tok
            dump(f"kf{l}", KF, f_tok)
            dump(f"ef{l}", EF, f_tok)
            dump(f"eb{l}", EB, f_tok)

            hq = []
            for h in range(4):
                b = main.get()
                c = c_["qh"] + 128 * h
                t = wmm(b["ap"][:, 0:T], win, range(8), [(c, c + 128)], rhsT, ht, b["free"])
                t = a_act(Qh[:, h, 0:T], b["ap"][:, 0:T], ACT.Silu, t, big_free)
                b["free"] = [t]
                hq.append(t)
            bs = [main.get() for _ in range(4)]
            for k in range(8):
                ap, wt = W.get(win, k, [(c_["i"], c_["i"] + 512)])
                for a in range(4):
                    t = mm(bs[a]["ap"][:, :], H[:, k, 128 * a:128 * a + 128], ap, k == 0, k == 7, wt, ht,
                           bs[a]["free"] if k == 0 else None)
                W.used(t)
            hv = []
            for a in range(4):
                t2 = a_act(VH[:, a, :], bs[a]["ap"][:, :], ACT.Copy, t, big_free)
                bs[a]["free"] = [t2]
                hv.append(t2)

            g_tok = []

            def gates():
                for n in range(24):
                    b = main.get()
                    c = c_["gate"] + 128 * n
                    t = wmm(b["ap"][:, 0:T], win, range(8), [(c, c + 128)], rhsT, ht, b["free"])
                    t = a_act(G[:, n, 0:T], b["ap"][:, 0:T], ACT.Copy, t, z_done)
                    b["free"] = [t]
                    g_tok.append(t)
                    yield

            gate_fill = gates()

            def fill(n=1):
                for _ in range(n):
                    next(gate_fill, None)

            d_free = [list(s_free), list(s_free)]
            at_free = list(big_free)
            ST0 = [KB[:, :, 256 + 128 * z:384 + 128 * z] for z in range(2)]

            def states():
                rows = []
                for dr in range(2):
                    E, K, Dk = (EF, EB)[dr], (KF, KB)[dr], D[0][:, dr]
                    if dr == 0:
                        te = [a_act(Dk[:, h, :], E[:, h, 1, 1:257], ACT.Exp, f_tok, d_free[0], scale=-1.0,
                                    bias=E[:, h, 1, 256:257]) for h in range(4)]
                    else:
                        te = a_act(Dk, E[:, :, 1, 0:256], ACT.Exp, f_tok, d_free[0])
                    t = tt(Dk, Dk, K[:, :, 256:512], ALU.mult, te)
                    fill()
                    KR = D[1][:, dr].rearrange("p h t -> p (h t)")
                    for a in range(2):
                        b = aux.get()
                        for h in range(4):
                            t2 = tr(b["ap"][:, 128 * h:128 * h + 128], Dk[:, h, 128 * a:128 * a + 128], t, b["free"])
                        t2 = vcopy(KR[:, 512 * a:512 * a + 512], b["ap"][:, :], t2, d_free[1])
                        b["free"] = [t2]
                        rows.append(t2)
                done = []
                for dr in range(2):
                    b = aux.get()
                    KR = D[1][:, dr].rearrange("p h t -> p (h t)").rearrange("p (a h k) -> p a h k", a=2, h=4)
                    for h in range(4):
                        for a in range(2):
                            t = mm(b["ap"][:, 128 * h:128 * h + 128], KR[:, a, h, :],
                                   VH[:, 2 + a, 128 * h:128 * h + 128], a == 0, a == 1, rows, hv, b["free"])
                    t = vcopy(ST0[dr], b["ap"][:, :].rearrange("p (h k) -> p h k", h=4), t)
                    b["free"] = [t]
                    done.append(t)
                d_free[:] = [[t], [t]]
                return done

            def recurrence(s):
                c0 = 256 * s
                q = Qh[:, :, c0:c0 + 256]
                last = []
                Dd = D[0]
                t = tt(Dd[:, 1], KF[:, :, c0:c0 + 256], KB[:, :, c0:c0 + 256], ALU.add, f_tok, d_free[0])
                for a in range(2):
                    b = aux.get()
                    for h in range(4):
                        t2 = mm(b["ap"][:, 128 * h:128 * h + 128], Dd[:, 1, h, 128 * a:128 * a + 128],
                                q[:, h, 128 * a:128 * a + 128], True, True, t, hq, b["free"])
                    t3 = vcopy(AT[:, a, :, 128 * a:128 * a + 128], b["ap"][:, :].rearrange("p (h t) -> p h t", h=4),
                               t2, at_free)
                    b["free"] = [t3]
                    last.append(t3)
                d_free[0] = [t2]
                for lv in range(8):
                    Dd = D[(lv + 1) % 2]
                    hh = 1 << lv
                    nbk = 128 // hh

                    def v(ap, u):
                        return ap.rearrange("p h (b u j) -> p h b u j", u=2, j=hh)[:, :, :, u, :]
                    Ein = (EF[:, :, s, 1:257], EB[:, :, s, 1:257])
                    Eex = (EF[:, :, s, 0:256], EB[:, :, s, 0:256])

                    def mid(E):
                        m = v(E, 1)[:, :, :, 0:1]
                        a = [list(x) for x in m.ap]
                        m0 = E.rearrange("p h (b u j) -> p h b u j", u=2, j=hh)[:, :, :, 1, 0]
                        return bc(m0, 3, hh)
                    df = d_free[(lv + 1) % 2]
                    te = [tt(v(Dd[:, 0], 1), v(Ein[0], 1), mid(Eex[0]), ALU.subtract, f_tok, df),
                          tt(v(Dd[:, 1], 0), mid(Eex[0]), v(Ein[0], 0), ALU.subtract, f_tok, df),
                          tt(v(Dd[:, 0], 0), mid(Eex[1]), v(Eex[1], 0), ALU.subtract, f_tok, df),
                          tt(v(Dd[:, 1], 1), v(Eex[1], 1), mid(Eex[1]), ALU.subtract, f_tok, df)]
                    te = a_act(Dd, Dd, ACT.Exp, te)
                    tq = [tt(Dd[:, 0], Dd[:, 0], q, ALU.mult, te, hq),
                          tt(v(Dd[:, 1], 0), v(Dd[:, 1], 0), v(KF[:, :, c0:c0 + 256], 0), ALU.mult, te),
                          tt(v(Dd[:, 1], 1), v(Dd[:, 1], 1), v(KB[:, :, c0:c0 + 256], 1), ALU.mult, te)]
                    fill()
                    for a in range(2):
                        b = aux.get()
                        qa = a if lv < 7 else 1 - a
                        for h in range(4):
                            t2 = mm(b["ap"][:, 128 * h:128 * h + 128], Dd[:, 1, h, 128 * a:128 * a + 128],
                                    Dd[:, 0, h, 128 * qa:128 * qa + 128], True, True, tq, b["free"])
                        src = b["ap"][:, :].rearrange("p (h t) -> p h t", h=4)
                        dst = AT[:, a, :, 128 * qa:128 * qa + 128]
                        if lv < 7:
                            mk = bc(LM[:, 128 * lv:128 * lv + 128], 1, 4)
                            t3 = dve(lambda e, dst=dst, mk=mk, src=src: e.copy_predicated(dst, mk, src),
                                     t2, t_lm, last)
                        else:
                            t3 = vcopy(dst, src, t2, at_free)
                        b["free"] = [t3]
                        last.append(t3)
                    d_free[(lv + 1) % 2] = [t2]
                inter = []
                if s == 0:
                    Dd = D[0]
                    t1 = a_act(Dd[:, 0], EF[:, :, 0, 1:257], ACT.Exp, f_tok, d_free[0])
                    for h in range(4):
                        t2 = a_act(Dd[:, 1, h, :], EB[:, h, 0, 0:256], ACT.Exp, f_tok, d_free[0], scale=-1.0,
                                   bias=EB[:, h, 0, 256:257])
                    inter = [tt(Dd[:, 0], Dd[:, 0], q, ALU.mult, t1, hq), tt(Dd[:, 1], Dd[:, 1], q, ALU.mult, t2, hq)]
                otok = []
                for hp in range(2):
                    b = aux.get()
                    for h in (2 * hp, 2 * hp + 1):
                        o = b["ap"][:, 256 * (h % 2):256 * (h % 2) + 256]
                        n = 4 if s == 0 else 2
                        for a in range(2):
                            t = mm(o, VH[:, 2 * s + a, 128 * h:128 * h + 128], AT[:, a, h, :], a == 0, a == n - 1,
                                   last, hv, b["free"])
                        if s == 0:
                            for z in range(2):
                                t = mm(o, ST0[z][:, h, :], Dd[:, z, h, :], False, z == 1, inter, b_s)
                    t2 = vcopy(Qh[:, 2 * hp:2 * hp + 2, c0:c0 + 256], b["ap"][:, :].rearrange("p (h t) -> p h t", h=2), t)
                    b["free"] = [t2]
                    otok.append(t2)
                at_free[:] = [t]
                d_free[0] = [d_free[0], t]
                return otok, t

            o_tok = []
            if l == 0:
                o_tok += recurrence(1)[0]
            b_s = states()
            ot, lastmm = recurrence(0)
            o_tok += ot
            hg_done = [lastmm] + o_tok
            s_free[:] = [lastmm]
            dump(f"oh{l}", Qh[:, :, 0:T], o_tok)
            fill(24)

            GH = R[:, 0:2048].rearrange("p (h t) -> p h t", h=4)
            gt = []
            for h in range(4):
                b = main.get()
                c = c_["gh"] + 128 * h
                t = wmm(b["ap"][:, 0:T], win, range(8), [(c, c + 128)], rhsT, ht, b["free"])
                t = a_act(GH[:, h, 0:T], b["ap"][:, 0:T], ACT.Silu, t, hg_done)
                b["free"] = [t]
                gt.append(t)
            FR = R[:, 4096:6144].rearrange("p (g t) -> p g t", g=4)
            ft = []
            for g in range(4):
                b = main.get()
                c = c_["four"] + 128 * g
                t = wmm(b["ap"][:, 0:T], win, range(8), [(c, c + 128)], rhsT, ht, b["free"])
                t = vcopy(FR[:, g, 0:T], b["ap"][:, 0:T], t, hg_done)
                b["free"] = [t]
                ft.append(t)
            rt = []
            for h in range(4):
                t, m = rstd(lambda i: Qh[:, h, 0:T], 1, T, 128, s_free, o_tok,
                            sq=lambda i, h=h: S3[:, h, 0:T])
                t = stt(Qh[:, h, 0:T], Qh[:, h, 0:T], vec("hgrn_norm_g_2", l), RS[:, 0:T], ALU.mult, ALU.mult, t)
                rs_free[:] = [t]
                rt.append(tt(Qh[:, h, 0:T], Qh[:, h, 0:T], GH[:, h, 0:T], ALU.mult, t, gt))
            s_free[:] = [m]
            dump(f"ohr{l}", Qh[:, :, 0:T], rt)

            OF = R[:, 2048:4096].rearrange("p (g t) -> p g t", g=4)
            Zs = [R[:, 6144 + 512 * i:6656 + 512 * i] for i in range(2)]
            zfree = [hg_done, hg_done]
            cdsd, ctm, nst = const["cdsd"], const["ct"], const["nst"]
            oft = []
            n = 0
            for g in range(4):
                bo = main.get()
                for s in range(T // 256):
                    b = aux.get()
                    for a in range(2):
                        t = mm(b["ap"][:, 256 * a:256 * a + 256],
                               FR[:, g, 256 * s + 128 * a:256 * s + 128 * a + 128], cdsd, True, True, ft[g], b["free"])
                    Zb = Zs[n % 2]
                    t = vcopy(Zb, b["ap"][:, :], t, zfree[n % 2])
                    b["free"] = [t]
                    o = bo["ap"][:, 256 * s:256 * s + 256]
                    for a in range(2):
                        t2 = mm(o, Zb[:, 256 * a:256 * a + 128], ctm[:, 256 * a:256 * a + 256], a == 0, False, t,
                                bo["free"])
                        t2 = mm(o, Zb[:, 256 * a + 128:256 * a + 256], nst[:, 256 * a:256 * a + 256], False, a == 1)
                    zfree[n % 2] = [t2]
                    n += 1
                t = a_act(OF[:, g, 0:T], bo["ap"][:, 0:T], ACT.Copy, t2, hg_done)
                bo["free"] = [t]
                oft.append(t)
            four_done = [t2]
            dump(f"of{l}", OF[:, :, 0:T], oft)

            Q2 = R[:, 4096:6144].rearrange("p (j t) -> p j t", j=4)
            K2 = R[:, 6144:6656]
            V2 = R[:, 6656:7168].rearrange("p (a n) -> p a n", a=4)
            OA = BIG[:, 14336:16384].rearrange("p (j t) -> p j t", j=4)
            vb = [main.get() for _ in range(4)]
            for k in range(8):
                ap, wt = W.get(win, k, [(c_["v"], c_["v"] + 128)])
                for a in range(4):
                    t = mm(vb[a]["ap"][:, 0:128], H[:, k, 128 * a:128 * a + 128], ap, k == 0, k == 7,
                           wt, ht, vb[a]["free"] if k == 0 else None)
                W.used(t)
            v2t = []
            for a in range(4):
                v2t.append(vcopy(V2[:, a, :], vb[a]["ap"][:, 0:128], t, four_done))
                vb[a]["free"] = [v2t[-1]]

            def head_norm(dst, cols, TT, gname, sq):
                b = main.get()
                t = wmm(b["ap"][:, 0:TT], win, range(8), cols, lambda i: H[:, i, 0:TT], ht, b["free"])
                t = vcopy(dst[:, 0:TT], b["ap"][:, 0:TT], t, four_done)
                b["free"] = [t]
                t, m = rstd(lambda i: dst[:, 0:TT], 1, TT, 64, s_free, t, ones_=blk, sq=lambda i: sq[:, 0:TT])
                t = stt(dst[:, 0:TT], dst[:, 0:TT], vec(gname, l), RS[:, 0:TT], ALU.mult, ALU.mult, t)
                rs_free[:] = [t]
                b = aux.get()
                t2 = mm(b["ap"][:, 0:256], const["perm"], dst[:, 0:256], True, True, t, b["free"])
                t2 = tt(sq[:, 0:256], b["ap"][:, 0:256], const["ropes"], ALU.mult, t2, m)
                b["free"] = [t2]
                t = tt(dst[:, 0:256], dst[:, 0:256], const["ropec"], ALU.mult, t, t2)
                return tt(dst[:, 0:256], dst[:, 0:256], sq[:, 0:256], ALU.add, t, t2)

            kt_ = head_norm(K2, [(c_["k"], c_["k"] + 128)], 512, "k_norm_g_2", S3[:, 4, :])
            qt_ = []
            for j in range(4):
                c = c_["q"]
                qt_.append(head_norm(Q2[:, j, :], [(c + 64 * j, c + 64 * j + 64), (c + 64 * j + 256, c + 64 * j + 320)],
                                     T, "q_norm_g_2", S3[:, j, :]))
            s_free[:] = [kt_, qt_[-1]]
            h_free[:] = [pe.last]
            dump(f"q{l}", Q2[:, :, 0:T], qt_)
            dump(f"k{l}", K2, kt_)
            a_tok = []
            qkt = [kt_] + qt_

            def x_unit(j, kv, a):
                off = 64 * kv

                def score(b, after):
                    return mm(b["ap"][:, :], Q2[off:off + 64, j, 128 * a:128 * a + 128], K2[off:off + 64, :],
                              True, True, after, b["free"])

                def pv(P, tp, after):
                    if a == 0 and kv == 0:
                        x_unit.bank = main.get()
                    b = x_unit.bank
                    for c in range(4):
                        t = mm(b["ap"][off:off + 64, 128 * a:128 * a + 128], V2[:, c, off:off + 64],
                               P[:, 128 * c:128 * c + 128], c == 0, c == 3, tp, after, b["free"])
                    if a == 1 and kv == 1:
                        t2 = vcopy(OA[:, j, 0:256], b["ap"][:, 0:256], t, hg_done)
                        b["free"] = [t2]
                        a_tok.append(t2)
                    return t
                return Unit(score, 1, (const["win"][:, 512 * a:512 * a + 512], None),
                            vec("attn_sink_2", 8 * l + j + 4 * kv), pv, qkt, v2t)

            def c_unit(j, kv):
                off = 64 * kv

                def score(b, after):
                    for a in range(2):
                        t = mm(b["ap"][:, 256 * a:256 * a + 256], Q2[off:off + 64, j, 256 + 128 * a:384 + 128 * a],
                               K2[off:off + 64, 256:512], True, True, after, b["free"])
                    return t

                def pv(P, tp, after):
                    if kv == 0:
                        c_unit.bank = main.get()
                    b = c_unit.bank
                    for a in range(2):
                        for c in range(2):
                            t = mm(b["ap"][off:off + 64, 128 * a:128 * a + 128], V2[:, 2 + c, off:off + 64],
                                   P[:, 256 * a + 128 * c:256 * a + 128 * c + 128], c == 0, c == 1, tp, after,
                                   b["free"])
                    if kv == 1:
                        t2 = vcopy(OA[:, j, 256:512], b["ap"][:, 0:256], t, hg_done)
                        b["free"] = [t2]
                        a_tok.append(t2)
                    return t
                return Unit(score, 2, None, vec("attn_sink_2", 8 * l + j + 4 * kv), pv, qkt, v2t)

            units = [x_unit(j, kv, a) for j in range(4) for kv in range(2) for a in range(2)]
            if l == 0:
                units += [c_unit(j, kv) for j in range(4) for kv in range(2)]
            run_units(units)
            dump(f"oa{l}", OA[:, :, 0:T], a_tok)

            sg = [a_act(G[:, n, 0:T], G[:, n, 0:T], ACT.Sigmoid, g_tok[n])
                  for n in [8 * br + d for d in range(8) for br in range(3)]]
            sig = {8 * br + d: sg[3 * d + br] for d in range(8) for br in range(3)}
            yt = []
            br_src = [(OF, oft), (OA, a_tok), (Qh, rt)]
            for d in range(8):
                acc = S3[:, d, 0:T]
                prev = None
                for br, (src, st) in enumerate(br_src):
                    b = main.get()
                    c = [(128 * d, 128 * d + 128)]
                    t = None
                    for i in range(4):
                        key = ("w_branch_2", l, br, "split" if br == 1 else None)
                        ap, wt = W.get(key, i, c)
                        t = mm(b["ap"][:, 0:T], ap, src[:, i, 0:T], i == 0, i == 3, wt, st, b["free"] if i == 0 else None)
                        W.used(t)
                    if br == 0:
                        prev = tt(acc, b["ap"][:, 0:T], G[:, d, 0:T], ALU.mult, t, sig[d], s_free)
                        b["free"] = [prev]
                    else:
                        gg = G[:, 8 * br + d, 0:T]
                        t = tt(gg, b["ap"][:, 0:T], gg, ALU.mult, t, sig[8 * br + d])
                        b["free"] = [t]
                        prev = tt(acc, acc, gg, ALU.add, t, prev)
                yt.append(prev)
            dump(f"y{l}", S3[:, :, 0:T], yt)

            def add_out(name, ks, rhs, mod_i, *after):
                xt, ct = [], []
                for d in range(8):
                    b = main.get()
                    t = wmm(b["ap"][:, 0:T], name, ks, [(128 * d, 128 * d + 128)], rhs, after, b["free"])
                    for c in range(T // 256):
                        sl = slice(256 * c, 256 * c + 256)
                        t2 = stt(X[:, d, sl], b["ap"][:, sl], MOD[:, l, mod_i + d, c:c + 1], X[:, d, sl],
                                 ALU.mult, ALU.add, t)
                        (ct if c else xt).append(t2)
                    b["free"] = [t2]
                return xt, ct, t

            xt, ct, t = add_out(("w_out_2", l), range(8), lambda i: S3[:, i, 0:T], 16, yt)
            s_free[:] = [t]
            dump(f"xa{l}", X[:, :, 0:T], xt, ct)
            h2 = adaln(l, 1, T, xt, ct)
            HID = BIG[:, :].rearrange("p (f t) -> p f t", f=32)
            mt = []
            for f in range(32):
                b = main.get()
                t = wmm(b["ap"][:, 0:T], ("w_ff1_2", l), range(8), [(128 * f, 128 * f + 128)], rhsT, h2, b["free"])
                t = a_act(HID[:, f, 0:T], b["ap"][:, 0:T], ACT.Relu, t, yt)
                t = tt(HID[:, f, 0:T], HID[:, f, 0:T], b["ap"][:, 0:T], ALU.mult, t)
                b["free"] = [t]
                mt.append(t)
            h_free[:] = [pe.last]
            xt, ct, t = add_out(("w_ff2_2", l), range(32), lambda i: HID[:, i, 0:T], 40, mt)
            big_free[:] = [t]
            ct_ = ct
            dump(f"xb{l}", X[:, :, 0:T], xt, ct)

        t_o = sync.dma(lambda e: e.dma_start(d_out.rearrange("p (k t) -> p k t", k=8), X[:, :, 0:256]),
                       s_out, 16, xt)
        sync(None, t_o, t_ln, t_sk, t_nk, outs)

        d_w = dram("wstream", (W.n, 128, 2048))
        for q in (sync, pe, act, dve, pool):
            q.number()
        with nc.Block() as block:
            block.sync(sync.emit)
            block.tensor(pe.emit)
            block.scalar(act.emit)
            block.vector(dve.emit)
            block.gpsimd(pool.emit)
        return W.n


def weight(inputs, name):
    if name[0] == "w_branch_2":
        w = inputs["w_branch_2"][name[1], name[2]]
        if name[3]:
            w = w.reshape(2, 4, 64, -1).transpose(1, 0, 2, 3).reshape(512, -1)
        return w
    return inputs[name[0]][name[1]]


def pack_stream(inputs, order, blocks):
    out = np.zeros((blocks, 128, 2048), np.float32)
    for n, col, name, k, cols in order:
        w = weight(inputs, name)
        for a, b in cols:
            out[n, :, col:col + b - a] = w[128 * k:128 * k + 128, a:b]
            col += b - a
    return out


def columns(v):
    return np.ascontiguousarray(np.asarray(v).reshape(-1, 128).T)


def pack_vecs(inputs):
    v = np.zeros((128, NVEC), np.float32)

    def put(name, a):
        at, n = VEC[name]
        assert a.shape == (128, n), (name, a.shape)
        v[:, at:at + n] = a
    for name in ("ffn1_pre_g", "ffn1_post_g", "mix_pre_g", "na_out_g", "dil_out_g", "mix_post_g", "ffn2_pre_g",
                 "ffn2_post_g", "b_mod_2", "norm1_g_2", "norm2_g_2", "hgrn_lb_logits_2", "hgrn_norm_g_2"):
        put(name, columns(inputs[name]))
    put("cc", np.stack([columns(inputs["c_2"]), columns(inputs["c_ctx_2"])], 2).reshape(128, 16))
    for name in ("q_norm_g_2", "k_norm_g_2"):
        put(name, np.concatenate([inputs[name].T, inputs[name].T], 0))
    put("attn_sink_2", np.broadcast_to(inputs["attn_sink_2"].reshape(1, 16), (128, 16)))
    put("neglb", np.full((128, 1), -LOG_FLOOR, np.float32))
    put("eps", np.full((128, 1), EPS, np.float32))
    return v


def kernel(debug=None, **inputs):
    import concourse.bacc as bacc
    from concourse.bass_utils import run_bass_kernel_spmd

    inputs = {k: np.asarray(v) for k, v in inputs.items()}
    consts = const_arrays()
    sizes = {n: consts[n].shape[1] for n in CONSTS}
    shapes = {"consts": sizes}
    order = []
    nc = bacc.Bacc("TRN2", target_bir_lowering=False, num_devices=1)
    blocks = build_program(nc, shapes, order, debug)
    xc = np.concatenate([inputs["x"][0], inputs["ctx_2"][0]], 0).T
    arrays = {
        "xin": np.ascontiguousarray(xc.reshape(8, 128, 512).transpose(1, 0, 2)).reshape(128, 4096),
        "wstream": pack_stream(inputs, order, blocks),
        "consts": np.ascontiguousarray(np.concatenate([consts[n] for n in CONSTS], 1)),
        "b1mask": consts["b1mask"],
        "vecs": pack_vecs(inputs),
        "lmask": level_masks(),
        "onehot": bucket_onehot(),
        "t5t": np.ascontiguousarray(inputs["t5_rel_bias"].T),
        "narel": np.ascontiguousarray(inputs["na_rel_bias"].reshape(8, 465)),
    }
    r = run_bass_kernel_spmd(nc, [arrays], core_ids=[0])
    y = r.results[0]["yout"]
    return np.ascontiguousarray(y.reshape(128, 8, 256).transpose(2, 1, 0)).reshape(1, 256, 1024)
```

```python
from contextlib import ExitStack

import numpy as np

import concourse.bass as bass
from concourse import mybir

ALU = mybir.AluOpType
ACT = mybir.ActivationFunctionType
F32 = mybir.dt.float32
F32R = mybir.dt.float32r
U8 = mybir.dt.uint8
AX = mybir.AxisListType.X

NEG = -1e30
EPS = 1e-6
LOG_FLOOR = float(np.log(np.float32(1e-30)))
NRAW, NSPL, AHEAD = 4, 3, 2
KB_ = 1024
ARENA = 96 * KB_ + 512


def const_arrays():
    i = np.arange(128)
    t = np.arange(256)
    c = {}
    c["ident"] = np.eye(128)
    c["ones"] = np.ones((128, 128))
    c["blk"] = (i[:, None] // 64 == i[None, :] // 64).astype(float)
    perm = np.zeros((128, 128))
    for d in range(128):
        if d % 32 < 16:
            perm[d + 16, d] = -1.0
        else:
            perm[d - 16, d] = 1.0
    c["perm"] = perm
    freq = (np.float32(10000.0) ** (-np.arange(0, 32, 2, dtype=np.float32) / np.float32(32))).astype(np.float32)
    pos = np.where((i[:, None] % 64) < 32, (t // 64)[None, :], (t % 64)[None, :]).astype(np.float32)
    ang = (pos * freq[i % 16][:, None]).astype(np.float32).astype(np.float64)
    c["ropec"], c["ropes"] = np.cos(ang), np.sin(ang)
    w = 2 * np.pi * np.outer(i, i) / 128
    c["cdsd"] = np.concatenate([np.cos(w), np.sin(w)], 1) / np.sqrt(128.0)
    w = 2 * np.pi * (np.outer(t, t) % 256) / 256
    c["ct"] = np.concatenate([np.cos(w)[:128], np.cos(w)[128:]], 1) / 16.0
    c["nst"] = -np.concatenate([np.sin(w)[:128], np.sin(w)[128:]], 1) / 16.0
    k = np.arange(256)
    win = []
    for a in range(2):
        q = a * 128 + i
        win.append(np.where(np.abs(k[None] - q[:, None]) <= 128, 0.0, NEG))
    c["win"] = np.concatenate(win, 1)
    na, dil = [], []
    for a in range(2):
        q = a * 128 + i
        s = np.clip(q % 64 - 8, 0, 48)
        kc = k % 64
        na.append(np.where((kc[None] >= s[:, None]) & (kc[None] < s[:, None] + 16), 0.0, NEG))
        d = k[None] - q[:, None]
        n = (np.abs(d) <= 64).astype(int) + (d % 4 == 0) + (d % 16 == 0)
        dil.append(np.where(n > 0, np.log(np.maximum(n, 1)), NEG))
    c["b1mask"] = np.concatenate(na + dil, 1)
    return {n: np.ascontiguousarray(v, dtype=np.float32) for n, v in c.items()}


def bucket_onehot():
    rel = np.arange(-255, 257)
    n = np.abs(rel)
    large = 8 + (np.log(np.maximum(n, 1).astype(np.float32) / np.float32(8))
                 / np.float32(np.log(1024 / 8)) * np.float32(8)).astype(np.int32)
    b = np.where(rel > 0, 16, 0) + np.where(n < 8, n, np.minimum(large, 15))
    return (np.arange(32)[:, None] == b[None, :]).astype(np.float32)


def level_masks():
    i = np.arange(128)
    m = []
    for lv in range(7):
        h = 1 << lv
        same = i[:, None] // (2 * h) == i[None, :] // (2 * h)
        m.append(same & ((i[:, None] // h) % 2 != (i[None, :] // h) % 2))
    return np.concatenate(m, 1).astype(np.float32)


CONSTS = ["ident", "ones", "blk", "perm", "ropec", "ropes", "cdsd", "ct", "nst", "win"]
VEC = {}


def vec_columns():
    at = 0
    for name, n in [("ffn1_pre_g", 8), ("ffn1_post_g", 8), ("mix_pre_g", 8), ("na_out_g", 4), ("dil_out_g", 4),
                    ("mix_post_g", 8), ("ffn2_pre_g", 8), ("ffn2_post_g", 8), ("cc", 16), ("b_mod_2", 96),
                    ("norm1_g_2", 16), ("norm2_g_2", 16), ("q_norm_g_2", 2), ("k_norm_g_2", 2),
                    ("hgrn_lb_logits_2", 16), ("hgrn_norm_g_2", 2), ("attn_sink_2", 16), ("eps", 1), ("neglb", 1)]:
        VEC[name] = (at, n)
        at += n
    return at


NVEC = vec_columns()


class Tok:
    def __init__(self, sem=None, val=None):
        self.sem, self.val, self.used = sem, val, False


class Queue:

    def __init__(self, sem):
        self.sem, self.ops = sem, []

    def __call__(self, fn, *after):
        tok = self.last = Tok()
        self.ops.append((fn, self.flat(after), tok, None))
        return tok

    def dma(self, fn, sem, val, *after):
        self.ops.append((fn, self.flat(after), None, sem))
        return Tok(sem, val)

    @staticmethod
    def flat(x):
        out = []
        for t in x:
            if isinstance(t, (list, tuple)):
                out += Queue.flat(t)
            elif t is not None:
                t.used = True
                out.append(t)
        return out

    def number(self):
        n = 0
        for _, _, tok, _ in self.ops:
            if tok is not None and tok.used:
                n += 1
                tok.sem, tok.val = self.sem, n

    def emit(self, eng):
        seen = {}
        for fn, after, tok, dsem in self.ops:
            need = {}
            for t in after:
                if self.skip_own and t.sem is self.sem:
                    continue
                k = id(t.sem)
                if t.val > need.get(k, (None, 0))[1]:
                    need[k] = (t.sem, t.val)
            for k, (s, v) in need.items():
                if seen.get(k, 0) < v:
                    eng.wait_ge(s, v)
                    seen[k] = v
            if fn is None:
                continue
            ins = fn(eng)
            if dsem is not None:
                ins.then_inc(dsem, 16)
            elif tok.used:
                ins.then_inc(self.sem, 1)

    skip_own = False


def bc(ap, dim, n):
    a = [list(x) for x in ap.ap]
    a.insert(dim, [0, n])
    return bass.AP(ap.tensor, ap.offset, a)


class Banks:

    def __init__(self, tensors):
        self.banks = [{"ap": t, "free": []} for t in tensors]
        self.at = 0

    def get(self):
        b = self.banks[self.at % len(self.banks)]
        self.at += 1
        return b


def build_program(nc, csizes, plan, debug=None):
    ctx = ExitStack()

    def sb(name, shape, dt=F32):
        return ctx.enter_context(nc.sbuf_tensor(name, shape, dt))

    def sem(name):
        return ctx.enter_context(nc.semaphore(name))

    def dram(name, shape, dt=F32, kind="ExternalInput"):
        return nc.dram_tensor(name, shape, dt, kind=kind).ap()

    with ctx:
        order = []
        nconst = sum(csizes.values())
        d_x = dram("xin", (128, 4096))
        d_c = dram("consts", (128, nconst))
        d_bm = dram("b1mask", (128, 1024))
        d_v = dram("vecs", (128, NVEC))
        d_m = dram("lmask", (128, 896))
        d_oh = dram("onehot", (32, 512))
        d_t5 = dram("t5t", (32, 8))
        d_na = dram("narel", (8, 465))
        d_out = dram("yout", (128, 2048), kind="ExternalOutput")
        d_line = dram("lines", (8, 512), kind="Internal")
        d_sk = dram("dilskew", (8, 128, 512), kind="Internal")
        d_nk = dram("naskew", (8, 64, 465), kind="Internal")

        WR = [sb(f"wr{i}", [128, 1024]) for i in range(NRAW)]
        WH = [sb(f"wh{i}", [128, 1024], F32R) for i in range(NSPL)]
        WL = [sb(f"wl{i}", [128, 1024], F32R) for i in range(NSPL)]
        X = sb("X", [128, 8, 512])
        HH = sb("HH", [128, 8, 512], F32R)
        HL = sb("HL", [128, 8, 512], F32R)
        TM = Banks([sb(f"tm{i}", [128, 512]) for i in range(3)])
        RM = Banks([sb(f"rm{i}", [128, 512]) for i in range(1)])
        CT = sb("CT", [128, nconst])
        V = sb("V", [128, NVEC])
        LM = sb("LM", [128, 896], U8)
        MOD = sb("MOD", [128, 2, 48, 2])
        GS = sb("GS", [128, 2, 2, 8, 2])
        CS = sb("CS", [128, 8, 32])
        LB = sb("LB", [128, 5, 8])
        ST = sb("ST", [128, 3, 8])
        base = (nc.sbuf_base + 31) // 32 * 32
        sb("arena", [128, (ARENA + 64) // 4])

        def at_(name, kb, shape, dt=F32):
            n = 4
            for d in shape:
                n *= d
            assert kb * KB_ + n <= ARENA, name
            return nc.alloc_sbuf_tensor_at(name, [128] + shape, dt, offset=base + int(kb * KB_))

        psum = [ctx.enter_context(nc.psum_tensor(f"ps{i}", [128, 512], F32)) for i in range(8)]
        main = Banks(psum[0:4])
        aux = Banks(psum[4:8])

        sync, pe = Queue(sem("s_sync")), Queue(sem("s_pe"))
        act, dve, pool = Queue(sem("s_act")), Queue(sem("s_dve")), Queue(sem("s_pool"))
        pe.skip_own = True
        slot_sem = [sem(f"s_w{i}") for i in range(NRAW)]
        s_out = sem("s_out")

        const = {}
        at = 0
        for n, w in csizes.items():
            const[n] = CT[:, at:at + w]
            at += w
        ident, ones, blk = const["ident"], const["ones"], const["blk"]
        ones256 = bass.AP(ones.tensor, ones.offset, [list(ones.ap[0]), [0, 256]])

        def vec(name, j, n=1):
            return V[:, VEC[name][0] + j:VEC[name][0] + j + n]

        class Stream:
            def __init__(self):
                self.n, self.col, self.kind = -1, 1024, None
                self.next_dma = self.next_split = 0
                self.raw_done, self.spl_done, self.dma_tok, self.spl_tok = {}, {}, {}, {}

            def pump(self, upto):
                while self.next_dma <= upto and (self.next_dma < NRAW or self.next_dma - NRAW in self.raw_done):
                    n = self.next_dma
                    slot = n % NRAW
                    self.dma_tok[n] = sync.dma(lambda e, n=n, slot=slot: e.dma_start(WR[slot][:, :], d_w[n]),
                                               slot_sem[slot], 16 * (n // NRAW + 1), self.raw_done.get(n - NRAW))
                    self.next_dma += 1

            def split(self, upto):
                while self.next_split <= upto:
                    n = self.next_split
                    self.pump(n)
                    if n == self.n or (n < len(plan) and plan[n]):
                        src, i = WR[n % NRAW][:, :], n % NSPL
                        hi, lo = WH[i][:, :], WL[i][:, :]
                        free = self.spl_done.get(n - NSPL)
                        th = act(lambda e, hi=hi, src=src: e.activation(hi, src, ACT.Copy), self.dma_tok[n], free)
                        tl = dve(lambda e, hi=hi, lo=lo, src=src: e.tensor_tensor(
                            lo, src, hi.bitcast(F32), ALU.subtract), th)
                        self.spl_tok[n] = (th, tl)
                        self.raw_done[n] = [tl]
                    self.next_split += 1

            def get(self, name, k, cols, split=True):
                w = sum(b - a for a, b in cols)
                if self.col + w > 1024 or split != self.kind:
                    self.n, self.col, self.kind = self.n + 1, 0, split
                    kinds.append(split)
                    if plan:
                        assert plan[self.n] == split
                        self.split(min(self.n + AHEAD, len(plan) - 1))
                        self.pump(min(self.n + NRAW, len(plan) - 1))
                n, c = self.n, self.col
                order.append((n, c, name, k, tuple(cols)))
                self.col += w
                if not plan:
                    z = WH[0][:, c:c + w]
                    return (z, z, (None, None)) if split else (WR[0][:, c:c + w], None)
                if split:
                    i = n % NSPL
                    return WH[i][:, c:c + w], WL[i][:, c:c + w], self.spl_tok[n]
                return WR[n % NRAW][:, c:c + w], self.dma_tok[n]

            def used(self, tok):
                self.spl_done[self.n] = [tok]
                if not self.kind:
                    self.raw_done[self.n] = [tok]

        kinds = []
        W = Stream()

        def mm(out, lhsT, rhs, start, stop, *after, **kw):
            return pe(lambda e: e.matmul(out, lhsT, rhs, start=start, stop=stop, **kw), *after)

        def tr(out, in_, *after):
            return pe(lambda e: e.transpose(out, in_, ident), *after)

        def mm3(out, ah, al, bh, bl, start, stop, ta, tb, *after):
            mm(out, ah, bh, start, False, ta[0], tb[0], after)
            mm(out, ah, bl, False, False, tb[1])
            return mm(out, al, bh, False, stop, ta[1])

        def wmm(bank_ap, name, ks, cols, rhs, *after):
            t = None
            for i, k in enumerate(ks):
                wh, wl, wt = W.get(name, k, cols)
                xh, xl, xt = rhs(i)
                t = mm3(bank_ap, wh, wl, xh, xl, i == 0, i == len(ks) - 1, wt, xt, after if i == 0 else None)
                W.used(t)
            return t

        def a_act(out, in_, func, *after, **kw):
            return act(lambda e: e.activation(out, in_, func, **kw), *after)

        def tt(out, a, b, op, *after, q=None):
            return (q or dve)(lambda e: e.tensor_tensor(out, a, b, op), *after)

        def ts(out, a, s1, s2, op0, op1, *after):
            if op1 is None:
                return dve(lambda e: e.tensor_scalar(out, a, s1, None, op0), *after)
            return dve(lambda e: e.tensor_scalar(out, a, s1, s2, op0, op1), *after)

        def stt(out, a, s, b, op0, op1, *after):
            return dve(lambda e: e.scalar_tensor_tensor(out=out, in0=a, scalar=s, in1=b, op0=op0, op1=op1), *after)

        def vcopy(out, a, *after):
            return dve(lambda e: e.tensor_copy(out, a), *after)

        n_load = [0]
        outs = []

        def load(q, dst, src, *after):
            s = sem(f"s_ld{n_load[0]}")
            n_load[0] += 1
            return q.dma(lambda e: e.dma_start(dst, src), s, 16, *after)

        def dump(name, ap, *after):
            if plan and debug is not None and name in debug:
                shp = [p for p in ap.shape]
                d = nc.dram_tensor("dbg_" + name, shp, F32, kind="ExternalOutput").ap()
                outs.append(pool.dma(lambda e: e.dma_start(d, ap), sem("s_d" + name), 16, *after))
                for q in (pe, act, dve, pool):
                    q(None, outs[-1])

        xd = d_x.rearrange("p (k t) -> p k t", k=8)
        t_v = load(act, V[:, :], d_v)
        t_xk = [load(act, X[:, 2 * i:2 * i + 2, :], xd[:, 2 * i:2 * i + 2, :]) for i in range(4)]
        t_x = [t_xk[i // 2] for i in range(8)]
        t_c = load(act, CT[:, :], d_c)
        OHT = at_("OHT", 0, [512])
        T5T = at_("T5T", 2, [8])
        LNT = at_("LNT", 3, [512])
        LMF = at_("LMF", 5, [896])
        t_oh = load(pool, OHT[0:32, :], d_oh)
        t_t5 = load(pool, T5T[0:32, :], d_t5)
        t = load(pool, LMF[:, :], d_m)
        B1M = at_("B1M", 84, [1024])
        t_bm = load(pool, B1M[:, :], d_bm)
        NAB = at_("NAB", 44, [2, 8, 256])
        DILB = at_("DILB", 60, [2, 8, 256])
        t_lm = vcopy(LM[:, :], LMF[:, :], t)

        t_nk = pool.dma(lambda e: e.dma_start(d_nk, bass.AP(d_na.tensor, 0, [[465, 8], [0, 64], [1, 465]])),
                        sem("s_nk"), 16)
        b = aux.get()
        t = mm(b["ap"][0:8, :], T5T[0:32, :], OHT[0:32, :], True, True, t_oh, t_t5)
        t = vcopy(LNT[0:8, :], b["ap"][0:8, :], t)
        b["free"] = [t]
        t_ln = load(pool, d_line, LNT[0:8, :], t)
        t_sk = pool.dma(lambda e: e.dma_start(d_sk, bass.AP(d_line.tensor, 0, [[512, 8], [0, 128], [1, 512]])),
                        sem("s_sk"), 16, t_ln)
        hid_free = [t_ln, t_lm]
        s_nb = sem("s_nb")
        for a in range(2):
            for r in range(2):
                for kr in range(4):
                    row = 2 * a + r
                    src = bass.AP(d_nk.tensor, (kr - row + 7) * 31 + 15, [[464, 64], [64 * 465, 8], [1, 64]])
                    dst = NAB[64 * r:64 * r + 64, a, :, kr * 64:kr * 64 + 64]
                    t_nb = pool.dma(lambda e, src=src, dst=dst: e.dma_start(dst, src), s_nb, 16 * 16, t_nk)
        s_db = sem("s_db")
        for a in range(2):
            src = bass.AP(d_sk.tensor, 255 - 128 * a, [[511, 128], [65536, 8], [1, 256]])
            t_db = pool.dma(lambda e, src=src, a=a: e.dma_start(DILB[:, a], src), s_db, 32, t_sk)

        t = dve(lambda e: e.memset(CS[:, :, :], 0.0))
        cc = V[:, VEC["cc"][0]:VEC["cc"][0] + 16].rearrange("p (k c) -> p k c", c=2)
        t_cs = a_act(CS[:, :, 0:2], cc, ACT.Silu, t, t_v)

        def modulation(l):
            for r in range(3):
                b = aux.get()
                free = list(b["free"])
                for k in range(8):
                    for j in range(4):
                        ap, wt = W.get(("w_mod_2", l), k, [((4 * r + j) * 512, (4 * r + j + 1) * 512)], False)
                        t = mm(b["ap"][32 * j:32 * j + 32, :], CS[:, k, :], ap, k == 0, k == 7,
                               wt, t_cs, free if k == 0 else None)
                        W.used(t)
                tm = TM.get()
                t = vcopy(tm["ap"][:, :], b["ap"][:, :], t, tm["free"])
                b["free"] = [t]
                yield
                b = aux.get()
                for c in range(4):
                    t2 = tr(b["ap"][:, 128 * c:128 * c + 128], tm["ap"][:, 128 * c:128 * c + 128], t, b["free"], t_c)
                tm["free"] = [t2]
                src = b["ap"][:, :].rearrange("p (ch j z) -> p ch j z", ch=4, j=4)[:, :, :, 0:2]
                dst = MOD[:, l, 16 * r:16 * r + 16, :].rearrange("p (j ch) c -> p ch j c", ch=4)
                bm = bc(vec("b_mod_2", 48 * l + 16 * r, 16).rearrange("p (j ch) -> p ch j", ch=4), 3, 2)
                t = tt(dst, src, bm, ALU.add, t2)
                b["free"] = [t]
            for i, (nm, sc) in enumerate((("norm1_g_2", 8), ("norm2_g_2", 32))):
                g = bc(vec(nm, 8 * l, 8), 2, 2)
                t = stt(GS[:, l, i], MOD[:, l, sc:sc + 8, :], 1.0, g, ALU.add, ALU.mult, t)
            t_mod[l] = t
            yield

        t_mod = [None, None]

        lg = vec("hgrn_lb_logits_2", 0, 16)
        l0, l1 = lg[:, 0:8], lg[:, 8:16]
        t = tt(LB[:, 0, :], l0, l1, ALU.max, t_v)
        t1 = tt(LB[:, 1, :], l0, LB[:, 0, :], ALU.subtract, t)
        t2 = tt(LB[:, 2, :], l1, LB[:, 0, :], ALU.subtract, t)
        t = a_act(LB[:, 3:5, :], LB[:, 1:3, :], ACT.Exp, t1, t2)
        t = tt(LB[:, 0, :], LB[:, 3, :], LB[:, 4, :], ALU.add, t)
        t = a_act(LB[:, 1, :], LB[:, 0, :], ACT.Ln, t)
        t = tt(LB[:, 2, :], LB[:, 2, :], LB[:, 1, :], ALU.subtract, t)
        t1 = a_act(LB[:, 3, :], LB[:, 2, :], ACT.Exp, t)
        t2 = ts(LB[:, 0, :], LB[:, 2, :], LOG_FLOOR, None, ALU.max, None, t1)
        t_lb = ts(LB[:, 1, :], LB[:, 3, :], -1.0, 1.0, ALU.mult, ALU.add, t1)
        t_lb = [t_lb, t2, ts(LB[:, 4, :], LB[:, 0, :], -1.0, None, ALU.mult, None, t2)]

        def rstd(src, n, T, D, toks, ones_=None):
            b = aux.get()
            for i in range(n):
                tm = TM.get()
                t = a_act(tm["ap"][:, 0:T], src(i), ACT.Square, toks[i], tm["free"])
                t = mm(b["ap"][:, 0:T], ones_ if ones_ is not None else ones, tm["ap"][:, 0:T], i == 0, i == n - 1,
                       t, t_c, b["free"] if i == 0 else None)
                tm["free"] = [t]
            r = RM.get()
            t = a_act(r["ap"][:, 0:T], b["ap"][:, 0:T], ACT.Ln, t, r["free"], bias=vec("eps", 0), scale=1.0 / D)
            b["free"] = [t]
            t = a_act(r["ap"][:, 0:T], r["ap"][:, 0:T], ACT.Exp, t, scale=-0.5)
            return r, t

        def halves(hi, lo, src, *after):
            th = a_act(hi, src, ACT.Copy, after)
            return [th, tt(lo, src, hi.bitcast(F32), ALU.subtract, th)]

        h_free = []

        def norm_plain(g, toks):
            r, t = rstd(lambda i: X[:, i, 0:256], 8, 256, 1024, toks)
            out = []
            for i in range(8):
                tm = TM.get()
                v = tm["ap"][:, 0:256]
                t2 = stt(v, X[:, i, 0:256], vec(g, i), r["ap"][:, 0:256], ALU.mult, ALU.mult, t, tm["free"])
                out.append(halves(HH[:, i, 0:256], HL[:, i, 0:256], v, t2, h_free))
                tm["free"] = out[-1]
            r["free"] = [t2]
            return out

        def xrhs(toks, T=256):
            return lambda i: (HH[:, i, 0:T], HL[:, i, 0:T], toks[i])

        Y = at_("Y", 76, [8, 256])
        y_free = []

        def residual_norm(g, half, toks):
            r, t = rstd(lambda i: Y[:, i, :], 8, 256, 1024, [toks[i // 2] for i in range(8)])
            out = []
            for i in range(8):
                t2 = stt(Y[:, i, :], Y[:, i, :], vec(g, i), r["ap"][:, 0:256], ALU.mult, ALU.mult, t)
                out.append(stt(X[:, i, 0:256], Y[:, i, :], half, X[:, i, 0:256], ALU.mult, ALU.add, t2))
            r["free"] = [t2]
            y_free[:] = [out[-1]]
            return out

        def pair_out(name, ks, rhs, n_pairs, dst, *after):
            toks = []
            for j in range(n_pairs):
                b = main.get()
                for h in range(2):
                    c = (2 * j + h) * 128
                    t = wmm(b["ap"][:, 256 * h:256 * h + 256], name, ks, [(c, c + 128)], rhs, b["free"])
                out = dst(j)
                src = b["ap"][:, :].rearrange("p (h t) -> p h t", h=2)
                t = vcopy(out, src, t, after)
                b["free"] = [t]
                toks.append(t)
            return toks

        NH = at_("NHH", 0, [22, 256], F32R)
        NL = at_("NHL", 22, [22, 256], F32R)

        def ffn(n, toks):
            ht = []
            rhs = xrhs(toks)
            for f in range(22):
                b = main.get()
                c = [(f * 128, f * 128 + 128)]
                t = wmm(b["ap"][:, 0:256], (f"ffn{n}_w_gate", 0), range(8), c, rhs, b["free"])
                t = wmm(b["ap"][:, 256:512], (f"ffn{n}_w_up", 0), range(8), c, rhs)
                tm = TM.get()
                v = tm["ap"][:, 0:256]
                t1 = a_act(v, b["ap"][:, 0:256], ACT.Silu, t, tm["free"])
                t1 = tt(v, v, b["ap"][:, 256:512], ALU.mult, t1)
                b["free"] = [t1]
                ht.append(halves(NH[:, f, :], NL[:, f, :], v, t1, hid_free))
                tm["free"] = ht[-1]
            h_free[:] = [t]
            out = pair_out((f"ffn{n}_w_down", 0), range(22), lambda i: (NH[:, i, :], NL[:, i, :], ht[i]), 4,
                           lambda j: Y[:, 2 * j:2 * j + 2, :], y_free)
            hid_free[:] = [pe.last]
            return out

        toks = norm_plain("ffn1_pre_g", t_x)
        toks = ffn(1, toks)
        toks = residual_norm("ffn1_post_g", 0.5, toks)
        dump("x1", X[:, :, 0:256], toks)
        toks = norm_plain("mix_pre_g", toks)

        bt = []
        for m, B, tb in ((0, NAB, t_nb), (1, DILB, t_db)):
            for a in range(2):
                mk = B1M[:, 512 * m + 256 * a:512 * m + 256 * a + 256]
                bt.append(tt(B[:, a], B[:, a], bc(mk, 1, 8), ALU.add, tb, t_bm))

        QT = at_("QT", 0, [8, 256])
        KT = at_("KT", 8, [8, 256])
        VR = at_("VR", 16, [2, 1024])
        OT = at_("OT", 24, [8, 256])
        rhs = xrhs(toks)
        qk = pair_out(("w_qkv", 0), range(8), rhs, 8,
                      lambda j: (QT if j < 4 else KT)[:, 2 * (j % 4):2 * (j % 4) + 2, :], hid_free)

        def value_rows(name, c0, tiles, toks, dst, *after):
            bs = [main.get() for _ in range(tiles)]
            for k in range(8):
                wh, wl, wt = W.get(name, k, [(c0, c0 + 512)])
                for a in range(tiles):
                    sl = slice(128 * a, 128 * a + 128)
                    t = mm3(bs[a]["ap"][:, :], HH[:, k, sl], HL[:, k, sl], wh, wl, k == 0, k == 7, toks[k], wt,
                            bs[a]["free"] if k == 0 else None)
                W.used(t)
            out = []
            for a in range(tiles):
                t2 = vcopy(dst(a), bs[a]["ap"][:, :], t, after)
                bs[a]["free"] = [t2]
                out.append(t2)
            return out

        vt = []
        for h in range(2):
            vt += value_rows(("w_qkv", 0), 2048 + 512 * h, 2, toks, lambda a: VR[:, a, 512 * h:512 * h + 512], hid_free)
        h_free[:] = [pe.last]

        NB_ = 3
        st_free = [[] for _ in range(NB_)]
        unit_no = [0]

        class Unit:

            def __init__(self, score, rows, bias, sinkcol, pv, after_score, after_v, sbuf, pbuf):
                self.score, self.rows, self.bias, self.sinkcol = score, rows, bias, sinkcol
                self.pv, self.after_score, self.after_v = pv, after_score, after_v
                self.s, self.p = sbuf.get(), pbuf.get()
                self.i = unit_no[0] % NB_
                unit_no[0] += 1

            def first(self):
                i, rows = self.i, self.rows
                n = 512 // rows
                b = aux.get()
                t = self.score(b, self.after_score)
                s = self.s["ap"][:, :]
                sv = s.rearrange("p (r k) -> p r k", r=rows)
                if self.bias is None:
                    t = ts(s, b["ap"][:, :], 0.125, None, ALU.mult, None, t, self.s["free"])
                else:
                    bias, tb, w = self.bias
                    if w < 512:
                        a_act(s[:, w:512], b["ap"][:, w:512], ACT.Copy, t, self.s["free"], scale=0.125)
                        src, dst = b["ap"][:, 0:w], s[:, 0:w]
                        t = stt(dst, src, 0.125, bias, ALU.mult, ALU.add, act.last, tb)
                        t = [t, act.last]
                    else:
                        src = b["ap"][:, :].rearrange("p (r k) -> p r k", r=rows)
                        t = stt(sv, src, 0.125, bias, ALU.mult, ALU.add, t, tb, self.s["free"])
                b["free"] = [t]
                mx = ST[:, i, 0:rows]
                t = dve(lambda e: e.tensor_reduce(mx, sv, AX, ALU.max), t, st_free[i])
                nm = ST[:, i, 2:2 + rows]
                if self.sinkcol is not None:
                    t = ts(nm, mx, self.sinkcol, -1.0, ALU.max, ALU.mult, t, t_v)
                else:
                    t = ts(nm, mx, -1.0, None, ALU.mult, None, t)
                den = ST[:, i, 4:4 + rows]
                tn = t
                ta = []
                for r in range(rows):
                    ta.append(a_act(sv[:, r, :], sv[:, r, :], ACT.Exp, tn, bias=nm[:, r:r + 1],
                                    accum_out=den[:, r:r + 1]))
                if self.sinkcol is not None:
                    ta.append(a_act(ST[:, i, 6:6 + rows], nm, ACT.Exp, tn, bias=self.sinkcol))
                self.ta, self.den, self.sv, self.n = ta, den, sv, n

            def mid(self):
                i, den, ta = self.i, self.den, self.ta
                if self.sinkcol is not None:
                    ta = tt(den, den, ST[:, i, 6:6 + self.rows], ALU.add, ta)
                t = dve(lambda e: e.reciprocal(den, den), ta)
                self.t = tt(self.sv, self.sv, bc(den, 2, self.n), ALU.mult, t)
                st_free[i] = [self.t]

            def second(self):
                b = aux.get()
                for c in range(4):
                    sl = slice(128 * c, 128 * c + 128)
                    t = tr(b["ap"][:, sl], self.s["ap"][:, sl], self.t, b["free"])
                self.s["free"] = [t]
                t = a_act(self.p["ap"][:, :], b["ap"][:, :], ACT.Copy, t, self.p["free"])
                b["free"] = [t]
                self.t2 = t

            def third(self):
                self.p["free"] = [self.pv(self.p["ap"], self.t2, self.after_v)]

        def run_units(units, fill=lambda: None):
            n = len(units)
            made = []
            for j in range(n + 3):
                if j < n:
                    made.append(units[j]())
                    made[j].first()
                if 2 <= j <= n + 1:
                    made[j - 2].second()
                fill()
                if 1 <= j <= n:
                    made[j - 1].mid()
                if j >= 3:
                    made[j - 3].third()

        otoks = []
        S1 = Banks([at_(f"s1_{i}", 84 + 2 * i, [512]) for i in range(3)])
        P1B = Banks([at_(f"p1_{i}", 90 + 2 * i, [512]) for i in range(3)])
        for q in S1.banks:
            q["free"] = list(bt)
        held = {}

        def block1_unit(kind, h):
            head = 8 * kind + h
            j, off = head // 2, 64 * (head % 2)

            def score(b, after):
                for a in range(2):
                    t = mm(b["ap"][:, 256 * a:256 * a + 256], QT[off:off + 64, j, 128 * a:128 * a + 128],
                           KT[off:off + 64, j, :], True, True, after, b["free"])
                return t

            def pv(P, tp, after):
                if off == 0:
                    held["b"] = main.get()
                b = held["b"]
                for a in range(2):
                    for kt in range(2):
                        t = mm(b["ap"][off:off + 64, 128 * a:128 * a + 128],
                               VR[:, kt, 64 * head:64 * head + 64], P[:, 256 * a + 128 * kt:256 * a + 128 * kt + 128],
                               kt == 0, kt == 1, tp, after, b["free"])
                if off:
                    t2 = vcopy(OT[:, j, :], b["ap"][:, 0:256], t, hid_free)
                    b["free"] = [t2]
                    otoks.append(t2)
                return t
            return lambda: Unit(score, 2, ((NAB, DILB)[kind][:, :, h, :], bt, 512), None, pv, qk, vt, S1, P1B)

        mods = [modulation(0), modulation(1)]

        def fill_mod():
            for g in mods:
                if next(g, "end") != "end":
                    return

        run_units([block1_unit(kind, h) for kind in range(2) for h in range(8)], fill_mod)
        for _ in range(10):
            fill_mod()
        dump("o1", OT[:, :, :], otoks)
        ot2 = []
        for part, g in ((0, "na_out_g"), (1, "dil_out_g")):
            r, t = rstd(lambda i: OT[:, 4 * part + i, :], 4, 256, 512, otoks[4 * part:4 * part + 4])
            for i in range(4):
                n = 4 * part + i
                t2 = stt(OT[:, n, :], OT[:, n, :], vec(g, i), r["ap"][:, 0:256], ALU.mult, ALU.mult, t)
                ot2.append(halves(HH[:, n, 0:256], HL[:, n, 0:256], OT[:, n, :], t2, h_free))
            r["free"] = [t2]
        toks = pair_out(("w_out", 0), range(8), xrhs(ot2), 4, lambda j: Y[:, 2 * j:2 * j + 2, :], y_free)
        h_free[:] = [pe.last]
        hid_free[:] = [pe.last]
        toks = residual_norm("mix_post_g", 1.0, toks)
        dump("x2", X[:, :, 0:256], toks)
        toks = norm_plain("ffn2_pre_g", toks)
        toks = ffn(2, toks)
        xt = residual_norm("ffn2_post_g", 0.5, toks)
        dump("x3", X[:, :, 0:256], xt)
        ct = t_x

        GA = at_("GA", 0, [12, 512])
        GB = at_("GB", 40, [12, 512])
        G1 = at_("G1", 0, [24, 256])
        YA = at_("YA", 0, [12, 512], F32R)
        YB = at_("YB", 40, [12, 512], F32R)
        Y1 = at_("Y1", 0, [24, 256], F32R)
        Qh = at_("Qh", 24, [4, 512])
        KF = at_("KF", 32, [4, 512])
        KB = at_("KB", 40, [4, 512])
        EF = at_("EF", 48, [4, 2, 257])
        EB = at_("EB", 56.25, [4, 2, 257])
        VH = at_("VH", 64.5, [4, 512])
        AT = at_("AT", 72.5, [2, 4, 256])
        D = [at_(f"D{i}", 80.5 + 8 * i, [2, 4, 256]) for i in range(2)]
        ZB = at_("ZB", 0, [4, 512])
        PB = at_("PB", 8, [4, 512])
        LF = at_("LF", 16, [4, 512])
        A2 = at_("A2", 80.5, [2, 4, 512])
        OHH = at_("OHH", 64.5, [4, 512], F32R)
        OHL = at_("OHL", 72.5, [4, 512], F32R)
        GH = at_("GH", 32, [4, 512])
        FR = at_("FR", 80.5, [4, 512])
        Q2 = at_("Q2", 88.5, [4, 512])
        K2 = at_("K2", 24, [512])
        V2 = at_("V2", 26, [4, 128])
        S2 = [at_(f"s2_{i}", 28 + 2 * i, [512]) for i in range(3)]
        P2 = [at_(f"p2_{i}", 34 + 2 * i, [512]) for i in range(3)]
        HIDH = at_("HIDH", 0, [16, 512], F32R)
        HIDL = at_("HIDL", 32, [16, 512], F32R)
        HIDH1 = at_("HIDH1", 0, [32, 256], F32R)
        HIDL1 = at_("HIDL1", 32, [32, 256], F32R)

        c_ = {}
        at = 0
        for n, w in (("k", 128), ("v", 128), ("i", 512), ("ff", 512), ("fb", 512), ("q", 512), ("qh", 512),
                     ("gh", 512), ("four", 512), ("gate", 3072)):
            c_[n] = at
            at += w
        a_free = [pe.last, xt[-1]]

        def adaln(l, i, T, xt, ct):
            toks = [[xt[k]] + ([ct[k]] if T > 256 else []) for k in range(8)]
            r, t = rstd(lambda k: X[:, k, 0:T], 8, T, 1024, toks)
            out = []
            for k in range(8):
                tm = TM.get()
                out.append([[], []])
                for c in range(T // 256):
                    sl = slice(256 * c, 256 * c + 256)
                    v = tm["ap"][:, sl]
                    sh = MOD[:, l, 24 * i + k, c:c + 1]
                    t2 = stt(v, X[:, k, sl], GS[:, l, i, k, c:c + 1], r["ap"][:, sl], ALU.mult, ALU.mult,
                             t, tm["free"], t_mod[l])
                    th = a_act(HH[:, k, sl], v, ACT.Identity, t2, h_free, bias=sh)
                    tl = stt(HL[:, k, sl], v, sh, HH[:, k, sl].bitcast(F32), ALU.add, ALU.subtract, th)
                    out[-1][0].append(th)
                    out[-1][1].append(tl)
                tm["free"] = out[-1][1]
            r["free"] = [t2]
            return out

        for l in range(2):
            T = 512 if l == 0 else 256
            win = ("w_in_2", l)
            ht = adaln(l, 0, 512, xt, ct)
            rT, r512 = xrhs(ht, T), xrhs(ht, 512)

            def win_tile(cols, rhs, TT):
                b = main.get()
                return b, wmm(b["ap"][:, 0:TT], win, range(8), cols, rhs, b["free"])

            def forget(dr, seg, free):
                if l == 0:
                    loglb, neglb = [LOG_FLOOR] * 4, [vec("neglb", 0)] * 4
                else:
                    loglb = [LB[:, 0, 4 * dr + h:4 * dr + h + 1] for h in range(4)]
                    neglb = [LB[:, 4, 4 * dr + h:4 * dr + h + 1] for h in range(4)]
                tl, tz, tq = [], [], []
                for h in range(4):
                    c = c_[seg] + 128 * h
                    b, t = win_tile([(c, c + 128)], r512, 512)
                    z = a_act(ZB[:, h, :], b["ap"][:, :], ACT.Copy, t, free)
                    b["free"] = [z]
                    t1 = a_act(A2[:, 1, h, :], ZB[:, h, :], ACT.Abs, z, t_lb, free, bias=neglb[h])
                    t0 = stt(A2[:, 0, h, :], ZB[:, h, :], -1.0, ZB[:, h, :], ALU.mult, ALU.max, z, free)
                    t = a_act(A2[:, :, h, :], A2[:, :, h, :], ACT.Exp, t1, t0, scale=-1.0)
                    t = a_act(A2[:, :, h, :], A2[:, :, h, :], ACT.Ln, t, bias=1.0)
                    tp = ts(PB[:, h, :], ZB[:, h, :], 0.0, None, ALU.max, None, z, free)
                    tz = stt(ZB[:, h, :], ZB[:, h, :], loglb[h], PB[:, h, :], ALU.max, ALU.subtract, tp, t1)
                    td = tt(LF[:, h, :], A2[:, 1, h, :], A2[:, 0, h, :], ALU.subtract, t, free)
                    tf = tt(LF[:, h, :], LF[:, h, :], ZB[:, h, :], ALU.add, td, tz)
                    tp = tt(PB[:, h, :], PB[:, h, :], A2[:, 0, h, :], ALU.add, t, tz)
                    tl.append(tf)
                    tq.append(tp)
                K, E = (KF, KB)[dr], (EF, EB)[dr]
                out = []
                tm = dve(lambda e: e.memset(E[:, :, :, 0:1], 0.0), a_free)
                for h in range(4):
                    t = a_act(K[:, h, :], PB[:, h, :], ACT.Exp, tq[h], a_free, scale=-1.0)
                    if l:
                        t = ts(K[:, h, :], K[:, h, :], LB[:, 1, 4 * dr + h:4 * dr + h + 1], None, ALU.mult, None, t)
                    out.append(t)
                    for s in range(2):
                        t = dve(lambda e, h=h, s=s: e.tensor_tensor_scan(
                            E[:, h, s, 1:257], ones256, LF[:, h, 256 * s:256 * s + 256], 0.0, ALU.mult, ALU.add),
                            tl[h], t_c, a_free)
                return out + [t, tm]

            f_tok = forget(0, "ff", a_free)
            hq = []
            for h in range(4):
                c = c_["qh"] + 128 * h
                b, t = win_tile([(c, c + 128)], rT, T)
                t = a_act(Qh[:, h, 0:T], b["ap"][:, 0:T], ACT.Silu, t, a_free)
                b["free"] = [t]
                hq.append(t)
            f_tok = f_tok + forget(1, "fb", f_tok)
            d_free = [list(f_tok), list(f_tok)]
            dump(f"kf{l}", KF[:, :, :], f_tok)
            hv = value_rows(win, c_["i"], 4, ht, lambda a: VH[:, a, :], a_free)

            g_tok = {}

            def g_ap(n):
                if l:
                    return G1[:, n, :]
                return GA[:, n, :] if n < 12 else GB[:, n - 12, :]

            def gate(n, *after):
                d, br = n // 3, n % 3
                c = c_["gate"] + 1024 * br + 128 * d
                b, t = win_tile([(c, c + 128)], rT, T)
                t = a_act(g_ap(n), b["ap"][:, 0:T], ACT.Copy, t, after)
                b["free"] = [t]
                g_tok[n] = t

            n_gate = [0]

            def fill(last=12 if l == 0 else 24):
                if n_gate[0] < last:
                    gate(n_gate[0], f_tok)
                    n_gate[0] += 1

            at_free = list(a_free)
            ST0 = [KB[:, :, 256 + 128 * z:384 + 128 * z] for z in range(2)]

            def states():
                rows = []
                for dr in range(2):
                    E, K, Dk = (EF, EB)[dr], (KF, KB)[dr], D[0][:, dr]
                    if dr == 0:
                        te = [a_act(Dk[:, h, :], E[:, h, 1, 1:257], ACT.Exp, f_tok, d_free[0], scale=-1.0,
                                    bias=E[:, h, 1, 256:257]) for h in range(4)]
                    else:
                        te = a_act(Dk, E[:, :, 1, 0:256], ACT.Exp, f_tok, d_free[0])
                    t = tt(Dk, Dk, K[:, :, 256:512], ALU.mult, te)
                    fill()
                    KR = D[1][:, dr].rearrange("p h t -> p (h t)")
                    for a in range(2):
                        b = aux.get()
                        for h in range(4):
                            t2 = tr(b["ap"][:, 128 * h:128 * h + 128], Dk[:, h, 128 * a:128 * a + 128], t, b["free"])
                        t2 = vcopy(KR[:, 512 * a:512 * a + 512], b["ap"][:, :], t2, d_free[1])
                        b["free"] = [t2]
                        rows.append(t2)
                done = []
                for dr in range(2):
                    b = aux.get()
                    KR = D[1][:, dr].rearrange("p h t -> p (h t)").rearrange("p (a h k) -> p a h k", a=2, h=4)
                    for h in range(4):
                        for a in range(2):
                            t = mm(b["ap"][:, 128 * h:128 * h + 128], KR[:, a, h, :],
                                   VH[:, 2 + a, 128 * h:128 * h + 128], a == 0, a == 1, rows, hv, b["free"])
                    t = vcopy(ST0[dr], b["ap"][:, :].rearrange("p (h k) -> p h k", h=4), t)
                    b["free"] = [t]
                    done.append(t)
                d_free[:] = [[t], [t]]
                return done

            def recurrence(s):
                c0 = 256 * s
                q = Qh[:, :, c0:c0 + 256]
                kf, kb = KF[:, :, c0:c0 + 256], KB[:, :, c0:c0 + 256]
                last = []
                Ein = (EF[:, :, s, 1:257], EB[:, :, s, 1:257])
                Eex = (EF[:, :, s, 0:256], EB[:, :, s, 0:256])

                def prepare(lv):
                    Dd = D[(lv + 1) % 2]
                    df = d_free[(lv + 1) % 2]
                    if lv < 0:
                        return [tt(Dd[:, 1], kf, kb, ALU.add, f_tok, df)]
                    hh = 1 << lv

                    def v(ap, u):
                        return ap.rearrange("p h (b u j) -> p h b u j", u=2, j=hh)[:, :, :, u, :]

                    def mid(E):
                        return bc(E.rearrange("p h (b u j) -> p h b u j", u=2, j=hh)[:, :, :, 1, 0], 3, hh)
                    te = [tt(v(Dd[:, 0], 1), v(Ein[0], 1), mid(Eex[0]), ALU.subtract, f_tok, df),
                          tt(v(Dd[:, 0], 0), mid(Eex[1]), v(Eex[1], 0), ALU.subtract, f_tok, df),
                          tt(v(Dd[:, 1], 0), mid(Eex[0]), v(Ein[0], 0), ALU.subtract, f_tok, df),
                          tt(v(Dd[:, 1], 1), v(Eex[1], 1), mid(Eex[1]), ALU.subtract, f_tok, df)]
                    return a_act(Dd[:, 0], Dd[:, 0], ACT.Exp, te[0:2]), a_act(Dd[:, 1], Dd[:, 1], ACT.Exp, te[2:4])

                def weigh(lv, te):
                    if lv < 0:
                        return te
                    Dd = D[(lv + 1) % 2]
                    hh = 1 << lv

                    def v(ap, u):
                        return ap.rearrange("p h (b u j) -> p h b u j", u=2, j=hh)[:, :, :, u, :]
                    return [tt(Dd[:, 0], Dd[:, 0], q, ALU.mult, te[0], hq),
                            tt(v(Dd[:, 1], 0), v(Dd[:, 1], 0), v(kf, 0), ALU.mult, te[1]),
                            tt(v(Dd[:, 1], 1), v(Dd[:, 1], 1), v(kb, 1), ALU.mult, te[1])]

                def products(lv, tq):
                    Dd = D[(lv + 1) % 2]
                    qs = q if lv < 0 else Dd[:, 0]
                    for a in range(2):
                        b = aux.get()
                        qa = a if lv < 7 else 1 - a
                        for h in range(4):
                            t2 = mm(b["ap"][:, 128 * h:128 * h + 128], Dd[:, 1, h, 128 * a:128 * a + 128],
                                    qs[:, h, 128 * qa:128 * qa + 128], True, True, tq, hq, b["free"])
                        src = b["ap"][:, :].rearrange("p (h t) -> p h t", h=4)
                        dst = AT[:, a, :, 128 * qa:128 * qa + 128]
                        if 0 <= lv < 7:
                            mk = bc(LM[:, 128 * lv:128 * lv + 128], 1, 4)
                            t3 = dve(lambda e, dst=dst, mk=mk, src=src: e.copy_predicated(dst, mk, src),
                                     t2, t_lm, last)
                        else:
                            t3 = vcopy(dst, src, t2, at_free)
                        b["free"] = [t3]
                        last.append(t3)
                    d_free[(lv + 1) % 2] = [t2]

                te = prepare(-1)
                for lv in range(-1, 8):
                    nxt = prepare(lv + 1) if lv < 7 else None
                    tq = weigh(lv, te)
                    fill()
                    products(lv, tq)
                    te = nxt
                inter = []
                Dd = D[0]
                if s == 0:
                    t1 = a_act(Dd[:, 0], EF[:, :, 0, 1:257], ACT.Exp, f_tok, d_free[0])
                    for h in range(4):
                        t2 = a_act(Dd[:, 1, h, :], EB[:, h, 0, 0:256], ACT.Exp, f_tok, d_free[0], scale=-1.0,
                                   bias=EB[:, h, 0, 256:257])
                    inter = [tt(Dd[:, 0], Dd[:, 0], q, ALU.mult, t1, hq), tt(Dd[:, 1], Dd[:, 1], q, ALU.mult, t2, hq)]
                    fill()
                otok = []
                for hp in range(2):
                    b = aux.get()
                    for h in (2 * hp, 2 * hp + 1):
                        o = b["ap"][:, 256 * (h % 2):256 * (h % 2) + 256]
                        n = 4 if s == 0 else 2
                        for a in range(2):
                            t = mm(o, VH[:, 2 * s + a, 128 * h:128 * h + 128], AT[:, a, h, :], a == 0, a == n - 1,
                                   last, hv, b["free"])
                        if s == 0:
                            for z in range(2):
                                t = mm(o, ST0[z][:, h, :], Dd[:, z, h, :], False, z == 1, inter, b_s)
                    t2 = vcopy(Qh[:, 2 * hp:2 * hp + 2, c0:c0 + 256], b["ap"][:, :].rearrange("p (h t) -> p h t", h=2), t)
                    b["free"] = [t2]
                    otok.append(t2)
                at_free[:] = [t]
                d_free[0] = [d_free[0], t]
                return otok, t

            o_tok = []
            if l == 0:
                o_tok += recurrence(1)[0]
            b_s = states()
            ot, lastmm = recurrence(0)
            o_tok += ot
            hg_done = [lastmm] + o_tok
            dump(f"oh{l}", Qh[:, :, 0:T], o_tok)
            while n_gate[0] < (12 if l == 0 else 24):
                fill()

            gt = []
            for h in range(4):
                c = c_["gh"] + 128 * h
                b, t = win_tile([(c, c + 128)], rT, T)
                t = a_act(GH[:, h, 0:T], b["ap"][:, 0:T], ACT.Silu, t, hg_done)
                b["free"] = [t]
                gt.append(t)
            ft = []
            for g in range(4):
                c = c_["four"] + 128 * g
                b, t = win_tile([(c, c + 128)], rT, T)
                t = vcopy(FR[:, g, 0:T], b["ap"][:, 0:T], t, hg_done)
                b["free"] = [t]
                ft.append(t)
            oht = []
            for h in range(4):
                o = Qh[:, h, 0:T]
                r, t = rstd(lambda i: o, 1, T, 128, [o_tok])
                t = stt(o, o, vec("hgrn_norm_g_2", l), r["ap"][:, 0:T], ALU.mult, ALU.mult, t)
                r["free"] = [t]
                t = tt(o, o, GH[:, h, 0:T], ALU.mult, t, gt[h])
                oht.append(halves(OHH[:, h, 0:T], OHL[:, h, 0:T], o, t, hg_done))
            oh_done = [oht[-1]]
            if l == 0:
                for n in range(12, 24):
                    gate(n, hg_done)

            def head_norm(dst, cols, TT, gname, *after):
                b, t = win_tile(cols, xrhs(ht, TT), TT)
                t = vcopy(dst[:, 0:TT], b["ap"][:, 0:TT], t, after)
                b["free"] = [t]
                r, t = rstd(lambda i: dst[:, 0:TT], 1, TT, 64, [t], ones_=blk)
                t = stt(dst[:, 0:TT], dst[:, 0:TT], vec(gname, l), r["ap"][:, 0:TT], ALU.mult, ALU.mult, t)
                r["free"] = [t]
                b = aux.get()
                tm = TM.get()
                t2 = mm(b["ap"][:, 0:256], const["perm"], dst[:, 0:256], True, True, t, b["free"])
                t2 = tt(tm["ap"][:, 0:256], b["ap"][:, 0:256], const["ropes"], ALU.mult, t2, tm["free"])
                b["free"] = [t2]
                t = tt(dst[:, 0:256], dst[:, 0:256], const["ropec"], ALU.mult, t, t2)
                t = tt(dst[:, 0:256], dst[:, 0:256], tm["ap"][:, 0:256], ALU.add, t, t2)
                tm["free"] = [t]
                return t

            b, t = win_tile([(c_["v"], c_["v"] + 128)], r512, 512)
            tm = TM.get()
            t = vcopy(tm["ap"][:, :], b["ap"][:, :], t, tm["free"])
            b["free"] = [t]
            vtr = (tm, t)
            kt_ = head_norm(K2, [(c_["k"], c_["k"] + 128)], 512, "k_norm_g_2", oh_done)
            b = aux.get()
            for c in range(4):
                t = tr(b["ap"][:, 128 * c:128 * c + 128], tm["ap"][:, 128 * c:128 * c + 128], vtr[1], b["free"])
            tm["free"] = [t]
            v2t = vcopy(V2[:, :, :], b["ap"][:, :].rearrange("p (a n) -> p a n", a=4), t, oh_done)
            b["free"] = [v2t]
            qt_ = []
            for j in range(4):
                c = c_["q"]
                qt_.append(head_norm(Q2[:, j, :], [(c + 64 * j, c + 64 * j + 64), (c + 64 * j + 256, c + 64 * j + 320)],
                                     T, "q_norm_g_2", hg_done))
            h_free[:] = [pe.last]

            zb = Banks(P2)
            sbk = Banks(S2)
            for q in zb.banks + sbk.banks:
                q["free"] = list(oh_done)
            cdsd, ctm, nst = const["cdsd"], const["ct"], const["nst"]
            oft = []

            def fourier(g):
                bo = main.get()
                zz = []
                for s in range(T // 256):
                    b = aux.get()
                    for a in range(2):
                        t = mm(b["ap"][:, 256 * a:256 * a + 256],
                               FR[:, g, 256 * s + 128 * a:256 * s + 128 * a + 128], cdsd, True, True, ft[g], b["free"])
                    z = zb.get()
                    t = vcopy(z["ap"][:, :], b["ap"][:, :], t, z["free"])
                    b["free"] = [t]
                    zz.append((z, t))
                for s, (z, t) in enumerate(zz):
                    Zb = z["ap"]
                    o = bo["ap"][:, 256 * s:256 * s + 256]
                    for a in range(2):
                        mm(o, Zb[:, 256 * a:256 * a + 128], ctm[:, 256 * a:256 * a + 256], a == 0, False, t,
                           bo["free"])
                        t2 = mm(o, Zb[:, 256 * a + 128:256 * a + 256], nst[:, 256 * a:256 * a + 256], False, a == 1)
                    z["free"] = [t2]
                tm = TM.get()
                v = tm["ap"][:, 0:T]
                t = a_act(v, bo["ap"][:, 0:T], ACT.Copy, t2, tm["free"])
                bo["free"] = [t]
                oft.append(halves(HH[:, g, 0:T], HL[:, g, 0:T], v, t, h_free))
                tm["free"] = oft[-1]

            for g in range(4):
                fourier(g)

            a_tok = []
            qkt = [kt_] + qt_

            def keep_out(j, c0, b, t):
                tm = TM.get()
                v = tm["ap"][:, 0:256]
                t = vcopy(v, b["ap"][:, 0:256], t, tm["free"])
                b["free"] = [t]
                a_tok.append((j, halves(HH[:, 4 + j, c0:c0 + 256], HL[:, 4 + j, c0:c0 + 256], v, t, h_free)))
                tm["free"] = a_tok[-1][1]

            def x_unit(j, kv, a):
                off = 64 * kv

                def score(b, after):
                    return mm(b["ap"][:, :], Q2[off:off + 64, j, 128 * a:128 * a + 128], K2[off:off + 64, :],
                              True, True, after, b["free"])

                def pv(P, tp, after):
                    if a == 0 and kv == 0:
                        held["b"] = main.get()
                    b = held["b"]
                    for c in range(4):
                        t = mm(b["ap"][off:off + 64, 128 * a:128 * a + 128], V2[:, c, off:off + 64],
                               P[:, 128 * c:128 * c + 128], c == 0, c == 3, tp, after, b["free"])
                    if a == 1 and kv == 1:
                        keep_out(j, 0, b, t)
                    return t
                return lambda: Unit(score, 1, (const["win"][:, 256 * a:256 * a + 256], None, 256),
                                    vec("attn_sink_2", 8 * l + j + 4 * kv), pv, qkt, v2t, sbk, zb)

            def c_unit(j, kv):
                off = 64 * kv

                def score(b, after):
                    for a in range(2):
                        t = mm(b["ap"][:, 256 * a:256 * a + 256], Q2[off:off + 64, j, 256 + 128 * a:384 + 128 * a],
                               K2[off:off + 64, 256:512], True, True, after, b["free"])
                    return t

                def pv(P, tp, after):
                    if kv == 0:
                        held["b"] = main.get()
                    b = held["b"]
                    for a in range(2):
                        for c in range(2):
                            t = mm(b["ap"][off:off + 64, 128 * a:128 * a + 128], V2[:, 2 + c, off:off + 64],
                                   P[:, 256 * a + 128 * c:256 * a + 128 * c + 128], c == 0, c == 1, tp, after,
                                   b["free"])
                    if kv == 1:
                        keep_out(j, 256, b, t)
                    return t
                return lambda: Unit(score, 2, None, vec("attn_sink_2", 8 * l + j + 4 * kv), pv, qkt, v2t, sbk, zb)

            units = [x_unit(j, kv, a) for j in range(4) for kv in range(2) for a in range(2)]
            if l == 0:
                units += [c_unit(j, kv) for j in range(4) for kv in range(2)]
            run_units(units)
            at_j = [[t for jj, tk in a_tok if jj == j for t in tk] for j in range(4)]

            sg = {n: a_act(g_ap(n), g_ap(n), ACT.Sigmoid, g_tok[n]) for n in range(24)}
            if l == 0:
                def y_ap(d, z):
                    return (YA, YB)[d // 4][:, 3 * (d % 4) + z, :]
            else:
                def y_ap(d, z):
                    return Y1[:, 3 * d + z, :]
            br_rhs = [lambda i: (HH[:, i, 0:T], HL[:, i, 0:T], oft[i]),
                      lambda i: (HH[:, 4 + i, 0:T], HL[:, 4 + i, 0:T], [at_j[i], None]),
                      lambda i: (OHH[:, i, 0:T], OHL[:, i, 0:T], oht[i])]
            yt = []
            for d in range(8):
                tm = TM.get()
                acc = tm["ap"][:, 0:T]
                for br in range(3):
                    b = main.get()
                    key = ("w_branch_2", l, br, "split" if br == 1 else None)
                    t = wmm(b["ap"][:, 0:T], key, range(4), [(128 * d, 128 * d + 128)], br_rhs[br], b["free"])
                    gg = g_ap(3 * d + br)
                    if br == 0:
                        prev = tt(acc, b["ap"][:, 0:T], gg, ALU.mult, t, sg[3 * d], tm["free"])
                        b["free"] = [prev]
                    else:
                        t = tt(gg, b["ap"][:, 0:T], gg, ALU.mult, t, sg[3 * d + br])
                        b["free"] = [t]
                        prev = tt(acc, acc, gg, ALU.add, t, prev)
                yt.append(halves(y_ap(d, 0), y_ap(d, 1), acc, prev))
                tm["free"] = yt[-1]
            h_free[:] = [pe.last]

            def add_out(name, ks, rhs, mod_i, xt0, ct0):
                xt, ct = [], []
                for d in range(8):
                    b = main.get()
                    t = wmm(b["ap"][:, 0:T], name, ks, [(128 * d, 128 * d + 128)], rhs, b["free"])
                    for c in range(T // 256):
                        sl = slice(256 * c, 256 * c + 256)
                        t2 = stt(X[:, d, sl], b["ap"][:, sl], MOD[:, l, mod_i + d, c:c + 1], X[:, d, sl],
                                 ALU.mult, ALU.add, t, (ct0 if c else xt0)[d])
                        (ct if c else xt).append(t2)
                    b["free"] = [t2]
                return xt, ct

            xt, ct = add_out(("w_out_2", l), range(8), lambda i: (y_ap(i, 0), y_ap(i, 1), yt[i]), 16, xt, ct)
            y_done = [pe.last]
            dump(f"xa{l}", X[:, :, 0:T], xt, ct)
            h2 = adaln(l, 1, T, xt, ct)
            r2 = xrhs(h2, T)
            hfree = y_done
            for part in range(2 if l == 0 else 1):
                nf = 16 if l == 0 else 32
                hh, hl = (HIDH, HIDL) if l == 0 else (HIDH1, HIDL1)
                mt = []
                for i in range(nf):
                    f = nf * part + i
                    b = main.get()
                    t = wmm(b["ap"][:, 0:T], ("w_ff1_2", l), range(8), [(128 * f, 128 * f + 128)], r2, b["free"])
                    tm = TM.get()
                    v = tm["ap"][:, 0:T]
                    t = a_act(v, b["ap"][:, 0:T], ACT.Relu, t, tm["free"])
                    t = tt(v, v, b["ap"][:, 0:T], ALU.mult, t)
                    b["free"] = [t]
                    mt.append(halves(hh[:, i, :], hl[:, i, :], v, t, hfree))
                    tm["free"] = mt[-1]
                if part == (1 if l == 0 else 0):
                    h_free[:] = [pe.last]
                xt, ct = add_out(("w_ff2_2", l), range(nf * part, nf * part + nf),
                                 lambda i: (hh[:, i, :], hl[:, i, :], mt[i]), 40, xt, ct)
                hfree = [pe.last]
            a_free = [pe.last]
            dump(f"xb{l}", X[:, :, 0:T], xt, ct)

        t_o = sync.dma(lambda e: e.dma_start(d_out.rearrange("p (k t) -> p k t", k=8), X[:, :, 0:256]),
                       s_out, 16, xt)
        sync(None, t_o, t_ln, t_sk, t_nk, outs)

        if not plan:
            return kinds, order
        d_w = dram("wstream", (len(kinds), 128, 1024))
        for q in (sync, pe, act, dve, pool):
            q.number()
        with nc.Block() as block:
            block.sync(sync.emit)
            block.tensor(pe.emit)
            block.scalar(act.emit)
            block.vector(dve.emit)
            block.gpsimd(pool.emit)
        return kinds, order


def weight(inputs, name):
    if name[0] == "w_branch_2":
        w = inputs["w_branch_2"][name[1], name[2]]
        if name[3]:
            w = w.reshape(2, 4, 64, -1).transpose(1, 0, 2, 3).reshape(512, -1)
        return w
    return inputs[name[0]][name[1]]


def pack_stream(inputs, order, blocks):
    out = np.zeros((blocks, 128, 1024), np.float32)
    for n, col, name, k, cols in order:
        w = weight(inputs, name)
        for a, b in cols:
            out[n, :, col:col + b - a] = w[128 * k:128 * k + 128, a:b]
            col += b - a
    return out


def columns(v):
    return np.ascontiguousarray(np.asarray(v).reshape(-1, 128).T)


def pack_vecs(inputs):
    v = np.zeros((128, NVEC), np.float32)

    def put(name, a):
        at, n = VEC[name]
        assert a.shape == (128, n), (name, a.shape)
        v[:, at:at + n] = a
    for name in ("ffn1_pre_g", "ffn1_post_g", "mix_pre_g", "na_out_g", "dil_out_g", "mix_post_g", "ffn2_pre_g",
                 "ffn2_post_g", "b_mod_2", "norm1_g_2", "norm2_g_2", "hgrn_lb_logits_2", "hgrn_norm_g_2"):
        put(name, columns(inputs[name]))
    put("cc", np.stack([columns(inputs["c_2"]), columns(inputs["c_ctx_2"])], 2).reshape(128, 16))
    for name in ("q_norm_g_2", "k_norm_g_2"):
        put(name, np.concatenate([inputs[name].T, inputs[name].T], 0))
    put("attn_sink_2", np.broadcast_to(inputs["attn_sink_2"].reshape(1, 16), (128, 16)))
    put("neglb", np.full((128, 1), -LOG_FLOOR, np.float32))
    put("eps", np.full((128, 1), EPS, np.float32))
    return v


def kernel(debug=None, **inputs):
    import concourse.bacc as bacc
    from concourse.bass_utils import run_bass_kernel_spmd

    inputs = {k: np.asarray(v) for k, v in inputs.items()}
    consts = const_arrays()
    sizes = {n: consts[n].shape[1] for n in CONSTS}
    plan, _ = build_program(bacc.Bacc("TRN2", target_bir_lowering=False, num_devices=1), sizes, None)
    nc = bacc.Bacc("TRN2", target_bir_lowering=False, num_devices=1)
    kinds, order = build_program(nc, sizes, plan, debug)
    blocks = len(kinds)
    xc = np.concatenate([inputs["x"][0], inputs["ctx_2"][0]], 0).T
    arrays = {
        "xin": np.ascontiguousarray(xc.reshape(8, 128, 512).transpose(1, 0, 2)).reshape(128, 4096),
        "wstream": pack_stream(inputs, order, blocks),
        "consts": np.ascontiguousarray(np.concatenate([consts[n] for n in CONSTS], 1)),
        "b1mask": consts["b1mask"],
        "vecs": pack_vecs(inputs),
        "lmask": level_masks(),
        "onehot": bucket_onehot(),
        "t5t": np.ascontiguousarray(inputs["t5_rel_bias"].T),
        "narel": np.ascontiguousarray(inputs["na_rel_bias"].reshape(8, 465)),
    }
    r = run_bass_kernel_spmd(nc, [arrays], core_ids=[0])
    y = r.results[0]["yout"]
    return np.ascontiguousarray(y.reshape(128, 8, 256).transpose(2, 1, 0)).reshape(1, 256, 1024)
```

```python
from contextlib import ExitStack

import numpy as np

import concourse.bass as bass
from concourse import mybir

ALU = mybir.AluOpType
ACT = mybir.ActivationFunctionType
F32 = mybir.dt.float32
F32R = mybir.dt.float32r
U8 = mybir.dt.uint8
AX = mybir.AxisListType.X

NEG = -1e30
EPS = 1e-6
LOG_FLOOR = float(np.log(np.float32(1e-30)))
NRAW, NSPL, AHEAD = 4, 3, 2
KB_ = 1024
ARENA = 96 * KB_ + 512


def const_arrays():
    i = np.arange(128)
    t = np.arange(256)
    c = {}
    c["ident"] = np.eye(128)
    c["ones"] = np.ones((128, 128))
    c["blk"] = (i[:, None] // 64 == i[None, :] // 64).astype(float)
    perm = np.zeros((128, 128))
    for d in range(128):
        if d % 32 < 16:
            perm[d + 16, d] = -1.0
        else:
            perm[d - 16, d] = 1.0
    c["perm"] = perm
    freq = (np.float32(10000.0) ** (-np.arange(0, 32, 2, dtype=np.float32) / np.float32(32))).astype(np.float32)
    pos = np.where((i[:, None] % 64) < 32, (t // 64)[None, :], (t % 64)[None, :]).astype(np.float32)
    ang = (pos * freq[i % 16][:, None]).astype(np.float32).astype(np.float64)
    c["ropec"], c["ropes"] = np.cos(ang), np.sin(ang)
    w = 2 * np.pi * np.outer(i, i) / 128
    c["cdsd"] = np.concatenate([np.cos(w), np.sin(w)], 1) / np.sqrt(128.0)
    w = 2 * np.pi * (np.outer(t, t) % 256) / 256
    c["ct"] = np.concatenate([np.cos(w)[:128], np.cos(w)[128:]], 1) / 16.0
    c["nst"] = -np.concatenate([np.sin(w)[:128], np.sin(w)[128:]], 1) / 16.0
    k = np.arange(256)
    win = []
    for a in range(2):
        q = a * 128 + i
        win.append(np.where(np.abs(k[None] - q[:, None]) <= 128, 0.0, NEG))
    c["win"] = np.concatenate(win, 1)
    na, dil = [], []
    for a in range(2):
        q = a * 128 + i
        s = np.clip(q % 64 - 8, 0, 48)
        kc = k % 64
        na.append(np.where((kc[None] >= s[:, None]) & (kc[None] < s[:, None] + 16), 0.0, NEG))
        d = k[None] - q[:, None]
        n = (np.abs(d) <= 64).astype(int) + (d % 4 == 0) + (d % 16 == 0)
        dil.append(np.where(n > 0, np.log(np.maximum(n, 1)), NEG))
    c["b1mask"] = np.concatenate(na + dil, 1)
    return {n: np.ascontiguousarray(v, dtype=np.float32) for n, v in c.items()}


def bucket_onehot():
    rel = np.arange(-255, 257)
    n = np.abs(rel)
    large = 8 + (np.log(np.maximum(n, 1).astype(np.float32) / np.float32(8))
                 / np.float32(np.log(1024 / 8)) * np.float32(8)).astype(np.int32)
    b = np.where(rel > 0, 16, 0) + np.where(n < 8, n, np.minimum(large, 15))
    return (np.arange(32)[:, None] == b[None, :]).astype(np.float32)


def level_masks():
    i = np.arange(128)
    m = []
    for lv in range(7):
        h = 1 << lv
        same = i[:, None] // (2 * h) == i[None, :] // (2 * h)
        m.append(same & ((i[:, None] // h) % 2 != (i[None, :] // h) % 2))
    return np.concatenate(m, 1).astype(np.float32)


NFIRST = 512
CONSTS = ["ident", "ones", "blk", "perm", "ropec", "ropes", "cdsd", "ct", "nst", "win"]
VEC = {}


def vec_columns():
    at = 0
    for name, n in [("ffn1_pre_g", 8), ("ffn1_post_g", 8), ("mix_pre_g", 8), ("na_out_g", 4), ("dil_out_g", 4),
                    ("mix_post_g", 8), ("ffn2_pre_g", 8), ("ffn2_post_g", 8), ("cc", 16), ("b_mod_2", 96),
                    ("norm1_g_2", 16), ("norm2_g_2", 16), ("q_norm_g_2", 2), ("k_norm_g_2", 2),
                    ("hgrn_lb_logits_2", 16), ("hgrn_norm_g_2", 2), ("attn_sink_2", 16), ("eps", 1), ("neglb", 1)]:
        VEC[name] = (at, n)
        at += n
    return at


NVEC = vec_columns()


class Tok:
    def __init__(self, sem=None, val=None):
        self.sem, self.val, self.used = sem, val, False


class Queue:

    def __init__(self, sem):
        self.sem, self.ops = sem, []

    def __call__(self, fn, *after):
        tok = Tok()
        if fn is not None:
            self.last = tok
        self.ops.append((fn, self.flat(after), tok, None))
        return tok

    def dma(self, fn, sem, val, *after):
        self.ops.append((fn, self.flat(after), None, sem))
        return Tok(sem, val)

    @staticmethod
    def flat(x):
        out = []
        for t in x:
            if isinstance(t, (list, tuple)):
                out += Queue.flat(t)
            elif t is not None:
                t.used = True
                out.append(t)
        return out

    def number(self):
        n = 0
        for _, _, tok, _ in self.ops:
            if tok is not None and tok.used:
                n += 1
                tok.sem, tok.val = self.sem, n

    def emit(self, eng):
        seen = {}
        for fn, after, tok, dsem in self.ops:
            need = {}
            for t in after:
                if self.skip_own and t.sem is self.sem:
                    continue
                k = id(t.sem)
                if t.val > need.get(k, (None, 0))[1]:
                    need[k] = (t.sem, t.val)
            for k, (s, v) in need.items():
                if seen.get(k, 0) < v:
                    eng.wait_ge(s, v)
                    seen[k] = v
            if fn is None:
                continue
            ins = fn(eng)
            if dsem is not None:
                ins.then_inc(dsem, 16)
            elif tok.used:
                ins.then_inc(self.sem, 1)

    skip_own = False


def bc(ap, dim, n):
    a = [list(x) for x in ap.ap]
    a.insert(dim, [0, n])
    return bass.AP(ap.tensor, ap.offset, a)


class Banks:

    def __init__(self, tensors):
        self.banks = [{"ap": t, "free": [], "had": None} for t in tensors]

    def get(self):
        b = next(b for b in self.banks if b["free"] is not b["had"])
        self.banks.remove(b)
        self.banks.append(b)
        b["had"] = b["free"]
        return b


def pipeline(gens, width, fill):
    gens, active = list(gens), []
    while gens or active:
        if gens and len(active) < width:
            active.append(gens.pop(0))
        for g in list(active):
            if next(g, "end") == "end":
                active.remove(g)
            fill()


def build_program(nc, csizes, plan, debug=None):
    ctx = ExitStack()

    def sb(name, shape, dt=F32):
        return ctx.enter_context(nc.sbuf_tensor(name, shape, dt))

    def sem(name):
        return ctx.enter_context(nc.semaphore(name))

    def dram(name, shape, dt=F32, kind="ExternalInput"):
        return nc.dram_tensor(name, shape, dt, kind=kind).ap()

    with ctx:
        order = []
        nconst = sum(csizes.values())
        d_x = dram("xin", (128, 4096))
        d_c = dram("consts", (128, nconst))
        d_bm = dram("b1mask", (128, 1024))
        d_v = dram("vecs", (128, NVEC))
        d_m = dram("lmask", (128, 896))
        d_oh = dram("onehot", (32, 512))
        d_t5 = dram("t5t", (32, 8))
        d_na = dram("narel", (8, 465))
        d_out = dram("yout", (128, 2048), kind="ExternalOutput")
        d_line = dram("lines", (8, 512), kind="Internal")
        d_sk = dram("dilskew", (8, 128, 512), kind="Internal")
        d_nk = dram("naskew", (8, 64, 465), kind="Internal")

        WR = [sb(f"wr{i}", [128, 1024]) for i in range(NRAW)]
        WH = [sb(f"wh{i}", [128, 1024], F32R) for i in range(NSPL)]
        WL = [sb(f"wl{i}", [128, 1024], F32R) for i in range(NSPL)]
        X = sb("X", [128, 8, 512])
        HH = sb("HH", [128, 8, 512], F32R)
        HL = sb("HL", [128, 8, 512], F32R)
        TM = Banks([sb(f"tm{i}", [128, 512]) for i in range(3)])
        RM = Banks([sb(f"rm{i}", [128, 512]) for i in range(1)])
        CT = sb("CT", [128, nconst])
        V = sb("V", [128, NVEC])
        LM = sb("LM", [128, 896], U8)
        MOD = sb("MOD", [128, 2, 48, 2])
        GS = sb("GS", [128, 2, 2, 8, 2])
        CS = sb("CS", [128, 8, 32])
        LB = sb("LB", [128, 5, 8])
        ST = sb("ST", [128, 4, 8])
        base = (nc.sbuf_base + 31) // 32 * 32
        sb("arena", [128, (ARENA + 64) // 4])

        def at_(name, kb, shape, dt=F32):
            n = 4
            for d in shape:
                n *= d
            assert kb * KB_ + n <= ARENA, name
            return nc.alloc_sbuf_tensor_at(name, [128] + shape, dt, offset=base + int(kb * KB_))

        psum = [ctx.enter_context(nc.psum_tensor(f"ps{i}", [128, 512], F32)) for i in range(8)]
        main = Banks(psum[0:4])
        aux = Banks(psum[4:8])

        sync, pe = Queue(sem("s_sync")), Queue(sem("s_pe"))
        act, dve, pool = Queue(sem("s_act")), Queue(sem("s_dve")), Queue(sem("s_pool"))
        pe.skip_own = True
        slot_sem = [sem(f"s_w{i}") for i in range(NRAW)]
        s_out = sem("s_out")

        const = {}
        at = 0
        for n, w in csizes.items():
            const[n] = CT[:, at:at + w]
            at += w
        ident, ones, blk = const["ident"], const["ones"], const["blk"]
        ones256 = bass.AP(ones.tensor, ones.offset, [list(ones.ap[0]), [0, 256]])

        def vec(name, j, n=1):
            return V[:, VEC[name][0] + j:VEC[name][0] + j + n]

        class Stream:
            def __init__(self):
                self.n, self.col, self.kind = -1, 1024, None
                self.next_dma = self.next_split = 0
                self.low = dve
                self.raw_done, self.spl_done, self.dma_tok, self.spl_tok = {}, {}, {}, {}

            def pump(self, upto):
                while self.next_dma <= upto and (self.next_dma < NRAW or self.next_dma - NRAW in self.raw_done):
                    n = self.next_dma
                    slot = n % NRAW
                    self.dma_tok[n] = sync.dma(lambda e, n=n, slot=slot: e.dma_start(WR[slot][:, :], d_w[n]),
                                               slot_sem[slot], 16 * (n // NRAW + 1), self.raw_done.get(n - NRAW))
                    self.next_dma += 1

            def split(self, upto):
                while self.next_split <= upto:
                    n = self.next_split
                    self.pump(n)
                    if n == self.n or (n < len(plan) and plan[n]):
                        src, i = WR[n % NRAW][:, :], n % NSPL
                        hi, lo = WH[i][:, :], WL[i][:, :]
                        free = self.spl_done.get(n - NSPL)
                        th = act(lambda e, hi=hi, src=src: e.activation(hi, src, ACT.Copy), self.dma_tok[n], free)
                        tl = self.low(lambda e, hi=hi, lo=lo, src=src: e.tensor_tensor(
                            lo, src, hi.bitcast(F32), ALU.subtract), th, free)
                        self.spl_tok[n] = (th, tl)
                        self.raw_done[n] = [tl]
                    self.next_split += 1

            def get(self, name, k, cols, split=True):
                w = sum(b - a for a, b in cols)
                if self.col + w > 1024 or split != self.kind:
                    self.n, self.col, self.kind = self.n + 1, 0, split
                    kinds.append(split)
                    if plan:
                        assert plan[self.n] == split
                        self.split(min(self.n + AHEAD, len(plan) - 1))
                        self.pump(min(self.n + NRAW, len(plan) - 1))
                n, c = self.n, self.col
                order.append((n, c, name, k, tuple(cols)))
                self.col += w
                if not plan:
                    z = WH[0][:, c:c + w]
                    return (z, z, (None, None)) if split else (WR[0][:, c:c + w], None)
                if split:
                    i = n % NSPL
                    return WH[i][:, c:c + w], WL[i][:, c:c + w], self.spl_tok[n]
                return WR[n % NRAW][:, c:c + w], self.dma_tok[n]

            def used(self, tok):
                self.spl_done[self.n] = [tok]
                if not self.kind:
                    self.raw_done[self.n] = [tok]

        kinds = []
        W = Stream()

        def mm(out, lhsT, rhs, start, stop, *after, **kw):
            return pe(lambda e: e.matmul(out, lhsT, rhs, start=start, stop=stop, **kw), *after)

        def tr(out, in_, *after):
            return pe(lambda e: e.transpose(out, in_, ident), *after)

        def mm3(out, ah, al, bh, bl, start, stop, ta, tb, *after):
            mm(out, ah, bh, start, False, ta[0], tb[0], after)
            mm(out, ah, bl, False, False, tb[1])
            return mm(out, al, bh, False, stop, ta[1])

        def wmm(bank_ap, name, ks, cols, rhs, *after):
            t = None
            for i, k in enumerate(ks):
                wh, wl, wt = W.get(name, k, cols)
                xh, xl, xt = rhs(i)
                t = mm3(bank_ap, wh, wl, xh, xl, i == 0, i == len(ks) - 1, wt, xt, after if i == 0 else None)
                W.used(t)
            return t

        table = [None]

        def a_act(out, in_, func, *after, **kw):
            if func in (ACT.Exp, ACT.Ln):
                if table[0] != "log_exp":
                    act(lambda e: e.preload_act_table_set("natural_log_exp_and_others"))
                table[0] = "log_exp"
            elif func in (ACT.Silu, ACT.Sigmoid):
                table[0] = func
            return act(lambda e: e.activation(out, in_, func, **kw), *after)

        def tt(out, a, b, op, *after, q=None):
            return (q or dve)(lambda e: e.tensor_tensor(out, a, b, op), *after)

        def ts(out, a, s1, s2, op0, op1, *after):
            if op1 is None:
                return dve(lambda e: e.tensor_scalar(out, a, s1, None, op0), *after)
            return dve(lambda e: e.tensor_scalar(out, a, s1, s2, op0, op1), *after)

        def stt(out, a, s, b, op0, op1, *after):
            return dve(lambda e: e.scalar_tensor_tensor(out=out, in0=a, scalar=s, in1=b, op0=op0, op1=op1), *after)

        def vcopy(out, a, *after):
            return dve(lambda e: e.tensor_copy(out, a), *after)

        n_load = [0]
        outs = []

        def load(q, dst, src, *after):
            s = sem(f"s_ld{n_load[0]}")
            n_load[0] += 1
            return q.dma(lambda e: e.dma_start(dst, src), s, 16, *after)

        def dump(name, ap, *after):
            if plan and debug is not None and name in debug:
                shp = [p for p in ap.shape]
                d = nc.dram_tensor("dbg_" + name, shp, F32, kind="ExternalOutput").ap()
                outs.append(pool.dma(lambda e: e.dma_start(d, ap), sem("s_d" + name), 16, *after))
                for q in (pe, act, dve, pool):
                    q(None, outs[-1])

        xd = d_x.rearrange("p (k t) -> p k t", k=8)
        t_v = load(act, V[:, :], d_v)
        t_xk = [load(act, X[:, 2 * i:2 * i + 2, 0:256], xd[:, 2 * i:2 * i + 2, 0:256]) for i in range(4)]
        t_x = [t_xk[i // 2] for i in range(8)]
        t_c = load(act, CT[:, 0:NFIRST], d_c[:, 0:NFIRST])
        B1M = at_("B1M", 84, [1024])
        NAB = at_("NAB", 44, [2, 8, 256])
        DILB = at_("DILB", 60, [2, 8, 256])
        OHT = at_("OHT", 88, [512])
        T5T = at_("T5T", 90, [8])
        LNT = at_("LNT", 91, [512])
        LMF = at_("LMF", 93, [896])
        hid_free = []
        bias = {}

        def bias_loads():
            after = pe.last
            bias["ctx"] = load(pool, X[:, :, 256:512], xd[:, :, 256:512], after)
            bias["const"] = load(pool, CT[:, NFIRST:], d_c[:, NFIRST:])
            bias["oh"] = load(pool, OHT[0:32, :], d_oh)
            bias["t5"] = load(pool, T5T[0:32, :], d_t5)
            bias["lm"] = load(pool, LMF[:, :], d_m)
            bias["bm"] = load(pool, B1M[:, :], d_bm)
            t_nk = pool.dma(lambda e: e.dma_start(d_nk, bass.AP(d_na.tensor, 0, [[465, 8], [0, 64], [1, 465]])),
                            sem("s_nk"), 16)
            s_nb = sem("s_nb")
            for a in range(2):
                for r in range(2):
                    for kr in range(4):
                        row = 2 * a + r
                        src = bass.AP(d_nk.tensor, (kr - row + 7) * 31 + 15, [[464, 64], [64 * 465, 8], [1, 64]])
                        dst = NAB[64 * r:64 * r + 64, a, :, kr * 64:kr * 64 + 64]
                        t = pool.dma(lambda e, src=src, dst=dst: e.dma_start(dst, src), s_nb, 16 * 16, t_nk)
            bias["nb"] = t
            outs.append(t_nk)

        def bias_skew():
            bias["lmask"] = vcopy(LM[:, :], LMF[:, :], bias["lm"])
            b = aux.get()
            t = mm(b["ap"][0:8, :], T5T[0:32, :], OHT[0:32, :], True, True, bias["oh"], bias["t5"], b["free"])
            t = vcopy(LNT[0:8, :], b["ap"][0:8, :], t)
            b["free"] = [t]
            t_ln = load(pool, d_line, LNT[0:8, :], t)
            t_sk = pool.dma(lambda e: e.dma_start(d_sk, bass.AP(d_line.tensor, 0, [[512, 8], [0, 128], [1, 512]])),
                            sem("s_sk"), 16, t_ln)
            outs.extend([t_ln, t_sk])
            bias["line"] = t_ln
            s_db = sem("s_db")
            for a in range(2):
                src = bass.AP(d_sk.tensor, 255 - 128 * a, [[511, 128], [65536, 8], [1, 256]])
                bias["db"] = pool.dma(lambda e, src=src, a=a: e.dma_start(DILB[:, a], src), s_db, 32, t_sk)

        t = dve(lambda e: e.memset(CS[:, :, :], 0.0))
        cc = V[:, VEC["cc"][0]:VEC["cc"][0] + 16].rearrange("p (k c) -> p k c", c=2)
        t_cs = a_act(CS[:, :, 0:2], cc, ACT.Silu, t, t_v)

        def modulation(l):
            for r in range(3):
                b = aux.get()
                free = list(b["free"])
                for k in range(8):
                    for j in range(4):
                        ap, wt = W.get(("w_mod_2", l), k, [((4 * r + j) * 512, (4 * r + j + 1) * 512)], False)
                        t = mm(b["ap"][32 * j:32 * j + 32, :], CS[:, k, :], ap, k == 0, k == 7,
                               wt, t_cs, free if k == 0 else None)
                        W.used(t)
                    if k < 7:
                        yield
                tm = TM.get()
                t = vcopy(tm["ap"][:, :], b["ap"][:, :], t, tm["free"])
                b["free"] = [t]
                b = aux.get()
                for c in range(4):
                    t2 = tr(b["ap"][:, 128 * c:128 * c + 128], tm["ap"][:, 128 * c:128 * c + 128], t, b["free"], t_c)
                tm["free"] = [t2]
                src = b["ap"][:, :].rearrange("p (ch j z) -> p ch j z", ch=4, j=4)[:, :, :, 0:2]
                dst = MOD[:, l, 16 * r:16 * r + 16, :].rearrange("p (j ch) c -> p ch j c", ch=4)
                bm = bc(vec("b_mod_2", 48 * l + 16 * r, 16).rearrange("p (j ch) -> p ch j", ch=4), 3, 2)
                t = tt(dst, src, bm, ALU.add, t2)
                b["free"] = [t]
            for i, (nm, sc) in enumerate((("norm1_g_2", 8), ("norm2_g_2", 32))):
                g = bc(vec(nm, 8 * l, 8), 2, 2)
                t = stt(GS[:, l, i], MOD[:, l, sc:sc + 8, :], 1.0, g, ALU.add, ALU.mult, t)
            t_mod[l] = t
            yield

        t_mod = [None, None]
        mods = [modulation(0), modulation(1)]
        mod_steps = [0, 0]

        def fill_mod(l=0, n=1):
            for _ in range(n):
                if next(mods[l], "end") != "end":
                    mod_steps[l] += 1

        lg = vec("hgrn_lb_logits_2", 0, 16)
        l0, l1 = lg[:, 0:8], lg[:, 8:16]
        t = tt(LB[:, 0, :], l0, l1, ALU.max, t_v)
        t1 = tt(LB[:, 1, :], l0, LB[:, 0, :], ALU.subtract, t)
        t2 = tt(LB[:, 2, :], l1, LB[:, 0, :], ALU.subtract, t)
        t = a_act(LB[:, 3:5, :], LB[:, 1:3, :], ACT.Exp, t1, t2)
        t = tt(LB[:, 0, :], LB[:, 3, :], LB[:, 4, :], ALU.add, t)
        t = a_act(LB[:, 1, :], LB[:, 0, :], ACT.Ln, t)
        t = tt(LB[:, 2, :], LB[:, 2, :], LB[:, 1, :], ALU.subtract, t)
        t1 = a_act(LB[:, 3, :], LB[:, 2, :], ACT.Exp, t)
        t2 = ts(LB[:, 0, :], LB[:, 2, :], LOG_FLOOR, None, ALU.max, None, t1)
        t_lb = ts(LB[:, 1, :], LB[:, 3, :], -1.0, 1.0, ALU.mult, ALU.add, t1)
        t_lb = [t_lb, t2, ts(LB[:, 4, :], LB[:, 0, :], -1.0, None, ALU.mult, None, t2)]

        def square_sums(src, T, first, last, t, over):
            tm = TM.get()
            t = a_act(tm["ap"][:, 0:T], src, ACT.Square, t, tm["free"])

            def add(b):
                t2 = mm(b["ap"][:, 0:T], over, tm["ap"][:, 0:T], first, last, t, t_c, b["free"] if first else None)
                tm["free"] = [t2]
                return t2
            return add

        def inverse_root(b, T, D, t, refine=False):
            r = RM.get()
            x, s = r["ap"][:, 0:T], b["ap"][:, 0:T]
            if not refine:
                t = a_act(x, s, ACT.Ln, t, r["free"], bias=vec("eps", 0), scale=1.0 / D)
                b["free"] = [t]
                return r, a_act(x, x, ACT.Exp, t, scale=-0.5)
            tm = TM.get()
            v = tm["ap"][:, 0:T]
            tv = ts(v, s, -0.5 / D, -0.5 * EPS, ALU.mult, ALU.add, t, tm["free"])
            b["free"] = [tv]
            t = a_act(x, v, ACT.Ln, tv, r["free"], scale=-2.0)
            t = a_act(x, x, ACT.Exp, t, scale=-0.5)
            t = tt(v, v, x, ALU.mult, t)
            t = tt(v, v, x, ALU.mult, t)
            t = stt(x, v, 1.5, x, ALU.add, ALU.mult, t)
            tm["free"] = [t]
            return r, t

        def rstd(src, n, T, D, toks, refine=False):
            b = aux.get()
            for i in range(n):
                t = square_sums(src(i), T, i == 0, i == n - 1, toks[i], ones)(b)
            return inverse_root(b, T, D, t, refine)

        class Lag:

            def __init__(self):
                self.part = None

            def __call__(self, part=None):
                if self.part:
                    self.part()
                self.part = part

        def halves(hi, lo, src, *after):
            th = a_act(hi, src, ACT.Copy, after)
            return [th, tt(lo, src, hi.bitcast(F32), ALU.subtract, th)]

        h_free = []

        def norm_plain(g, toks, steps=0):
            r, t = rstd(lambda i: X[:, i, 0:256], 8, 256, 1024, toks)
            out, lag = [], Lag()
            for i in range(8):
                tm = TM.get()
                v, hi, lo = tm["ap"][:, 0:256], HH[:, i, 0:256], HL[:, i, 0:256]
                t2 = stt(v, X[:, i, 0:256], vec(g, i), r["ap"][:, 0:256], ALU.mult, ALU.mult, t, tm["free"])
                th = a_act(hi, v, ACT.Copy, t2, h_free)

                def low(tm=tm, v=v, hi=hi, lo=lo, th=th):
                    out.append([th, tt(lo, v, hi.bitcast(F32), ALU.subtract, th)])
                    tm["free"] = out[-1]
                lag(low)
            lag()
            r["free"] = [t2]
            fill_mod(0, steps)
            return out

        def xrhs(toks, T=256):
            return lambda i: (HH[:, i, 0:T], HL[:, i, 0:T], toks[i])

        Y = at_("Y", 76, [8, 256])
        y_free = []

        def residual_norm(g, half, toks):
            r, t = rstd(lambda i: Y[:, i, :], 8, 256, 1024, [toks[i // 2] for i in range(8)])
            out = []
            for i in range(8):
                t2 = stt(Y[:, i, :], Y[:, i, :], vec(g, i), r["ap"][:, 0:256], ALU.mult, ALU.mult, t)
                out.append(stt(X[:, i, 0:256], Y[:, i, :], half, X[:, i, 0:256], ALU.mult, ALU.add, t2))
            r["free"] = [t2]
            y_free[:] = [out[-1]]
            return out

        def pair_out(name, ks, rhs, n_pairs, dst, *after):
            toks = []
            for j in range(n_pairs):
                b = main.get()
                for h in range(2):
                    c = (2 * j + h) * 128
                    t = wmm(b["ap"][:, 256 * h:256 * h + 256], name, ks, [(c, c + 128)], rhs, b["free"])
                out = dst(j)
                src = b["ap"][:, :].rearrange("p (h t) -> p h t", h=2)
                t = vcopy(out, src, t, after)
                b["free"] = [t]
                toks.append(t)
            return toks

        NH = at_("NHH", 0, [22, 256], F32R)
        NL = at_("NHL", 22, [22, 256], F32R)

        def ffn(n, toks, hooks):
            ht = []
            rhs = xrhs(toks)
            for f in range(22):
                b = main.get()
                c = [(f * 128, f * 128 + 128)]
                t = wmm(b["ap"][:, 0:256], (f"ffn{n}_w_gate", 0), range(8), c, rhs, b["free"])
                t = wmm(b["ap"][:, 256:512], (f"ffn{n}_w_up", 0), range(8), c, rhs)
                tm = TM.get()
                v = tm["ap"][:, 0:256]
                t1 = a_act(v, b["ap"][:, 0:256], ACT.Silu, t, tm["free"])
                t1 = tt(v, v, b["ap"][:, 256:512], ALU.mult, t1)
                b["free"] = [t1]
                ht.append(halves(NH[:, f, :], NL[:, f, :], v, t1, hid_free))
                tm["free"] = ht[-1]
                if f in hooks:
                    hooks[f]()
            h_free[:] = [pe.last]
            out = pair_out((f"ffn{n}_w_down", 0), range(22), lambda i: (NH[:, i, :], NL[:, i, :], ht[i]), 4,
                           lambda j: Y[:, 2 * j:2 * j + 2, :], y_free)
            hid_free[:] = [pe.last]
            return out

        if plan:
            W.pump(NRAW - 1)
            W.split(AHEAD - 1)
        toks = norm_plain("ffn1_pre_g", t_x)
        toks = ffn(1, toks, {0: bias_loads, 7: bias_skew})
        toks = residual_norm("ffn1_post_g", 0.5, toks)
        dump("x1", X[:, :, 0:256], toks)
        toks = norm_plain("mix_pre_g", toks, 3)

        bt = []
        t_bm = bias["bm"]
        t_lm = bias["lmask"]
        for m, B, tb in ((0, NAB, bias["nb"]), (1, DILB, bias["db"])):
            for a in range(2):
                mk = B1M[:, 512 * m + 256 * a:512 * m + 256 * a + 256]
                bt.append(tt(B[:, a], B[:, a], bc(mk, 1, 8), ALU.add, tb, t_bm))

        QT = at_("QT", 0, [8, 256])
        KT = at_("KT", 8, [8, 256])
        VR = at_("VR", 16, [2, 1024])
        OT = at_("OT", 24, [8, 256])
        rhs = xrhs(toks)
        qk = pair_out(("w_qkv", 0), range(8), rhs, 8,
                      lambda j: (QT if j < 4 else KT)[:, 2 * (j % 4):2 * (j % 4) + 2, :], hid_free)

        def value_rows(name, c0, tiles, toks, dst, *after):
            bs = [main.get() for _ in range(tiles)]
            for k in range(8):
                wh, wl, wt = W.get(name, k, [(c0, c0 + 512)])
                for a in range(tiles):
                    sl = slice(128 * a, 128 * a + 128)
                    t = mm3(bs[a]["ap"][:, :], HH[:, k, sl], HL[:, k, sl], wh, wl, k == 0, k == 7, toks[k], wt,
                            bs[a]["free"] if k == 0 else None)
                W.used(t)
            out = []
            for a in range(tiles):
                t2 = vcopy(dst(a), bs[a]["ap"][:, :], t, after)
                bs[a]["free"] = [t2]
                out.append(t2)
            return out

        vt = []
        for h in range(2):
            vt += value_rows(("w_qkv", 0), 2048 + 512 * h, 2, toks, lambda a: VR[:, a, 512 * h:512 * h + 512], hid_free)
        h_free[:] = [pe.last]

        NB_ = 4
        st_free = [[] for _ in range(NB_)]
        unit_no = [0]

        class Unit:

            def __init__(self, score, rows, bias, sinkcol, pv, after_score, after_v, sbuf, pbuf):
                self.score, self.rows, self.bias, self.sinkcol = score, rows, bias, sinkcol
                self.pv, self.after_score, self.after_v = pv, after_score, after_v
                self.s, self.pbuf = sbuf.get(), pbuf
                self.i = unit_no[0] % NB_
                unit_no[0] += 1

            def scores(self):
                b = self.b = aux.get()
                self.t0 = self.score(b, self.after_score)
                if self.bias and self.bias[2] < 512:
                    w = self.bias[2]
                    self.t0 = a_act(self.s["ap"][:, w:512], b["ap"][:, w:512], ACT.Copy, self.t0, self.s["free"],
                                    scale=0.125)

            def first(self):
                b, t, s, rows = self.b, self.t0, self.s["ap"][:, :], self.rows
                self.sv = s.rearrange("p (r k) -> p r k", r=rows)
                self.n = 512 // rows
                if self.bias is None:
                    t = ts(s, b["ap"][:, :], 0.125, None, ALU.mult, None, t, self.s["free"])
                else:
                    bias, tb, w = self.bias
                    if w < 512:
                        t = [stt(s[:, 0:w], b["ap"][:, 0:w], 0.125, bias, ALU.mult, ALU.add, t, tb), t]
                    else:
                        src = b["ap"][:, :].rearrange("p (r k) -> p r k", r=rows)
                        t = stt(self.sv, src, 0.125, bias, ALU.mult, ALU.add, t, tb, self.s["free"])
                b["free"] = [t]
                self.t0 = t

            def reduce(self):
                i, rows, sv, t = self.i, self.rows, self.sv, self.t0
                mx = ST[:, i, 0:rows]
                t = dve(lambda e: e.tensor_reduce(mx, sv, AX, ALU.max), t, st_free[i])
                nm = ST[:, i, 2:2 + rows]
                if self.sinkcol is not None:
                    t = ts(nm, mx, self.sinkcol, -1.0, ALU.max, ALU.mult, t, t_v)
                else:
                    t = ts(nm, mx, -1.0, None, ALU.mult, None, t)
                den = ST[:, i, 4:4 + rows]
                ta = [a_act(sv[:, r, :], sv[:, r, :], ACT.Exp, t, bias=nm[:, r:r + 1], accum_out=den[:, r:r + 1])
                      for r in range(rows)]
                if self.sinkcol is not None:
                    ta.append(a_act(ST[:, i, 6:6 + rows], nm, ACT.Exp, t, bias=self.sinkcol))
                self.ta, self.den = ta, den

            def mid(self):
                i, den, ta = self.i, self.den, self.ta
                if self.sinkcol is not None:
                    ta = tt(den, den, ST[:, i, 6:6 + self.rows], ALU.add, ta)
                t = dve(lambda e: e.reciprocal(den, den), ta)
                self.t = tt(self.sv, self.sv, bc(den, 2, self.n), ALU.mult, t)
                st_free[i] = [self.t]

            def second(self):
                b = aux.get()
                self.p = self.pbuf.get()
                for c in range(4):
                    sl = slice(128 * c, 128 * c + 128)
                    t = tr(b["ap"][:, sl], self.s["ap"][:, sl], self.t, b["free"])
                self.s["free"] = [t]
                t = a_act(self.p["ap"][:, :], b["ap"][:, :], ACT.Copy, t, self.p["free"])
                b["free"] = [t]
                self.t2 = t

            def third(self):
                self.p["free"] = [self.pv(self.p["ap"], self.t2, self.after_v)]

        def run_units(units, sring, fill):
            extra = TM.get()
            sring.banks.append(extra)
            extra["had"] = None
            n = len(units)
            made = []
            for j in range(-1, n + 3):
                if j + 1 < n:
                    made.append(units[j + 1]())
                    made[j + 1].scores()
                if 0 <= j < n:
                    made[j].reduce()
                if j + 1 < n:
                    made[j + 1].first()
                if 1 <= j <= n:
                    made[j - 1].mid()
                if 2 <= j <= n + 1:
                    made[j - 2].second()
                fill()
                if j >= 3:
                    made[j - 3].third()
            sring.banks.remove(extra)

        otoks = []
        S1 = Banks([at_(f"s1_{i}", 84 + 2 * i, [512]) for i in range(3)])
        P1B = Banks([at_(f"p1_{i}", 90 + 2 * i, [512]) for i in range(3)])
        for q in S1.banks + P1B.banks:
            q["free"] = [bt, bias["line"], t_lm]
        held = {}

        def block1_unit(kind, h):
            head = 8 * kind + h
            j, off = head // 2, 64 * (head % 2)

            def score(b, after):
                for a in range(2):
                    t = mm(b["ap"][:, 256 * a:256 * a + 256], QT[off:off + 64, j, 128 * a:128 * a + 128],
                           KT[off:off + 64, j, :], True, True, after, b["free"])
                return t

            def pv(P, tp, after):
                if off == 0:
                    held["b"] = main.get()
                b = held["b"]
                for a in range(2):
                    for kt in range(2):
                        t = mm(b["ap"][off:off + 64, 128 * a:128 * a + 128],
                               VR[:, kt, 64 * head:64 * head + 64], P[:, 256 * a + 128 * kt:256 * a + 128 * kt + 128],
                               kt == 0, kt == 1, tp, after, b["free"])
                if off:
                    t2 = vcopy(OT[:, j, :], b["ap"][:, 0:256], t, hid_free)
                    b["free"] = [t2]
                    otoks.append(t2)
                return t
            return lambda: Unit(score, 2, ((NAB, DILB)[kind][:, :, h, :], bt, 512), None, pv, qk, vt, S1, P1B)

        run_units([block1_unit(kind, h) for kind in range(2) for h in range(8)], S1,
                  fill_mod)
        dump("o1", OT[:, :, :], otoks)
        ot2 = []
        for part, g in ((0, "na_out_g"), (1, "dil_out_g")):
            r, t = rstd(lambda i: OT[:, 4 * part + i, :], 4, 256, 512, otoks[4 * part:4 * part + 4])
            for i in range(4):
                n = 4 * part + i
                t2 = stt(OT[:, n, :], OT[:, n, :], vec(g, i), r["ap"][:, 0:256], ALU.mult, ALU.mult, t)
                ot2.append(halves(HH[:, n, 0:256], HL[:, n, 0:256], OT[:, n, :], t2, h_free))
            r["free"] = [t2]
        toks = pair_out(("w_out", 0), range(8), xrhs(ot2), 4, lambda j: Y[:, 2 * j:2 * j + 2, :], y_free)
        h_free[:] = [pe.last]
        hid_free[:] = [pe.last]
        toks = residual_norm("mix_post_g", 1.0, toks)
        dump("x2", X[:, :, 0:256], toks)
        toks = norm_plain("ffn2_pre_g", toks, 3)
        toks = ffn(2, toks, {})
        xt = residual_norm("ffn2_post_g", 0.5, toks)
        fill_mod(0, 30)
        dump("x3", X[:, :, 0:256], xt)
        ct = [bias["ctx"]] * 8
        for q in (pe, dve):
            q(None, bias["const"])

        GA = at_("GA", 0, [12, 512])
        GB = at_("GB", 40, [12, 512])
        G1 = at_("G1", 0, [24, 256])
        YA = at_("YA", 0, [12, 512], F32R)
        YB = at_("YB", 40, [12, 512], F32R)
        Y1 = at_("Y1", 0, [24, 256], F32R)
        Qh = at_("Qh", 24, [4, 512])
        KF = at_("KF", 32, [4, 512])
        KB = at_("KB", 40, [4, 512])
        EF = at_("EF", 48, [4, 2, 257])
        EB = at_("EB", 56.25, [4, 2, 257])
        VH = at_("VH", 64.5, [4, 512])
        AT = at_("AT", 72.5, [2, 4, 256])
        D = [at_(f"D{i}", 80.5 + 8 * i, [2, 4, 256]) for i in range(2)]
        ZB = at_("ZB", 0, [4, 512])
        PB = at_("PB", 8, [4, 512])
        LF = at_("LF", 16, [4, 512])
        A2 = at_("A2", 80.5, [2, 4, 512])
        OHH = at_("OHH", 64.5, [4, 512], F32R)
        OHL = at_("OHL", 72.5, [4, 512], F32R)
        GH = at_("GH", 32, [4, 512])
        FR = at_("FR", 80.5, [4, 512])
        Q2 = at_("Q2", 88.5, [4, 512])
        K2 = at_("K2", 24, [512])
        V2 = at_("V2", 26, [4, 128])
        S2 = [at_(f"s2_{i}", 28 + 2 * i, [512]) for i in range(3)]
        P2 = [at_(f"p2_{i}", 34 + 2 * i, [512]) for i in range(3)]
        HIDH = at_("HIDH", 0, [16, 512], F32R)
        HIDL = at_("HIDL", 32, [16, 512], F32R)
        HIDH1 = at_("HIDH1", 0, [32, 256], F32R)
        HIDL1 = at_("HIDL1", 32, [32, 256], F32R)

        c_ = {}
        at = 0
        for n, w in (("k", 128), ("v", 128), ("i", 512), ("ff", 512), ("fb", 512), ("q", 512), ("qh", 512),
                     ("gh", 512), ("four", 512), ("gate", 3072)):
            c_[n] = at
            at += w
        a_free = [pe.last, xt[-1]]

        def adaln(l, i, T, xt, ct):
            toks = [[xt[k]] + ([ct[k]] if T > 256 else []) for k in range(8)]
            r, t = rstd(lambda k: X[:, k, 0:T], 8, T, 1024, toks)
            out, lag = [], Lag()
            for k in range(8):
                tm = TM.get()
                ths = []
                for c in range(T // 256):
                    sl = slice(256 * c, 256 * c + 256)
                    v = tm["ap"][:, sl]
                    sh = MOD[:, l, 24 * i + k, c:c + 1]
                    t2 = stt(v, X[:, k, sl], GS[:, l, i, k, c:c + 1], r["ap"][:, sl], ALU.mult, ALU.mult,
                             t, tm["free"], t_mod[l])
                    ths.append(a_act(HH[:, k, sl], v, ACT.Identity, t2, h_free, bias=sh))

                def low(k=k, tm=tm, ths=ths):
                    tls = []
                    for c, th in enumerate(ths):
                        sl = slice(256 * c, 256 * c + 256)
                        tls.append(stt(HL[:, k, sl], tm["ap"][:, sl], MOD[:, l, 24 * i + k, c:c + 1],
                                       HH[:, k, sl].bitcast(F32), ALU.add, ALU.subtract, th))
                    out.append([ths, tls])
                    tm["free"] = tls
                lag(low)
            lag()
            r["free"] = [t2]
            if l == 0:
                fill_mod(1, 2)
            return out

        for l in range(2):
            T = 512 if l == 0 else 256
            win = ("w_in_2", l)
            ht = adaln(l, 0, 512, xt, ct)
            rT, r512 = xrhs(ht, T), xrhs(ht, 512)

            def win_tile(cols, rhs, TT):
                b = main.get()
                return b, wmm(b["ap"][:, 0:TT], win, range(8), cols, rhs, b["free"])

            def forget(dr, seg, free):
                if l == 0:
                    loglb, neglb = [LOG_FLOOR] * 4, [vec("neglb", 0)] * 4
                else:
                    loglb = [LB[:, 0, 4 * dr + h:4 * dr + h + 1] for h in range(4)]
                    neglb = [LB[:, 4, 4 * dr + h:4 * dr + h + 1] for h in range(4)]
                K, E = (KF, KB)[dr], (EF, EB)[dr]
                tm = dve(lambda e: e.memset(E[:, :, :, 0:1], 0.0), a_free)
                out = []
                frees, free = free, None
                for h in range(4):
                    free = frees[h]
                    c = c_[seg] + 128 * h
                    b, t = win_tile([(c, c + 128)], r512, 512)
                    if l == 0:
                        fill_mod(1)
                    z = a_act(ZB[:, h, :], b["ap"][:, :], ACT.Copy, t, free)
                    b["free"] = [z]
                    t1 = a_act(A2[:, 1, h, :], ZB[:, h, :], ACT.Abs, z, t_lb, free, bias=neglb[h])
                    t0 = stt(A2[:, 0, h, :], ZB[:, h, :], -1.0, ZB[:, h, :], ALU.mult, ALU.max, z, free)
                    t = a_act(A2[:, :, h, :], A2[:, :, h, :], ACT.Exp, t1, t0, scale=-1.0)
                    t = a_act(A2[:, :, h, :], A2[:, :, h, :], ACT.Ln, t, bias=1.0)
                    tp = ts(PB[:, h, :], ZB[:, h, :], 0.0, None, ALU.max, None, z, free)
                    tz = stt(ZB[:, h, :], ZB[:, h, :], loglb[h], PB[:, h, :], ALU.max, ALU.subtract, tp, t1)
                    td = tt(LF[:, h, :], A2[:, 1, h, :], A2[:, 0, h, :], ALU.subtract, t, free)
                    tf = tt(LF[:, h, :], LF[:, h, :], ZB[:, h, :], ALU.add, td, tz)
                    tp = tt(PB[:, h, :], PB[:, h, :], A2[:, 0, h, :], ALU.add, t, tz)
                    tk = a_act(K[:, h, :], PB[:, h, :], ACT.Exp, tp, a_free, scale=-1.0)
                    for s in range(2):
                        t = dve(lambda e, h=h, s=s: e.tensor_tensor_scan(
                            E[:, h, s, 1:257], ones256, LF[:, h, 256 * s:256 * s + 256], 0.0, ALU.mult, ALU.add),
                            tf, t_c, a_free)
                    if l:
                        tk = ts(K[:, h, :], K[:, h, :], LB[:, 1, 4 * dr + h:4 * dr + h + 1], None, ALU.mult, None, tk)
                    out.append([t, tk, tm])
                return out

            f_tok = forget(0, "ff", [a_free] * 4)
            hq = []
            for h in range(4):
                c = c_["qh"] + 128 * h
                b, t = win_tile([(c, c + 128)], rT, T)
                t = a_act(Qh[:, h, 0:T], b["ap"][:, 0:T], ACT.Silu, t, a_free)
                b["free"] = [t]
                hq.append(t)
            f_tok = f_tok + forget(1, "fb", f_tok)
            d_free = [[f_tok], [f_tok]]
            dump(f"kf{l}", KF[:, :, :], f_tok)
            hv = value_rows(win, c_["i"], 4, ht, lambda a: VH[:, a, :], a_free)

            g_tok = {}

            def g_ap(n):
                if l:
                    return G1[:, n, :]
                return GA[:, n, :] if n < 12 else GB[:, n - 12, :]

            def gate(n, *after):
                d, br = n // 3, n % 3
                c = c_["gate"] + 1024 * br + 128 * d
                b, t = win_tile([(c, c + 128)], rT, T)
                t = a_act(g_ap(n), b["ap"][:, 0:T], ACT.Copy, t, after)
                b["free"] = [t]
                g_tok[n] = t

            n_gate = [0]

            def fill(last=12):
                if n_gate[0] < last:
                    gate(n_gate[0], f_tok, hg_done if last == 24 else None)
                    n_gate[0] += 1
                if l == 0:
                    fill_mod(1)

            hg_done = []
            at_free = list(a_free)
            ST0 = [KB[:, :, 256 + 128 * z:384 + 128 * z] for z in range(2)]

            def states():
                rows = []
                for dr in range(2):
                    E, K, Dk = (EF, EB)[dr], (KF, KB)[dr], D[0][:, dr]
                    if dr == 0:
                        te = [a_act(Dk[:, h, :], E[:, h, 1, 1:257], ACT.Exp, f_tok, d_free[0], scale=-1.0,
                                    bias=E[:, h, 1, 256:257]) for h in range(4)]
                    else:
                        te = a_act(Dk, E[:, :, 1, 0:256], ACT.Exp, f_tok, d_free[0])
                    t = tt(Dk, Dk, K[:, :, 256:512], ALU.mult, te)
                    fill()
                    KR = D[1][:, dr].rearrange("p h t -> p (h t)")
                    for a in range(2):
                        b = aux.get()
                        for h in range(4):
                            t2 = tr(b["ap"][:, 128 * h:128 * h + 128], Dk[:, h, 128 * a:128 * a + 128], t, b["free"])
                        t2 = vcopy(KR[:, 512 * a:512 * a + 512], b["ap"][:, :], t2, d_free[1])
                        b["free"] = [t2]
                        rows.append(t2)
                done = []
                for dr in range(2):
                    b = aux.get()
                    KR = D[1][:, dr].rearrange("p h t -> p (h t)").rearrange("p (a h k) -> p a h k", a=2, h=4)
                    for h in range(4):
                        for a in range(2):
                            t = mm(b["ap"][:, 128 * h:128 * h + 128], KR[:, a, h, :],
                                   VH[:, 2 + a, 128 * h:128 * h + 128], a == 0, a == 1, rows, hv, b["free"])
                    t = vcopy(ST0[dr], b["ap"][:, :].rearrange("p (h k) -> p h k", h=4), t)
                    b["free"] = [t]
                    done.append(t)
                d_free[:] = [[t], [t]]
                return done

            def recurrence(s):
                c0 = 256 * s
                q = Qh[:, :, c0:c0 + 256]
                kf, kb = KF[:, :, c0:c0 + 256], KB[:, :, c0:c0 + 256]
                last = []
                Ein = (EF[:, :, s, 1:257], EB[:, :, s, 1:257])
                Eex = (EF[:, :, s, 0:256], EB[:, :, s, 0:256])

                def prepare(lv):
                    Dd = D[(lv + 1) % 2]
                    df = d_free[(lv + 1) % 2]
                    if lv < 0:
                        return [tt(Dd[:, 1], kf, kb, ALU.add, f_tok, df)]
                    hh = 1 << lv

                    def v(ap, u):
                        return ap.rearrange("p h (b u j) -> p h b u j", u=2, j=hh)[:, :, :, u, :]

                    def mid(E):
                        return bc(E.rearrange("p h (b u j) -> p h b u j", u=2, j=hh)[:, :, :, 1, 0], 3, hh)
                    te = [tt(v(Dd[:, 0], 1), v(Ein[0], 1), mid(Eex[0]), ALU.subtract, f_tok, df),
                          tt(v(Dd[:, 0], 0), mid(Eex[1]), v(Eex[1], 0), ALU.subtract, f_tok, df),
                          tt(v(Dd[:, 1], 0), mid(Eex[0]), v(Ein[0], 0), ALU.subtract, f_tok, df),
                          tt(v(Dd[:, 1], 1), v(Eex[1], 1), mid(Eex[1]), ALU.subtract, f_tok, df, q=pool)]
                    return a_act(Dd[:, 0], Dd[:, 0], ACT.Exp, te[0:2]), a_act(Dd[:, 1], Dd[:, 1], ACT.Exp, te[2:4])

                def weigh(lv, te):
                    if lv < 0:
                        return te
                    Dd = D[(lv + 1) % 2]
                    hh = 1 << lv

                    def v(ap, u):
                        return ap.rearrange("p h (b u j) -> p h b u j", u=2, j=hh)[:, :, :, u, :]
                    return [tt(Dd[:, 0], Dd[:, 0], q, ALU.mult, te[0], hq),
                            tt(v(Dd[:, 1], 0), v(Dd[:, 1], 0), v(kf, 0), ALU.mult, te[1]),
                            tt(v(Dd[:, 1], 1), v(Dd[:, 1], 1), v(kb, 1), ALU.mult, te[1])]

                def products(lv, tq):
                    Dd = D[(lv + 1) % 2]
                    qs = q if lv < 0 else Dd[:, 0]
                    copies = []
                    for a in range(2):
                        b = (aux, main)[a].get()
                        qa = a if lv < 7 else 1 - a
                        for h in range(4):
                            t2 = mm(b["ap"][:, 128 * h:128 * h + 128], Dd[:, 1, h, 128 * a:128 * a + 128],
                                    qs[:, h, 128 * qa:128 * qa + 128], True, True, tq, hq, b["free"])
                        src = b["ap"][:, :].rearrange("p (h t) -> p h t", h=4)
                        dst = AT[:, a, :, 128 * qa:128 * qa + 128]

                        def copy(b=b, src=src, dst=dst, t2=t2):
                            if 0 <= lv < 7:
                                mk = bc(LM[:, 128 * lv:128 * lv + 128], 1, 4)
                                t3 = dve(lambda e: e.copy_predicated(dst, mk, src), t2, t_lm, last)
                            else:
                                t3 = vcopy(dst, src, t2, at_free)
                            b["free"] = [t3]
                            last.append(t3)
                        copies.append(copy)
                    d_free[(lv + 1) % 2] = [t2]
                    return lambda: [c() for c in copies]

                te = prepare(-1)
                lag = Lag()
                for lv in range(-1, 8):
                    tq = weigh(lv, te)
                    fill()
                    lag(products(lv, tq))
                    te = prepare(lv + 1) if lv < 7 else None
                lag()
                inter = []
                Dd = D[0]
                if s == 0:
                    t1 = a_act(Dd[:, 0], EF[:, :, 0, 1:257], ACT.Exp, f_tok, d_free[0])
                    for h in range(4):
                        t2 = a_act(Dd[:, 1, h, :], EB[:, h, 0, 0:256], ACT.Exp, f_tok, d_free[0], scale=-1.0,
                                   bias=EB[:, h, 0, 256:257])
                    inter = [tt(Dd[:, 0], Dd[:, 0], q, ALU.mult, t1, hq), tt(Dd[:, 1], Dd[:, 1], q, ALU.mult, t2, hq)]
                    fill()
                otok = []
                for hp in range(2):
                    b = aux.get()
                    for h in (2 * hp, 2 * hp + 1):
                        o = b["ap"][:, 256 * (h % 2):256 * (h % 2) + 256]
                        n = 4 if s == 0 else 2
                        for a in range(2):
                            t = mm(o, VH[:, 2 * s + a, 128 * h:128 * h + 128], AT[:, a, h, :], a == 0, a == n - 1,
                                   last, hv, b["free"])
                        if s == 0:
                            for z in range(2):
                                t = mm(o, ST0[z][:, h, :], Dd[:, z, h, :], False, z == 1, inter, b_s)
                    t2 = vcopy(Qh[:, 2 * hp:2 * hp + 2, c0:c0 + 256], b["ap"][:, :].rearrange("p (h t) -> p h t", h=2), t)
                    b["free"] = [t2]
                    otok.append(t2)
                at_free[:] = [t]
                d_free[0] = [d_free[0], t]
                return otok, t

            o_tok = []
            W.low = pool
            if l == 0:
                o_tok += recurrence(1)[0]
            b_s = states()
            ot, lastmm = recurrence(0)
            o_tok += ot
            W.low = dve
            hg_done[:] = [lastmm] + o_tok
            dump(f"oh{l}", Qh[:, :, 0:T], o_tok)
            while n_gate[0] < 12:
                fill()

            zb = Banks(P2)
            sbk = Banks(S2)
            gt, ft = {}, {}
            oht, oft, qt_ = [None] * 4, [None] * 4, [None] * 4
            v2t, kt_ = [], []

            def scale_norm(dst, TT, G, gcol, t):
                add = square_sums(dst, TT, True, True, t, blk if G == 2 else ones)
                yield
                b = aux.get()
                r, t = inverse_root(b, TT, 128 // G, add(b), True)
                t = stt(dst, dst, gcol, r["ap"][:, 0:TT], ALU.mult, ALU.mult, t)
                r["free"] = [t]
                yield t

            def gate_h(h):
                c = c_["gh"] + 128 * h
                b, t = win_tile([(c, c + 128)], rT, T)
                gt[h] = a_act(GH[:, h, 0:T], b["ap"][:, 0:T], ACT.Silu, t, hg_done)
                b["free"] = [gt[h]]

            def readout(h):
                o = Qh[:, h, 0:T]
                for t in scale_norm(o, T, 1, vec("hgrn_norm_g_2", l), o_tok):
                    if t is None:
                        yield
                t = tt(o, o, GH[:, h, 0:T], ALU.mult, t, gt[h])
                oht[h] = halves(OHH[:, h, 0:T], OHL[:, h, 0:T], o, t, hg_done)

            def head_norm(dst, cols, TT, gname, out, *after):
                b, t = win_tile(cols, xrhs(ht, TT), TT)
                t = vcopy(dst[:, 0:TT], b["ap"][:, 0:TT], t, after)
                b["free"] = [t]
                for t in scale_norm(dst[:, 0:TT], TT, 2, vec(gname, l), t):
                    yield
                b = aux.get()
                tm = TM.get()
                t2 = mm(b["ap"][:, 0:256], const["perm"], dst[:, 0:256], True, True, t, b["free"])
                t2 = tt(tm["ap"][:, 0:256], b["ap"][:, 0:256], const["ropes"], ALU.mult, t2, tm["free"])
                b["free"] = [t2]
                t = tt(dst[:, 0:256], dst[:, 0:256], const["ropec"], ALU.mult, t, t2)
                t = tt(dst[:, 0:256], dst[:, 0:256], tm["ap"][:, 0:256], ALU.add, t, t2)
                tm["free"] = [t]
                out(t)

            def values():
                b, t = win_tile([(c_["v"], c_["v"] + 128)], r512, 512)
                tm = TM.get()
                t = vcopy(tm["ap"][:, :], b["ap"][:, :], t, tm["free"])
                b["free"] = [t]
                yield
                b = aux.get()
                for c in range(4):
                    t2 = tr(b["ap"][:, 128 * c:128 * c + 128], tm["ap"][:, 128 * c:128 * c + 128], t, b["free"])
                tm["free"] = [t2]
                t = vcopy(V2[:, :, :], b["ap"][:, :].rearrange("p (a n) -> p a n", a=4), t2, gone)
                b["free"] = [t]
                v2t.append(t)

            def four_in(g):
                c = c_["four"] + 128 * g
                b, t = win_tile([(c, c + 128)], rT, T)
                t = vcopy(FR[:, g, 0:T], b["ap"][:, 0:T], t, hg_done)
                b["free"] = [t]
                ft[g] = t
                yield

            cdsd, ctm, nst = const["cdsd"], const["ct"], const["nst"]

            def fourier(g):
                for s in range(T // 256):
                    b = aux.get()
                    for a in range(2):
                        t = mm(b["ap"][:, 256 * a:256 * a + 256],
                               FR[:, g, 256 * s + 128 * a:256 * s + 128 * a + 128], cdsd, True, True, ft[g], b["free"])
                    z = zb.get()
                    t = vcopy(z["ap"][:, :], b["ap"][:, :], t, z["free"])
                    b["free"] = [t]
                    yield
                    bo = main.get()
                    Zb, o = z["ap"], bo["ap"][:, 0:256]
                    for a in range(2):
                        mm(o, Zb[:, 256 * a:256 * a + 128], ctm[:, 256 * a:256 * a + 256], a == 0, False, t,
                           bo["free"])
                        t2 = mm(o, Zb[:, 256 * a + 128:256 * a + 256], nst[:, 256 * a:256 * a + 256], False, a == 1)
                    z["free"] = [t2]
                    t = a_act(FR[:, g, 256 * s:256 * s + 256], o, ACT.Copy, t2)
                    bo["free"] = [t]
                oft[g] = t

            def fill_all():
                fill(24)

            gone = []
            for h in range(4):
                gate_h(h)
            pipeline([readout(h) for h in range(4)], 2, fill_all)
            gone[:] = [oht]
            for q in zb.banks + sbk.banks:
                q["free"] = [oht]
            c = c_["q"]
            pipeline([values(), head_norm(K2, [(c_["k"], c_["k"] + 128)], 512, "k_norm_g_2", kt_.append, gone)]
                     + [head_norm(Q2[:, j, :], [(c + 64 * j, c + 64 * j + 64), (c + 64 * j + 256, c + 64 * j + 320)],
                                  T, "q_norm_g_2", lambda t, j=j: qt_.__setitem__(j, t), hg_done) for j in range(4)]
                     + [four_in(g) for g in range(4)] + [fourier(g) for g in range(4)], 2, fill_all)

            a_tok = {}
            qkt = [kt_] + qt_

            fh = []

            def fill_end():
                if n_gate[0] < 24:
                    fill_all()
                    h_free[:] = [pe.last]
                elif len(fh) < 4:
                    g = len(fh)
                    fh.append(halves(HH[:, g, 0:T], HL[:, g, 0:T], FR[:, g, 0:T], oft[g], h_free))

            def keep_out(j, c0, b, t):
                t = vcopy(Q2[:, j, c0:c0 + 256], b["ap"][:, 0:256], t)
                b["free"] = [t]
                a_tok.setdefault(j, []).append(t)

            def x_unit(j, kv, a):
                off = 64 * kv

                def score(b, after):
                    return mm(b["ap"][:, :], Q2[off:off + 64, j, 128 * a:128 * a + 128], K2[off:off + 64, :],
                              True, True, after, b["free"])

                def pv(P, tp, after):
                    if a == 0 and kv == 0:
                        held["b"] = main.get()
                    b = held["b"]
                    for c in range(4):
                        t = mm(b["ap"][off:off + 64, 128 * a:128 * a + 128], V2[:, c, off:off + 64],
                               P[:, 128 * c:128 * c + 128], c == 0, c == 3, tp, after, b["free"])
                    if a == 1 and kv == 1:
                        keep_out(j, 0, b, t)
                    return t
                return lambda: Unit(score, 1, (const["win"][:, 256 * a:256 * a + 256], None, 256),
                                    vec("attn_sink_2", 8 * l + j + 4 * kv), pv, qkt, v2t, sbk, zb)

            def c_unit(j, kv):
                off = 64 * kv

                def score(b, after):
                    for a in range(2):
                        t = mm(b["ap"][:, 256 * a:256 * a + 256], Q2[off:off + 64, j, 256 + 128 * a:384 + 128 * a],
                               K2[off:off + 64, 256:512], True, True, after, b["free"])
                    return t

                def pv(P, tp, after):
                    if kv == 0:
                        held["b"] = main.get()
                    b = held["b"]
                    for a in range(2):
                        for c in range(2):
                            t = mm(b["ap"][off:off + 64, 128 * a:128 * a + 128], V2[:, 2 + c, off:off + 64],
                                   P[:, 256 * a + 128 * c:256 * a + 128 * c + 128], c == 0, c == 1, tp, after,
                                   b["free"])
                    if kv == 1:
                        keep_out(j, 256, b, t)
                    return t
                return lambda: Unit(score, 2, None, vec("attn_sink_2", 8 * l + j + 4 * kv), pv, qkt, v2t, sbk, zb)

            units = [x_unit(j, kv, a) for j in range(4) for kv in range(2) for a in range(2)]
            if l == 0:
                units += [c_unit(j, kv) for j in range(4) for kv in range(2)]
            run_units(units, sbk, fill_end)
            while len(fh) < 4:
                fill_end()
            at_j = [halves(HH[:, 4 + j, 0:T], HL[:, 4 + j, 0:T], Q2[:, j, 0:T], a_tok[j], h_free) for j in range(4)]

            sg = {}

            def sigmoids(d):
                if d < 8:
                    for n in range(3 * d, 3 * d + 3):
                        sg[n] = a_act(g_ap(n), g_ap(n), ACT.Sigmoid, g_tok[n])

            sigmoids(0)
            if l == 0:
                def y_ap(d, z):
                    return (YA, YB)[d // 4][:, 3 * (d % 4) + z, :]
            else:
                def y_ap(d, z):
                    return Y1[:, 3 * d + z, :]
            br_rhs = [lambda i: (HH[:, i, 0:T], HL[:, i, 0:T], fh[i]),
                      lambda i: (HH[:, 4 + i, 0:T], HL[:, 4 + i, 0:T], at_j[i]),
                      lambda i: (OHH[:, i, 0:T], OHL[:, i, 0:T], oht[i])]
            yt = []
            for d in range(8):
                sigmoids(d + 1)
                tm = TM.get()
                acc = tm["ap"][:, 0:T]
                for br in range(3):
                    b = main.get()
                    key = ("w_branch_2", l, br, "split" if br == 1 else None)
                    t = wmm(b["ap"][:, 0:T], key, range(4), [(128 * d, 128 * d + 128)], br_rhs[br], b["free"])
                    gg = g_ap(3 * d + br)
                    if br == 0:
                        prev = tt(acc, b["ap"][:, 0:T], gg, ALU.mult, t, sg[3 * d], tm["free"])
                        b["free"] = [prev]
                    else:
                        t = tt(gg, b["ap"][:, 0:T], gg, ALU.mult, t, sg[3 * d + br])
                        b["free"] = [t]
                        prev = tt(acc, acc, gg, ALU.add, t, prev)
                yt.append(halves(y_ap(d, 0), y_ap(d, 1), acc, prev))
                tm["free"] = yt[-1]
            h_free[:] = [pe.last]

            def add_out(name, ks, rhs, mod_i, xt0, ct0):
                xt, ct = [], []
                for d in range(8):
                    b = main.get()
                    t = wmm(b["ap"][:, 0:T], name, ks, [(128 * d, 128 * d + 128)], rhs, b["free"])
                    for c in range(T // 256):
                        sl = slice(256 * c, 256 * c + 256)
                        t2 = stt(X[:, d, sl], b["ap"][:, sl], MOD[:, l, mod_i + d, c:c + 1], X[:, d, sl],
                                 ALU.mult, ALU.add, t, (ct0 if c else xt0)[d])
                        (ct if c else xt).append(t2)
                    b["free"] = [t2]
                return xt, ct

            xt, ct = add_out(("w_out_2", l), range(8), lambda i: (y_ap(i, 0), y_ap(i, 1), yt[i]), 16, xt, ct)
            y_done = [pe.last]
            dump(f"xa{l}", X[:, :, 0:T], xt, ct)
            h2 = adaln(l, 1, T, xt, ct)
            r2 = xrhs(h2, T)
            hfree = y_done
            for part in range(2 if l == 0 else 1):
                nf = 16 if l == 0 else 32
                hh, hl = (HIDH, HIDL) if l == 0 else (HIDH1, HIDL1)
                mt = []
                for i in range(nf):
                    f = nf * part + i
                    b = main.get()
                    t = wmm(b["ap"][:, 0:T], ("w_ff1_2", l), range(8), [(128 * f, 128 * f + 128)], r2, b["free"])
                    tm = TM.get()
                    v = tm["ap"][:, 0:T]
                    t = a_act(v, b["ap"][:, 0:T], ACT.Relu, t, tm["free"])
                    t = tt(v, v, b["ap"][:, 0:T], ALU.mult, t)
                    b["free"] = [t]
                    mt.append(halves(hh[:, i, :], hl[:, i, :], v, t, hfree))
                    tm["free"] = mt[-1]
                if l == 0:
                    fill_mod(1, 4 if part == 0 else 30)
                if part == (1 if l == 0 else 0):
                    h_free[:] = [pe.last]
                xt, ct = add_out(("w_ff2_2", l), range(nf * part, nf * part + nf),
                                 lambda i: (hh[:, i, :], hl[:, i, :], mt[i]), 40, xt, ct)
                hfree = [pe.last]
            a_free = [pe.last]
            dump(f"xb{l}", X[:, :, 0:T], xt, ct)

        yd = d_out.rearrange("p (k t) -> p k t", k=8)
        for k in range(8):
            t_o = sync.dma(lambda e, k=k: e.dma_start(yd[:, k, :], X[:, k, 0:256]), s_out, 16 * 8, xt[k])
        sync(None, t_o, outs)

        if not plan:
            return kinds, order
        d_w = dram("wstream", (len(kinds), 128, 1024))
        for q in (sync, pe, act, dve, pool):
            q.number()
        with nc.Block() as block:
            block.sync(sync.emit)
            block.tensor(pe.emit)
            block.scalar(act.emit)
            block.vector(dve.emit)
            block.gpsimd(pool.emit)
        return kinds, order


def weight(inputs, name):
    if name[0] == "w_branch_2":
        w = inputs["w_branch_2"][name[1], name[2]]
        if name[3]:
            w = w.reshape(2, 4, 64, -1).transpose(1, 0, 2, 3).reshape(512, -1)
        return w
    return inputs[name[0]][name[1]]


def pack_stream(inputs, order, blocks):
    out = np.zeros((blocks, 128, 1024), np.float32)
    for n, col, name, k, cols in order:
        w = weight(inputs, name)
        for a, b in cols:
            out[n, :, col:col + b - a] = w[128 * k:128 * k + 128, a:b]
            col += b - a
    return out


def columns(v):
    return np.ascontiguousarray(np.asarray(v).reshape(-1, 128).T)


def pack_vecs(inputs):
    v = np.zeros((128, NVEC), np.float32)

    def put(name, a):
        at, n = VEC[name]
        assert a.shape == (128, n), (name, a.shape)
        v[:, at:at + n] = a
    for name in ("ffn1_pre_g", "ffn1_post_g", "mix_pre_g", "na_out_g", "dil_out_g", "mix_post_g", "ffn2_pre_g",
                 "ffn2_post_g", "b_mod_2", "norm1_g_2", "norm2_g_2", "hgrn_lb_logits_2", "hgrn_norm_g_2"):
        put(name, columns(inputs[name]))
    put("cc", np.stack([columns(inputs["c_2"]), columns(inputs["c_ctx_2"])], 2).reshape(128, 16))
    for name in ("q_norm_g_2", "k_norm_g_2"):
        put(name, np.concatenate([inputs[name].T, inputs[name].T], 0))
    put("attn_sink_2", np.broadcast_to(inputs["attn_sink_2"].reshape(1, 16), (128, 16)))
    put("neglb", np.full((128, 1), -LOG_FLOOR, np.float32))
    put("eps", np.full((128, 1), EPS, np.float32))
    return v


def kernel(debug=None, **inputs):
    import concourse.bacc as bacc
    from concourse.bass_utils import run_bass_kernel_spmd

    inputs = {k: np.asarray(v) for k, v in inputs.items()}
    consts = const_arrays()
    sizes = {n: consts[n].shape[1] for n in CONSTS}
    plan, _ = build_program(bacc.Bacc("TRN2", target_bir_lowering=False, num_devices=1), sizes, None)
    nc = bacc.Bacc("TRN2", target_bir_lowering=False, num_devices=1)
    kinds, order = build_program(nc, sizes, plan, debug)
    blocks = len(kinds)
    xc = np.concatenate([inputs["x"][0], inputs["ctx_2"][0]], 0).T
    arrays = {
        "xin": np.ascontiguousarray(xc.reshape(8, 128, 512).transpose(1, 0, 2)).reshape(128, 4096),
        "wstream": pack_stream(inputs, order, blocks),
        "consts": np.ascontiguousarray(np.concatenate([consts[n] for n in CONSTS], 1)),
        "b1mask": consts["b1mask"],
        "vecs": pack_vecs(inputs),
        "lmask": level_masks(),
        "onehot": bucket_onehot(),
        "t5t": np.ascontiguousarray(inputs["t5_rel_bias"].T),
        "narel": np.ascontiguousarray(inputs["na_rel_bias"].reshape(8, 465)),
    }
    r = run_bass_kernel_spmd(nc, [arrays], core_ids=[0])
    y = r.results[0]["yout"]
    return np.ascontiguousarray(y.reshape(128, 8, 256).transpose(2, 1, 0)).reshape(1, 256, 1024)
```
